# Optimizing a Trainium2 kernel written in Bass

```python
import math
import jax, jax.numpy as jnp
from jax import lax
import numpy as np

D_MODEL = 4096
BATCH = 1
SEQ = 256
DEPTH = 1
DEC_BATCH = 8
DEC_SEQ = 8
PAST_LEN = 1024
PAGE_SIZE = 128

MIX_WIDTH = D_MODEL
ATTN_WIDTH = MIX_WIDTH // 2
POOL_WIDTH = MIX_WIDTH - ATTN_WIDTH
HEAD_DIM = 128
N_HEADS = ATTN_WIDTH // HEAD_DIM
N_KV_HEADS = 4
KV_WIDTH = N_KV_HEADS * HEAD_DIM
IDX_HEADS = 32
IDX_DIM = 128
TOPK_MAX = 256
POOL_WINDOWS = (2, 4, 8, 16)
N_POOL_GROUPS = 4
POOL_GROUP = POOL_WIDTH // N_POOL_GROUPS
POOL_STATE = 15
N_BUCKETS = 32
MAX_DISTANCE = 128
RMS_EPS = 1e-6
Q_BLOCK = 128
SPLITS = (ATTN_WIDTH, KV_WIDTH, KV_WIDTH, ATTN_WIDTH, IDX_HEADS * IDX_DIM, IDX_HEADS, IDX_DIM, POOL_WIDTH, POOL_WIDTH)
IN_WIDTH = ATTN_WIDTH * 2 + KV_WIDTH * 2 + IDX_HEADS * IDX_DIM + IDX_HEADS + IDX_DIM + POOL_WIDTH * 2

kernel_name = "hybrid_dsa_pool_decoder_step"

F32 = jnp.float32

def rmsnorm(x, g):
    xf = x.astype(F32)
    var = jnp.mean(xf * xf, axis=-1, keepdims=True)
    return (xf * lax.rsqrt(var + RMS_EPS) * g.astype(F32)).astype(x.dtype)

def project(x, ln_g, w_in):
    B, T, _ = x.shape
    h = jnp.einsum('btd,dn->btn', rmsnorm(x, ln_g), w_in)
    parts = []
    off = 0
    for width in SPLITS:
        parts.append(h[..., off:off + width])
        off += width
    q, k, v, g_a, qi, wi, ki, u, g_b = parts
    q = q.reshape(B, T, N_HEADS, HEAD_DIM)
    k = k.reshape(B, T, N_KV_HEADS, HEAD_DIM)
    v = v.reshape(B, T, N_KV_HEADS, HEAD_DIM)
    qi = qi.reshape(B, T, IDX_HEADS, IDX_DIM) * (IDX_DIM ** -0.5)
    wi = wi * (IDX_HEADS ** -0.5)
    return q, k, v, g_a, qi, wi, ki, u, g_b

def t5_bucket(dist):
    max_exact = N_BUCKETS // 2
    d = jnp.maximum(dist, 0)
    df = jnp.maximum(d.astype(F32), 1.0)
    large = max_exact + (jnp.log(df / max_exact) / math.log(MAX_DISTANCE / max_exact)
                         * (N_BUCKETS - max_exact)).astype(jnp.int32)
    large = jnp.minimum(large, N_BUCKETS - 1)
    return jnp.where(d < max_exact, d, large)

def indexer_scores(qi, wi, ki):
    s = jnp.einsum('bthd,bsd->bths', qi, ki, preferred_element_type=F32)
    return jnp.einsum('bth,bths->bts', wi.astype(F32), jax.nn.relu(s))

def sparse_attend(q, k_sel, v_sel, sel_pos, q_pos, valid, rel_bias):
    B, T, H, D = q.shape
    K = sel_pos.shape[-1]
    R = H // N_KV_HEADS
    qg = q.reshape(B, T, N_KV_HEADS, R, D)
    logits = jnp.einsum('btgrd,btkgd->btgrk', qg, k_sel, preferred_element_type=F32) * (D ** -0.5)
    bucket = t5_bucket(q_pos[None, :, None] - sel_pos)
    bias = rel_bias[bucket].astype(F32).reshape(B, T, K, N_KV_HEADS, R)
    logits = logits + jnp.transpose(bias, (0, 1, 3, 4, 2))
    logits = jnp.where(valid[:, :, None, None, :], logits, -1e30)
    p = jax.nn.softmax(logits, axis=-1)
    o = jnp.einsum('btgrk,btkgd->btgrd', p.astype(v_sel.dtype), v_sel)
    return o.reshape(B, T, H * D)

def gather_rows(rows, idx):
    return jax.vmap(lambda r, i: r[i])(rows, idx)

def prompt_attention(q, k, v, qi, wi, ki, rel_bias):
    B, S = q.shape[:2]
    topk = min(TOPK_MAX, S // 4)
    n_blk = S // Q_BLOCK
    key_pos = jnp.arange(S)

    def block(i):
        t0 = i * Q_BLOCK
        qb = lax.dynamic_slice_in_dim(q, t0, Q_BLOCK, axis=1)
        qib = lax.dynamic_slice_in_dim(qi, t0, Q_BLOCK, axis=1)
        wib = lax.dynamic_slice_in_dim(wi, t0, Q_BLOCK, axis=1)
        q_pos = t0 + jnp.arange(Q_BLOCK)
        sc = indexer_scores(qib, wib, ki)
        sc = jnp.where((key_pos[None, :] <= q_pos[:, None])[None], sc, -jnp.inf)
        _, sel = lax.top_k(sc, topk)
        valid = sel <= q_pos[None, :, None]
        return sparse_attend(qb, gather_rows(k, sel), gather_rows(v, sel), sel, q_pos, valid, rel_bias)

    out = lax.map(block, jnp.arange(n_blk))
    return jnp.transpose(out, (1, 0, 2, 3)).reshape(B, S, ATTN_WIDTH)

def sample_attention(q, k_new, v_new, qi, wi, ki_new, cache_k, cache_v, cache_idx_k, page_table, rel_bias):
    Bd, T = q.shape[:2]
    n_pages = page_table.shape[1]
    past = n_pages * PAGE_SIZE
    L = past + T
    topk = min(TOPK_MAX, L // 4)
    past_ki = cache_idx_k[page_table].reshape(Bd, past, IDX_DIM)
    ki_all = jnp.concatenate([past_ki, ki_new.astype(past_ki.dtype)], axis=1)
    q_pos = past + jnp.arange(T)
    key_pos = jnp.arange(L)
    sc = indexer_scores(qi, wi, ki_all)
    sc = jnp.where((key_pos[None, :] <= q_pos[:, None])[None], sc, -jnp.inf)
    _, sel = lax.top_k(sc, topk)
    valid = sel <= q_pos[None, :, None]
    in_past = (sel < past)[..., None, None]
    ps = jnp.minimum(sel, past - 1)
    phys = gather_rows(page_table, ps // PAGE_SIZE)
    row = ps % PAGE_SIZE
    ns = jnp.clip(sel - past, 0, T - 1)
    k_sel = jnp.where(in_past, cache_k[phys, row], gather_rows(k_new, ns).astype(cache_k.dtype))
    v_sel = jnp.where(in_past, cache_v[phys, row], gather_rows(v_new, ns).astype(cache_v.dtype))
    return sparse_attend(q, k_sel, v_sel, sel, q_pos, valid, rel_bias)

def multiscale_pool(u_full, first_pos, n_ctx, w_pool, pool_scale):
    B, N, W = u_full.shape
    T = N - n_ctx
    uf = u_full.astype(F32)
    cs = jnp.concatenate([jnp.zeros((B, 1, W), F32), jnp.cumsum(uf, axis=1)], axis=1)
    j = n_ctx + jnp.arange(T)
    pos = first_pos + j
    outs = []
    for g, win in enumerate(POOL_WINDOWS):
        sl = slice(g * POOL_GROUP, (g + 1) * POOL_GROUP)
        lo = jnp.maximum(j + 1 - win, 0)
        cnt = jnp.minimum(pos + 1, win).astype(F32)
        mean = (cs[:, j + 1, sl] - cs[:, lo, sl]) / cnt[None, :, None]
        d = mean - uf[:, n_ctx:, sl]
        outs.append(jnp.einsum('btc,cd->btd', d, w_pool[g].astype(F32)))
    return (jnp.concatenate(outs, axis=-1) * pool_scale.astype(F32)).astype(u_full.dtype)

def merge(x, o_a, g_a, o_b, g_b, w_out):
    mix = jnp.concatenate([o_a * jax.nn.silu(g_a), o_b * jax.nn.silu(g_b)], axis=-1)
    return x + jnp.einsum('btm,md->btd', mix.astype(x.dtype), w_out)

def setup_inputs(seed: int = 0) -> dict:
    key = jax.random.key(seed)
    ks = jax.random.split(key, 16)
    n_pages = PAST_LEN // PAGE_SIZE
    n_used = DEC_BATCH * n_pages
    n_phys = n_used + (n_used + 3) // 4
    page_table = jax.random.permutation(ks[0], n_phys)[:n_used].reshape(DEC_BATCH, n_pages).astype(jnp.int32)
    nrm = jax.random.normal
    return {
        "x_prompt": nrm(ks[1], (BATCH, SEQ, D_MODEL), F32),
        "x_sample": nrm(ks[2], (DEC_BATCH, DEC_SEQ, D_MODEL), F32),
        "cache_k": nrm(ks[3], (DEPTH, n_phys, PAGE_SIZE, N_KV_HEADS, HEAD_DIM), F32),
        "cache_v": nrm(ks[4], (DEPTH, n_phys, PAGE_SIZE, N_KV_HEADS, HEAD_DIM), F32),
        "cache_idx_k": nrm(ks[5], (DEPTH, n_phys, PAGE_SIZE, IDX_DIM), F32),
        "state_pool": nrm(ks[6], (DEPTH, DEC_BATCH, POOL_STATE, POOL_WIDTH), F32),
        "page_table": page_table,
        "rel_bias": 0.5 * nrm(ks[7], (N_BUCKETS, N_HEADS), F32),
        "ln_g": 1.0 + 0.1 * nrm(ks[8], (DEPTH, D_MODEL), F32),
        "w_in": nrm(ks[9], (DEPTH, D_MODEL, IN_WIDTH), F32) * (D_MODEL ** -0.5),
        "w_pool": nrm(ks[10], (DEPTH, N_POOL_GROUPS, POOL_GROUP, POOL_GROUP), F32) * (POOL_GROUP ** -0.5),
        "pool_scale": 1.0 + 0.1 * nrm(ks[11], (DEPTH, POOL_WIDTH), F32),
        "w_out": nrm(ks[12], (DEPTH, MIX_WIDTH, D_MODEL), F32) * (MIX_WIDTH ** -0.5),
        "final_g": 1.0 + 0.1 * nrm(ks[13], (D_MODEL,), F32),
    }

def reference(x_prompt, x_sample, cache_k, cache_v, cache_idx_k, state_pool, page_table,
              rel_bias, ln_g, w_in, w_pool, pool_scale, w_out, final_g):
    past = page_table.shape[1] * PAGE_SIZE
    hp, hs = x_prompt, x_sample
    kp, vp, ikp, pp = [], [], [], []
    ksm, vsm, iks, psm = [], [], [], []
    for layer in range(DEPTH):
        q, k, v, g_a, qi, wi, ki, u, g_b = project(hp, ln_g[layer], w_in[layer])
        o_a = prompt_attention(q, k, v, qi, wi, ki, rel_bias)
        o_b = multiscale_pool(u, 0, 0, w_pool[layer], pool_scale[layer])
        hp = merge(hp, o_a, g_a, o_b, g_b, w_out[layer])
        kp.append(k)
        vp.append(v)
        ikp.append(ki)
        pp.append(u[:, -POOL_STATE:])
        q, k, v, g_a, qi, wi, ki, u, g_b = project(hs, ln_g[layer], w_in[layer])
        o_a = sample_attention(q, k, v, qi, wi, ki, cache_k[layer], cache_v[layer],
                               cache_idx_k[layer], page_table, rel_bias)
        u_full = jnp.concatenate([state_pool[layer].astype(u.dtype), u], axis=1)
        o_b = multiscale_pool(u_full, past - POOL_STATE, POOL_STATE, w_pool[layer], pool_scale[layer])
        hs = merge(hs, o_a, g_a, o_b, g_b, w_out[layer])
        ksm.append(k)
        vsm.append(v)
        iks.append(ki)
        psm.append(u_full[:, -POOL_STATE:])
    y_prompt = rmsnorm(hp, final_g)
    y_sample = rmsnorm(hs, final_g)
    return (y_prompt, y_sample, jnp.stack(kp), jnp.stack(vp), jnp.stack(ikp), jnp.stack(pp),
            jnp.stack(ksm), jnp.stack(vsm), jnp.stack(iks), jnp.stack(psm))


_drawn_inputs = setup_inputs


def setup_inputs(seed=0):
    import zlib

    import numpy as np

    out = dict(_drawn_inputs(seed))
    spreads = {}
    factors = {}
    for name, (base, spread) in spreads.items():
        noise = np.random.default_rng([zlib.crc32(name.encode()), seed]).standard_normal(out[name].shape)
        drawn = base * np.exp(spread * noise) if base else spread * noise
        out[name] = __import__('jax').numpy.asarray(drawn.astype(out[name].dtype))
    for name, factor in factors.items():
        out[name] = (out[name] * factor).astype(out[name].dtype)
    return out
```

```python
from contextlib import ExitStack

import numpy as np
import concourse.bass as bass
from concourse import mybir

F32 = mybir.dt.float32
F32R = mybir.dt.float32r
BF16 = mybir.dt.bfloat16
I32 = mybir.dt.int32
ALU = mybir.AluOpType
ACT = mybir.ActivationFunctionType
AX = mybir.AxisListType
ds = bass.ds

P = 128
SLOTS = 4
KK = 4
AHEAD_SPLIT = 3
AHEAD_LOAD = 7
NEG = -1e30
TAKEN = -3e38
TAKEN_EDGE = -2e38


def hybrid_layer(nc, t, out):
    _, T_P, D = t["x_prompt"].shape
    NB_S, T_S, _ = t["x_sample"].shape
    N_PHYS, PAGE, G, HD = t["cache_k"].shape[1:]
    PAGES = t["page_table"].shape[1]
    PAST = PAGES * PAGE
    NBK, H = t["rel_bias"].shape
    POOLW = t["pool_scale"].shape[1]
    STATE = t["state_pool"].shape[2]
    NG = t["w_pool"].shape[1]
    ID = t["cache_idx_k"].shape[-1]
    AW, KVW = H * HD, G * HD
    IH = (t["w_in"].shape[2] - 2 * AW - 2 * KVW - ID - 2 * POOLW) // (ID + 1)
    R = H // G
    N_S = NB_S * T_S
    N = T_P + N_S
    TT = [(0, P), (P, P), (T_P, N_S)]
    KT = D // P
    CH = KT // KK
    QC = 2 * CH
    LS = PAST + T_S
    TOPK_P, TOPK_S = min(256, T_P // 4), min(256, LS // 4)
    SCALE = float(HD) ** -0.5
    W_SCALE = float(ID * IH) ** -0.5
    EPS = 1e-6
    TQ = T_S * IH
    L2 = P + T_P
    NEG_AT = PAST + T_S - 1
    VEC = NEG_AT + P + 1
    WINS = (2, 4, 8, 16)
    UW = STATE + T_P + NB_S * (STATE + T_S)
    assert T_P == 2 * P and HD == P and ID == P and PAGE == P and R * T_S == 32 and CH == 8

    C_Q, C_K = 0, AW
    C_GA = AW + 2 * KVW
    C_QI = C_GA + AW
    C_WI = C_QI + IH * ID
    C_KI = C_WI + IH
    C_U = C_KI + ID
    C_GB = C_U + POOLW
    W0 = IH + ID
    T_Q, T_K, T_V, T_GA = 0, AW // P, (AW + KVW) // P, C_GA // P
    T_QI = C_QI // P
    T_U = C_WI // P
    T_GB = T_U + POOLW // P
    N_TILES = T_GB + POOLW // P

    segs, chunk0, quad0 = {}, CH, 0
    for name, w, col, width, tile0 in (
            ("qi", "w_in", C_QI, IH * ID, T_QI), ("q", "w_in", C_Q, AW, T_Q), ("kv", "w_in", C_K, 2 * KVW, T_K),
            ("u", "w_in", C_U, POOLW, T_U), ("gb", "w_in", C_GB, POOLW, T_GB), ("ga", "w_in", C_GA, AW, T_GA),
            ("out", "w_out", 0, D, 0)):
        n = width // (4 * P)
        segs[name] = (w, col, n, chunk0, quad0, tile0)
        chunk0 += n * QC
        quad0 += n
    order = list(segs)
    CHUNKS = chunk0

    w_rows = {n: t[n][0].rearrange("(k p) n -> p k n", p=P) for n in ("w_in", "w_out")}

    def dram(name, shape):
        return nc.dram_tensor(name, shape, F32).ap()

    projT = dram("projT", (N_TILES, P, N))
    oT = dram("oT", (H, P, N))
    poolT = dram("poolT", (POOLW // P, P, N))
    mixT = dram("mixT", (POOLW // P, P, N))
    wsc = dram("wsc", (1, N_S * IH))
    scores = dram("scores", (N_S, LS))
    BIAS_W = T_P + P
    biasP = dram("biasP", (H, P * BIAS_W))
    biasS = dram("biasS", (H, T_S * (LS + T_S)))

    def tile_rows(ap, i):
        return ap[ds(i, 1)].rearrange("a p n -> (a p) n")

    def tiles(ap, i, n):
        return ap[ds(i, n)].rearrange("a p n -> p a n")

    root = ExitStack()
    with root:
        names = set()

        def sem(name):
            assert name not in names
            names.add(name)
            return root.enter_context(nc.semaphore(name))

        def sb(name, shape, dt=F32, ctx=root):
            return ctx.enter_context(nc.sbuf_tensor(name, shape, dt))

        bank = [root.enter_context(nc.psum_tensor(f"bank{i}", [P, 512], F32)) for i in range(4)]
        wide = root.enter_context(nc.psum_tensor("wide", [P, 4 * 512], F32))
        sbank = [wide[:, 512 * i:512 * i + 512] for i in range(4)]

        XH = sb("XH", [P, KT, N], F32R)
        XL = sb("XL", [P, KT, N], F32R)
        raw = sb("raw", [P, SLOTS, KK, 2 * P])
        hi = sb("hi", [P, SLOTS, KK, 2 * P], F32R)
        lo = sb("lo", [P, SLOTS, KK, 2 * P], F32R)
        stg = [sb(f"stg{i}", [P, 2, N]) for i in range(2)]
        ident = sb("ident", [P, P])
        identb = sb("identb", [P, P], BF16)
        gT = sb("gT", [P, KT])
        poolscT = sb("poolscT", [P, POOLW // P])
        kiT = sb("kiT", [P, N])
        wN = sb("wN", [P, 3, IH])
        ptab = sb("ptab", [1, NB_S * PAGES], I32)
        keep = sb("keep", [P, G * N + (LS + 1) // 2 + L2 + L2 // 2 + 3 * KVW + POOLW // P * NB_S * STATE])
        at = [0]

        def cut(n, dt=F32, back=None):
            if back is not None:
                at[0] = back
            ap = keep[:, at[0]:at[0] + n]
            at[0] += n
            return ap if dt == F32 else ap.bitcast(dt)

        kT = cut(G * N).rearrange("p (g n) -> p g n", g=G)
        maskS = cut((LS + 1) // 2, BF16)
        era = at[0]
        scP = cut(L2)
        maskP = cut(L2 // 2, BF16)
        vN = cut(3 * KVW).rearrange("p (a n) -> p a n", a=3)
        stT = cut(POOLW // P * NB_S * STATE).rearrange("p (a n) -> p a n", a=POOLW // P)
        qS = cut(H * N_S, back=era).rearrange("p (h n) -> p h n", h=H)

        stood = {e: sem(f"stood_{e}") for e in ("Pool", "DVE", "SP", "PE")}

        def alone(eng):
            eng.sem_inc(stood[eng.engine.name], 1)

        raw_in = [sem(f"raw_in{i}") for i in range(SLOTS)]
        hi_ready, lo_ready, chunk_used = sem("hi_ready"), sem("lo_ready"), sem("chunk_used")
        evac = [sem("evac0"), sem("evac1")]
        stored = [sem("stored0"), sem("stored1")]

        def load_chunk(sp, c, slot, src, width, guard=True):
            if guard:
                sp.wait_ge(lo_ready, c - (SLOTS - 1))
                alone(sp)
            sp.dma_start(raw[:, slot, :, 0:width], src).then_inc(raw_in[slot], 16)

        def chunk_src(name, q, j):
            w, col = segs[name][:2]
            return w_rows[w][:, KK * (j % CH) if name != "out" else (KK * (j % CH) + KT // 2) % KT:, :][
                :, 0:KK, ds(q * (4 * P) + (col + (j // CH) * 2 * P), 2 * P)]

        def load_segment(sp, name):
            _, _, n, c0, _, _ = segs[name]
            nxt = order[order.index(name) + 1] if name != "out" else None

            def quad(q, last):
                for j in range(QC):
                    k = j + AHEAD_LOAD
                    if k < QC:
                        src = chunk_src(name, q, k)
                    elif not last:
                        src = chunk_src(name, q + 1, k - QC)
                    elif nxt:
                        src = chunk_src(nxt, 0, k - QC)
                    else:
                        continue
                    load_chunk(sp, q * QC + (c0 + k), (c0 + k) % SLOTS, src, 2 * P)
            with sp.Fori(0, n - 1) as q:
                quad(q, False)
            quad(n - 1, True)

        def hi_chunk(act, c, slot, uses, width=2 * P, guard=True):
            act.wait_ge(raw_in[slot], uses)
            if guard:
                act.wait_ge(chunk_used, c - (SLOTS - 1))
            nc.scalar.activation(hi[:, slot, :, 0:width], raw[:, slot, :, 0:width], ACT.Copy).then_inc(hi_ready, 1)

        def lo_chunk(dve, c, slot, width=2 * P):
            dve.wait_ge(hi_ready, c + 1)
            nc.vector.tensor_tensor(lo[:, slot, :, 0:width], raw[:, slot, :, 0:width],
                                    hi[:, slot, :, 0:width].bitcast(F32), ALU.subtract).then_inc(lo_ready, 1)

        def products(pe, c, slot, j, banks, cols, rot=0):
            pe.wait_ge(lo_ready, c + 1)
            for kk in range(KK):
                k = (KK * j + kk + rot) % KT
                for n in range(2):
                    wh, wl = (w[:, slot, kk, cols[n]:cols[n] + P] for w in (hi, lo))
                    first, last = j == 0 and kk == 0, j == CH - 1 and kk == KK - 1
                    nc.tensor.matmul(bank[banks[n]][:, 0:N], wh, XH[:, k, :], start=first, stop=False)
                    nc.tensor.matmul(bank[banks[n]][:, 0:N], wh, XL[:, k, :], start=False, stop=False)
                    mm = nc.tensor.matmul(bank[banks[n]][:, 0:N], wl, XH[:, k, :], start=False, stop=last)
            mm.then_inc(chunk_used, 1)

        def pe_quad(pe, name, q, weave=None, before=None):
            _, _, _, c0, quad0, _ = segs[name]
            rot = KT // 2 if name == "out" else 0
            for j in range(QC):
                half = j // CH
                if j % CH == 0:
                    pe.wait_ge(evac[half], q + (quad0 + half))
                if before:
                    before(pe, j)
                products(pe, q * QC + (c0 + j), (c0 + j) % SLOTS, j % CH, (2 * half, 2 * half + 1), (0, P), rot)
                if weave:
                    weave(pe, q, j)

        def pe_segment(pe, name, weave=None):
            with pe.Fori(0, segs[name][2]) as q:
                pe_quad(pe, name, q, weave)

        def act_quad(act, name, q, weave=None, last=False, turned=None):
            _, _, _, c0, quad0, tile0 = segs[name]
            for j in range(QC):
                k = j + AHEAD_SPLIT
                if not (last and k >= QC):
                    hi_chunk(act, q * QC + (c0 + k), (c0 + k) % SLOTS,
                             q * (QC // SLOTS * 16) + 16 * ((c0 + k) // SLOTS + 1))
                if j % CH == CH - 1:
                    half = j // CH
                    act.wait_ge(chunk_used, q * QC + (c0 + j + 1))
                    if turned is None:
                        act.wait_ge(stored[half], q * 16 + 16 * quad0)
                    else:
                        act.wait_ge(stored[half], 16 * quad0)
                        act.wait_ge(turned, q)
                    for n_ in range(2):
                        copy = nc.scalar.activation(stg[half][:, n_, :], bank[2 * half + n_][:, 0:N], ACT.Copy)
                    copy.then_inc(evac[half], 1)
                    if turned is None:
                        act.wait_ge(evac[half], q + (quad0 + half + 1))
                        act.dma_start(tiles(projT, q * 4 + (tile0 + 2 * half), 2), stg[half][:]).then_inc(stored[half], 16)
                if weave:
                    weave(act, q, j)

        def act_segment(act, name, weave=None):
            with act.Fori(0, segs[name][2]) as q:
                act_quad(act, name, q, weave)

        def dve_quad(dve, name, q, weave=None, last=False):
            c0 = segs[name][3]
            for j in range(QC):
                k = j + AHEAD_SPLIT
                if not (last and k >= QC):
                    lo_chunk(dve, q * QC + (c0 + k), (c0 + k) % SLOTS)
                if weave:
                    weave(dve, q, j)

        def dve_segment(dve, name, weave=None):
            with dve.Fori(0, segs[name][2]) as q:
                dve_quad(dve, name, q, weave)

        def all_stored(eng, name):
            for half in range(2):
                eng.wait_ge(stored[half], 16 * (segs[name][4] + segs[name][2]))

        with ExitStack() as ph:
            xN = [sb(f"xN{i}", [P, D], ctx=ph) for i in range(3)]
            junk = keep[:, 0:D]
            ssq = sb("ssq", [P, 3], ctx=ph)
            rstd = sb("rstd", [P, 3], ctx=ph)
            root_ = sb("root_", [P, 3], ctx=ph)
            gN = sb("gN", [KT, P], ctx=ph)
            pscN = sb("pscN", [POOLW // P, P], ctx=ph)
            wiT = sb("wiT", [IH, N], ctx=ph)
            kiN = sb("kiN", [P, 3, P], ctx=ph)
            s_x = [sem(f"s_x{i}") for i in range(3)]
            s_small, s_sq, s_var, s_root, s_rstd, s_xn = (sem(n) for n in (
                "s_small", "s_sq", "s_var", "s_root", "s_rstd", "s_xn"))
            s_gT, s_gcopy, s_xT, s_xh, s_xl = (sem(n) for n in ("s_gT", "s_gcopy", "s_xT", "s_xh", "s_xl"))
            s_kin, s_kinc, s_bvec, s_bvecc, s_outA, s_identb = (sem(n) for n in (
                "s_kin", "s_kinc", "s_bvec", "s_bvecc", "s_outA", "s_identb"))
            s_onehot = sem("s_onehot")
            block = ph.enter_context(nc.Block())

            @block.sync
            def _(sp):
                for c in range(AHEAD_LOAD):
                    load_chunk(sp, c, c % SLOTS, w_rows["w_in"][:, KK * c:KK * c + KK, C_WI:C_WI + W0], W0, c >= SLOTS)
                for c in range(AHEAD_LOAD, AHEAD_LOAD + CH):
                    if c < CH:
                        load_chunk(sp, c, c % SLOTS, w_rows["w_in"][:, KK * c:KK * c + KK, C_WI:C_WI + W0], W0)
                    else:
                        load_chunk(sp, c, c % SLOTS, chunk_src("qi", 0, c - CH), 2 * P)
                load_segment(sp, "qi")

            @block.gpsimd
            def _(pool):
                pool.dma_start(ident[:], t["c_ident"]).then_inc(s_small, 16)
                pool.dma_start(gN[:], t["ln_g"][0].rearrange("(k p) -> k p", p=P)).then_inc(s_small, 16)
                pool.dma_start(pscN[:], t["pool_scale"][0].rearrange("(k p) -> k p", p=P)).then_inc(s_small, 16)
                pool.dma_start(ptab[:], t["page_table"].rearrange("(o b) p -> o (b p)", o=1)).then_inc(s_small, 16)
                pool.wait_ge(s_kinc, 1)
                pool.dma_start(out[4][0, 0].rearrange("(a p) d -> p a d", p=P), kiN[:, 0:2, :]).then_inc(s_outA, 16)
                pool.dma_start(out[8][0].rearrange("b s d -> (b s) d"), kiN[0:N_S, 2, :]).then_inc(s_outA, 16)
                pool.dma_start(wsc.rearrange("o (p h) -> (o p) h", h=IH), wN[0:N_S, 2, :]).then_inc(s_outA, 16)
                pool.wait_ge(s_outA, 48)

            @block.scalar
            def _(act):
                rows = [t["x_prompt"][0, 0:P], t["x_prompt"][0, P:T_P], t["x_sample"].rearrange("b s d -> (b s) d")]
                for i in range(3):
                    act.dma_start(xN[i][0:TT[i][1], :], rows[i]).then_inc(s_x[i], 16)
                for i in range(3):
                    r = TT[i][1]
                    act.wait_ge(s_x[i], 16)
                    if i:
                        act.wait_ge(s_sq, i)
                    nc.scalar.activation(junk[0:r, :], xN[i][0:r, :], ACT.Square,
                                         accum_out=ssq[0:r, i:i + 1]).then_inc(s_sq, 1)
                for i in range(3):
                    r = TT[i][1]
                    act.wait_ge(s_var, i + 1)
                    nc.scalar.activation(root_[0:r, i:i + 1], rstd[0:r, i:i + 1], ACT.Sqrt).then_inc(s_root, 1)
                for c in range(AHEAD_SPLIT):
                    hi_chunk(act, c, c, 16, W0, False)
                act.wait_ge(s_gcopy, 1)
                for k in range(KT):
                    act.wait_ge(s_xT, k + 1)
                    nc.scalar.activation(XH[:, k, :], sbank[k % 4][:, 0:N], ACT.Copy,
                                         scale=gT[:, k:k + 1]).then_inc(s_xh, 1)
                for j in range(CH):
                    c = j + AHEAD_SPLIT
                    hi_chunk(act, c, c % SLOTS, 16 * (c // SLOTS + 1), W0 if c < CH else 2 * P, c >= SLOTS)
                act.wait_ge(chunk_used, CH)
                nc.scalar.activation(wiT[:], bank[2][0:IH, 0:N], ACT.Copy, scale=W_SCALE)
                nc.scalar.activation(kiT[:], bank[3][:, 0:N], ACT.Copy).then_inc(evac[1], 1)
                act_segment(act, "qi")

            @block.vector
            def _(dve):
                for i in range(3):
                    r = TT[i][1]
                    dve.wait_ge(s_sq, i + 1)
                    nc.vector.tensor_scalar(rstd[0:r, i:i + 1], ssq[0:r, i:i + 1], 1.0 / D, EPS,
                                            ALU.mult, ALU.add).then_inc(s_var, 1)
                for c in range(AHEAD_SPLIT):
                    lo_chunk(dve, c, c, W0)
                for i in range(3):
                    r = TT[i][1]
                    dve.wait_ge(s_root, i + 1)
                    nc.vector.reciprocal(rstd[0:r, i:i + 1], root_[0:r, i:i + 1]).then_inc(s_rstd, 1)
                    dve.wait_ge(s_rstd, i + 1)
                    nc.vector.tensor_scalar(xN[i][0:r, :], xN[i][0:r, :], rstd[0:r, i:i + 1], None,
                                            ALU.mult).then_inc(s_xn, 1)
                dve.wait_ge(s_gT, 1)
                nc.vector.tensor_copy(gT[:], sbank[0][:, 0:KT])
                nc.vector.tensor_copy(identb[:], ident[:])
                nc.vector.tensor_copy(poolscT[:], sbank[0][:, KT:KT + POOLW // P]).then_inc(s_gcopy, 1)
                dve.wait_ge(s_gcopy, 1)
                for k in range(KT):
                    dve.wait_ge(s_xh, k + 1)
                    nc.vector.scalar_tensor_tensor(XL[:, k, :], sbank[k % 4][:, 0:N], gT[:, k:k + 1],
                                                   XH[:, k, :].bitcast(F32), ALU.mult, ALU.subtract).then_inc(s_xl, 1)
                for j in range(CH):
                    c = j + AHEAD_SPLIT
                    lo_chunk(dve, c, c % SLOTS, W0 if c < CH else 2 * P)
                dve_segment(dve, "qi")
                dve.wait_ge(s_kin, 1)
                nc.vector.tensor_copy(wN[:, 0:2, :], sbank[0][:, 0:2 * IH].rearrange("p (a h) -> p a h", a=2))
                nc.vector.tensor_copy(wN[0:N_S, 2, :], sbank[0][0:N_S, 2 * IH:3 * IH])
                nc.vector.tensor_copy(kiN[:, 0:2, :], sbank[1][:, 0:2 * P].rearrange("p (a h) -> p a h", a=2))
                nc.vector.tensor_copy(kiN[0:N_S, 2, :], sbank[1][0:N_S, 2 * P:3 * P]).then_inc(s_kinc, 1)

            @block.tensor
            def _(pe):
                pe.wait_ge(s_small, 64)
                nc.tensor.transpose(sbank[0][:, 0:KT], gN[:], ident[0:KT, 0:KT])
                nc.tensor.transpose(sbank[0][:, KT:KT + POOLW // P], pscN[:],
                                    ident[0:POOLW // P, 0:POOLW // P]).then_inc(s_gT, 1)
                pe.wait_ge(s_gcopy, 1)
                pe.wait_ge(s_xn, 3)
                for k in range(KT):
                    if k >= 4:
                        pe.wait_ge(s_xl, k - 3)
                    for i, (c0, r) in enumerate(TT):
                        tr = nc.tensor.transpose(sbank[k % 4][:, c0:c0 + r], xN[i][0:r, k * P:k * P + P],
                                                 ident[0:r, 0:r])
                    tr.then_inc(s_xT, 1)
                for c in range(CH):
                    pe.wait_ge(s_xl, KK * (c + 1))
                    products(pe, c, c % SLOTS, c, (2, 3), (0, IH))
                pe_segment(pe, "qi")
                for i, (c0, r) in enumerate(TT):
                    nc.tensor.transpose(sbank[0][0:r, i * IH:(i + 1) * IH], wiT[:, c0:c0 + r], ident[0:IH, 0:IH])
                for i, (c0, r) in enumerate(TT):
                    tr = nc.tensor.transpose(sbank[1][0:r, i * P:(i + 1) * P], kiT[:, c0:c0 + r], ident[:])
                tr.then_inc(s_kin, 1)

        HQ = IH // segs["q"][2]
        BQ = NB_S // segs["q"][2]
        with ExitStack() as ph:
            qiH = sb("qiH", [P, HQ, T_P], ctx=ph)
            qiS = sb("qiS", [P, IH, N_S], ctx=ph)
            wbc = sb("wbc", [P, N_S * IH], ctx=ph)
            ipg = sb("ipg", [P, PAGES, ID], ctx=ph)
            ikT = sb("ikT", [P, LS], ctx=ph)
            prod = sb("prod", [P, 2, TQ], ctx=ph)
            scT = sb("scT", [P, PAGES + 1, T_S], ctx=ph)
            sc8 = sb("sc8", [T_S, LS], ctx=ph)
            relu = sb("relu", [P, L2], ctx=ph)
            onehot = sb("onehot", [NBK, VEC], ctx=ph)
            relb = sb("relb", [NBK, H], ctx=ph)
            bvec = sb("bvec", [H, VEC], ctx=ph)
            (s_qiS, s_wbc, s_qiH, p_scored, p_relu, p_sum, s_ipg, s_itr, s_ikA, s_ikD, s_iks, s_sc, s_prod, s_red,
             s_bt, s_sc8, s_scst, s_zero, s_bias) = (sem(n) for n in (
                 "s_qiS", "s_wbc", "s_qiH", "p_scored", "p_relu", "p_sum", "s_ipg", "s_itr", "s_ikA", "s_ikD", "s_iks",
                 "s_sc", "s_prod", "s_red", "s_bt", "s_sc8", "s_scst", "s_zero", "s_bias"))
            block = ph.enter_context(nc.Block())
            PAIRS = [(p, min(2, PAGES - p)) for p in range(0, PAGES, 2)] + [(PAGES, 1)]
            NPAIR = len(PAIRS)

            @block.sync
            def _(sp):
                load_segment(sp, "q")

            @block.gpsimd
            def _(pool):
                all_stored(pool, "qi")
                pool.dma_start(onehot[:], t["c_onehot"]).then_inc(s_onehot, 16)
                pool.dma_start(relb[:], t["rel_bias"]).then_inc(s_onehot, 16)
                pool.dma_start(qiS[:], projT[T_QI:T_QI + IH, :, T_P:N].rearrange("h p n -> p h n")).then_inc(s_qiS, 16)
                pool.dma_start(wbc[:], wsc.to_broadcast([P, N_S * IH])).then_inc(s_wbc, 16)
                with pool.Fori(0, segs["q"][2]) as q:
                    pool.wait_ge(p_scored, q * HQ)
                    alone(pool)
                    pool.dma_start(qiH[:], projT[ds(q * HQ + T_QI, HQ), :, 0:T_P].rearrange("h p n -> p h n")).then_inc(s_qiH, 16)
                    for u in range(BQ):
                        b = q * BQ + u
                        pool.wait_ge(s_itr, b)
                        alone(pool)
                        for p in range(PAGES):
                            page = pool.value_load(ptab[0:1, ds(b * PAGES + p, 1)], min_val=0, max_val=N_PHYS - 1)
                            pool.dma_start(ipg[:, p, :], tile_rows(t["cache_idx_k"][0], page)).then_inc(s_ipg, 16)
                    for u in range(BQ):
                        b = q * BQ + u
                        pool.wait_ge(s_sc8, b + 1)
                        alone(pool)
                        pool.dma_start(scores[ds(b * T_S, T_S), :], sc8[:]).then_inc(s_scst, 16)
                pool.wait_ge(s_bvecc, 1)
                pool.dma_start(biasP.rearrange("h (c n) -> h c n", n=BIAS_W),
                               bvec[:, VEC - BIAS_W:VEC].unsqueeze(1).to_broadcast([H, P, BIAS_W])).then_inc(s_bias, 16)
                pool.dma_start(biasS.rearrange("h (c n) -> h c n", n=LS + T_S),
                               bvec[:, 0:LS + T_S].unsqueeze(1).to_broadcast([H, T_S, LS + T_S])).then_inc(s_bias, 16)
                pool.wait_ge(s_bias, 32)
                pool.wait_ge(s_scst, 16 * NB_S)

            def pe_weave(pe, q, j):
                if j % 2 == 1:
                    h = j // 2
                    if h == 0:
                        pe.wait_ge(s_qiH, q * 16 + 16)
                    pe.wait_ge(p_relu, q * HQ + h)
                    nc.tensor.matmul(sbank[0][:, 0:P], qiH[:, h, 0:P], kiT[:, 0:P], start=True, stop=True)
                    nc.tensor.matmul(sbank[0][:, P:L2], qiH[:, h, P:T_P], kiT[:, 0:T_P], start=True,
                                     stop=True).then_inc(p_scored, 1)
                u, s = j // 8, j % 8
                b = q * BQ + u
                if s == 1:
                    pe.wait_ge(s_ipg, b * (16 * PAGES) + 16 * PAGES)
                    pe.wait_ge(s_sc8, b)
                    for p in range(PAGES):
                        tr = nc.tensor.transpose(sbank[1 + p // 4][:, (p % 4) * P:(p % 4 + 1) * P], ipg[:, p, :], ident[:])
                    tr.then_inc(s_itr, 1)
                for i, (p, n) in enumerate(PAIRS):
                    if s != 3 + i // 2:
                        continue
                    if i == 0:
                        pe.wait_ge(s_ikA, b + 1)
                        pe.wait_ge(s_iks, b + 1)
                    if i >= 2:
                        pe.wait_ge(s_prod, b * NPAIR + (i - 1))
                    pe.wait_ge(s_qiS, 16)
                    alone(pe)
                    for m in range(n):
                        cols = P if p < PAGES else T_S
                        mm = nc.tensor.matmul(sbank[1 + i % 2][0:cols, m * TQ:(m + 1) * TQ],
                                              ikT[:, (p + m) * P:(p + m) * P + cols],
                                              qiS[:, :, ds(b * T_S, T_S)].rearrange("p h t -> p t h"),
                                              start=True, stop=True)
                    mm.then_inc(s_sc, 1)
                if s == 7:
                    pe.wait_ge(s_red, b * NPAIR + NPAIR)
                    for p in range(PAGES):
                        nc.tensor.transpose(wide[0:T_S, 512 + p * P:512 + (p + 1) * P], scT[:, p, :], ident[:])
                    nc.tensor.transpose(wide[0:T_S, 512 + PAST:512 + LS], scT[0:T_S, PAGES, :],
                                        ident[0:T_S, 0:T_S]).then_inc(s_bt, 1)

            def act_weave(act, q, j):
                if j % 2 == 1:
                    h = j // 2
                    act.wait_ge(p_scored, q * HQ + (h + 1))
                    act.wait_ge(p_sum, q * HQ + h)
                    nc.scalar.activation(relu[:], sbank[0][:, 0:L2], ACT.Relu).then_inc(p_relu, 1)
                u, s = j // 8, j % 8
                b = q * BQ + u
                if s == 1:
                    act.wait_ge(s_itr, b + 1)
                    act.wait_ge(s_sc, b * NPAIR)
                    nc.scalar.activation(ikT[:, 0:PAST], wide[:, 512:512 + PAST], ACT.Copy).then_inc(s_ikA, 1)

            def dve_weave(dve, q, j):
                u, s = j // 8, j % 8
                b = q * BQ + u
                if s == 1:
                    dve.wait_ge(s_sc, b * NPAIR)
                    nc.vector.tensor_copy(ikT[:, PAST:LS], kiT[:, ds(b * T_S + T_P, T_S)]).then_inc(s_iks, 1)
                if j % 2 == 1:
                    h = q * HQ + j // 2
                    dve.wait_ge(p_relu, h + 1)
                    dve.wait_ge(p_sum, h)
                    for i, (a, z) in enumerate(((0, P), (P, L2))):
                        ins = nc.vector.scalar_tensor_tensor(scP[:, a:z], relu[:, a:z], wN[:, i, ds(h, 1)], scP[:, a:z],
                                                             ALU.mult, ALU.add)
                    ins.then_inc(p_sum, 1)
                for i, (p, n) in enumerate(PAIRS):
                    if s != 3 + i // 2:
                        continue
                    cols = P if p < PAGES else T_S
                    dve.wait_ge(s_sc, b * NPAIR + (i + 1))
                    dve.wait_ge(s_red, b * NPAIR + i)
                    if i == 0:
                        dve.wait_ge(s_wbc, 16)
                        dve.wait_ge(s_bt, b)
                    nc.vector.scalar_tensor_tensor(
                        prod[0:cols, 0:n, :], sbank[1 + i % 2][0:cols, 0:n * TQ].rearrange("p (a c) -> p a c", a=n), 0.0,
                        wbc[0:cols, ds(b * TQ, TQ)].unsqueeze(1).to_broadcast([cols, n, TQ]),
                        ALU.max, ALU.mult).then_inc(s_prod, 1)
                    dve.wait_ge(s_prod, b * NPAIR + (i + 1))
                    nc.vector.tensor_reduce(scT[0:cols, p:p + n, :].rearrange("p a t -> p (a t)"),
                                            prod[0:cols, 0:n, :].rearrange("p a (t h) -> p (a t) h", h=IH),
                                            AX.X, ALU.add).then_inc(s_red, 1)
                if s == 7:
                    dve.wait_ge(s_bt, b + 1)
                    dve.wait_ge(s_scst, b * 16)
                    nc.vector.tensor_copy(sc8[:], wide[0:T_S, 512:512 + LS]).then_inc(s_sc8, 1)

            @block.scalar
            def _(act):
                act.wait_ge(s_zero, 1)
                act_segment(act, "q", act_weave)

            @block.vector
            def _(dve):
                nc.vector.memset(scP, 0.0).then_inc(s_zero, 1)
                dve.wait_ge(s_zero, 1)
                dve_segment(dve, "q", dve_weave)
                dve.wait_ge(s_bvec, 1)
                nc.vector.tensor_copy(bvec[:], wide[0:H, 0:VEC]).then_inc(s_bvecc, 1)

            @block.tensor
            def _(pe):
                pe_segment(pe, "q", pe_weave)
                pe.wait_ge(s_onehot, 32)
                pe.wait_ge(s_sc8, NB_S)
                for c in range(0, VEC, 512):
                    z = min(VEC, c + 512)
                    mm = nc.tensor.matmul(wide[0:H, c:z], relb[:], onehot[:, c:z], start=True, stop=True)
                mm.then_inc(s_bvec, 1)

        with ExitStack() as ph:
            vT = sb("vT", [P, G, N], ctx=ph)
            kN = sb("kN", [P, 3, KVW], ctx=ph)
            negP = sb("negP", [P, L2], ctx=ph)
            top8 = sb("top8", [P, 2, 8], ctx=ph)
            keepP = sb("keepP", [P, L2], ctx=ph)
            stN = sb("stN", [NB_S * STATE, POOLW], ctx=ph)
            s_cin, t_step, s_kvT, s_kvt, s_kvc, s_outC, s_stt, s_stc = (sem(n) for n in (
                "s_cin", "t_step", "s_kvT", "s_kvt", "s_kvc", "s_outC", "s_stt", "s_stc"))
            block = ph.enter_context(nc.Block())
            NQ = segs["kv"][2]
            ROUNDS = TOPK_P // 8
            RQ = ROUNDS // NQ
            FILLS = [(src, i) for src in (0, 1) for i in range(3)]
            ST_FILLS = POOLW // P // 4

            @block.sync
            def _(sp):
                load_segment(sp, "kv")

            @block.gpsimd
            def _(pool):
                pool.dma_start(negP[:], t["c_causal"]).then_inc(s_cin, 16)
                pool.dma_start(stN[:], t["state_pool"][0].rearrange("b s c -> (b s) c")).then_inc(s_cin, 16)
                all_stored(pool, "kv")
                pool.dma_start(kT, tiles(projT, T_K, G)).then_inc(s_kvT, 16)
                pool.dma_start(vT[:], tiles(projT, T_V, G)).then_inc(s_kvT, 16)
                pool.wait_ge(s_kvc, len(FILLS))
                for o, src in ((2, kN), (3, vN)):
                    pool.dma_start(out[o][0, 0].rearrange("(a p) g d -> p a (g d)", p=P), src[:, 0:2, :]).then_inc(s_outC, 16)
                    pool.dma_start(out[o + 4][0].rearrange("b s g d -> (b s) (g d)"), src[0:N_S, 2, :]).then_inc(s_outC, 16)
                pool.wait_ge(s_outC, 64)

            def dve_weave(dve, q, j):
                per = QC // RQ
                r, s = j // per, j % per
                base = q * (4 * RQ) + 4 * r
                for i, (a, z) in enumerate(((0, P), (P, L2))):
                    if s == 2 * i:
                        dve.wait_ge(t_step, base + (2 * i + 1))
                        alone(dve)
                        nc.vector.max(top8[:, i, :], scP[:, a:z]).then_inc(t_step, 1)
                    if s == 2 * i + 1:
                        dve.wait_ge(t_step, base + (2 * i + 2))
                        alone(dve)
                        nc.vector.match_replace(scP[:, a:z], top8[:, i, :], scP[:, a:z], TAKEN).then_inc(t_step, 1)

            @block.scalar
            def _(act):
                act_segment(act, "kv")

            @block.vector
            def _(dve):
                dve.wait_ge(s_cin, 32)
                nc.vector.tensor_tensor(scP, scP, negP[:], ALU.add).then_inc(t_step, 1)
                dve_segment(dve, "kv", dve_weave)
                steps = 4 * ROUNDS + 1
                dve.wait_ge(t_step, steps)
                nc.vector.tensor_scalar(keepP[:], scP, TAKEN_EDGE, NEG, ALU.is_ge, ALU.mult).then_inc(t_step, 1)
                dve.wait_ge(t_step, steps + 1)
                nc.vector.tensor_tensor(maskP, keepP[:], negP[:], ALU.min).then_inc(t_step, 1)
                for f, (src, i) in enumerate(FILLS):
                    r = TT[i][1]
                    dve.wait_ge(s_kvt, f + 1)
                    nc.vector.tensor_copy((kN, vN)[src][0:r, i, :], sbank[f % 4][0:r, 0:KVW]).then_inc(s_kvc, 1)
                for f in range(ST_FILLS):
                    dve.wait_ge(s_stt, f + 1)
                    nc.vector.tensor_copy(stT[:, 4 * f:4 * f + 4, :], sbank[(f + 2) % 4][:, 0:4 * NB_S * STATE].rearrange(
                        "p (a n) -> p a n", a=4)).then_inc(s_stc, 1)

            @block.tensor
            def _(pe):
                pe_segment(pe, "kv")
                pe.wait_ge(s_kvT, 32)
                for f, (src, i) in enumerate(FILLS):
                    c0, r = TT[i]
                    if f >= 4:
                        pe.wait_ge(s_kvc, f - 3)
                    for g in range(G):
                        tr = nc.tensor.transpose(sbank[f % 4][0:r, g * P:(g + 1) * P], (kT, vT)[src][:, g, c0:c0 + r], ident[:])
                    tr.then_inc(s_kvt, 1)
                pe.wait_ge(s_cin, 32)
                for f in range(ST_FILLS):
                    if f < 2:
                        pe.wait_ge(s_kvc, f + 3)
                    else:
                        pe.wait_ge(s_kvc, 6)
                        pe.wait_ge(s_stc, f - 1) if f >= 4 else None
                    for a in range(4):
                        tr = nc.tensor.transpose(sbank[(f + 2) % 4][:, a * NB_S * STATE:(a + 1) * NB_S * STATE],
                                                 stN[:, (4 * f + a) * P:(4 * f + a + 1) * P],
                                                 ident[0:NB_S * STATE, 0:NB_S * STATE])
                    tr.then_inc(s_stt, 1)

        with ExitStack() as ph:
            qh = sb("qh", [P, T_P], ctx=ph)
            relh = sb("relh", [P, L2], ctx=ph)
            lg = sb("lg", [P, L2], ctx=ph)
            pr = sb("pr", [P, L2], ctx=ph)
            pT = sb("pT", [P, L2], ctx=ph)
            ohT = sb("ohT", [P, T_P], ctx=ph)
            nmx = sb("nmx", [P, 2], ctx=ph)
            rs = sb("rs", [P, 2], ctx=ph)
            ri = sb("ri", [P, 2], ctx=ph)
            scS = sb("scS", [N_S, LS], ctx=ph)
            negS = sb("negS", [N_S, T_S], ctx=ph)
            tops = sb("tops", [N_S, 8], ctx=ph)
            uin = sb("uin", [P, 4, N], ctx=ph)
            ubuf = [sb(f"ubuf{i}", [P, 4, UW], ctx=ph) for i in range(3)]
            cntr = sb("cntr", [P, NG, STATE + 1], ctx=ph)
            fix = sb("fix", [P, 4, STATE + 1], ctx=ph)
            dl = sb("dl", [P, 4, N], ctx=ph)
            wp = sb("wp", [P, 4, 4 * P], ctx=ph)
            obuf = sb("obuf", [P, 4, N], ctx=ph)
            ut = [ubuf[m][:].rearrange("p a n -> p (a n)")[:, 0:8 * P].rearrange("p (a n) -> p a n", a=8) for m in range(2)]
            utN = wp[:].rearrange("p a n -> p (a n)")
            ut_in, ut_t, ut_c, ut_out = (sem(n) for n in ("ut_in", "ut_t", "ut_c", "ut_out"))
            (d_in, a_q, a_rel, a_s, a_lg, a_mx, a_exp, a_ri, a_pr, a_pt, a_ptc, a_pv, a_oh, a_st, ts_step, ts_fin,
             u_in, u_step, u_st, w_in_, w_pe, w_ev, w_st) = (sem(n) for n in (
                 "d_in", "a_q", "a_rel", "a_s", "a_lg", "a_mx", "a_exp", "a_ri", "a_pr", "a_pt", "a_ptc", "a_pv", "a_oh",
                 "a_st", "ts_step", "ts_fin", "u_in", "u_step", "u_st", "w_in_", "w_pe", "w_ev", "w_st"))
            block = ph.enter_context(nc.Block())
            NQ = segs["u"][2]
            HPQ = H // (2 * NQ)
            ROUNDS = TOPK_S // 8
            RQ = ROUNDS // (2 * NQ)
            UN = UW - STATE - T_P
            assert HPQ == 2 and NQ == R and NG == NQ and G == 4

            @block.sync
            def _(sp):
                load_segment(sp, "u")
                load_segment(sp, "gb")

            def head_number(half, q, u):
                return q * HPQ + (half * NQ * HPQ + u)

            def head_load(pool, half, q, u):
                h, n = q + (2 * half + u) * R, head_number(half, q, u)
                pool.wait_ge(a_s, n)
                alone(pool)
                pool.dma_start(qh[:], tile_rows(projT, h)[:, 0:T_P]).then_inc(a_q, 16)
                pool.wait_ge(a_lg, n)
                alone(pool)
                bias = biasP[ds(h, 1), P - 1:P - 1 + P * (BIAS_W - 1)].rearrange("o (a n) -> (o a) n", n=BIAS_W - 1)
                pool.dma_start(relh[:, P:L2], bias[:, 0:T_P]).then_inc(a_rel, 16)
                pool.dma_start(relh[:, 0:P], bias[:, P:T_P]).then_inc(a_rel, 16)

            def head_store(pool, half, q, u):
                h, n = q + (2 * half + u) * R, head_number(half, q, u)
                pool.wait_ge(a_oh, n + 1)
                alone(pool)
                pool.dma_start(tile_rows(oT, h)[:, 0:T_P], ohT[:]).then_inc(a_st, 16)

            U_STEPS = [0]

            def pool_steps(pool, g):
                win = WINS[g]
                base = sum(U_STEPS)
                n_ = [base]

                def done(ins):
                    n_[0] += 1
                    ins.then_inc(u_step, 1)
                    pool.wait_ge(u_step, n_[0])

                pool.wait_ge(stored[0], 16 * (segs["u"][4] + g + 1))
                pool.wait_ge(stored[1], 16 * (segs["u"][4] + g + 1))
                pool.dma_start(uin[:], tiles(projT, T_U + 4 * g, 4)).then_inc(u_in, 16)
                pool.wait_ge(u_in, 16 * (g + 1))
                U, A, B = ubuf
                if g:
                    pool.wait_ge(u_st, 16 * g)
                nc.gpsimd.memset(U[:, :, 0:STATE], 0.0)
                nc.gpsimd.tensor_copy(U[:, :, STATE:STATE + T_P], uin[:, :, 0:T_P])
                for a in range(4):
                    rows = U[:, a, STATE + T_P:UW].rearrange("p (b n) -> p b n", b=NB_S)
                    nc.gpsimd.tensor_copy(rows[:, :, 0:STATE], stT[:, 4 * g + a, :].rearrange("p (b n) -> p b n", b=NB_S))
                    ins = nc.gpsimd.tensor_copy(rows[:, :, STATE:], uin[:, a, T_P:N].rearrange("p (b n) -> p b n", b=NB_S))
                done(ins)
                src, w, lost = U, 1, 0
                while w < win:
                    dst = A if src is not A else B
                    done(nc.gpsimd.tensor_tensor(dst[:, :, lost + w:UW], src[:, :, lost + w:UW], src[:, :, lost:UW - w], ALU.add))
                    src, lost, w = dst, lost + w, 2 * w
                other = A if src is B else B
                done(nc.gpsimd.tensor_tensor(fix[:, :, 0:STATE], src[:, :, STATE:2 * STATE],
                                             cntr[:, g:g + 1, 0:STATE].to_broadcast([P, 4, STATE]), ALU.mult))
                done(nc.gpsimd.tensor_scalar(other[:, :, STATE:UW], src[:, :, STATE:UW], 1.0 / win, None, ALU.mult))
                dp = src[:].rearrange("p a n -> p (a n)")[:, 0:4 * N].rearrange("p (a n) -> p a n", a=4)
                nc.gpsimd.tensor_tensor(dp[:, :, 0:STATE], fix[:, :, 0:STATE], U[:, :, STATE:2 * STATE], ALU.subtract)
                ins = nc.gpsimd.tensor_tensor(dp[:, :, STATE:T_P], other[:, :, 2 * STATE:STATE + T_P],
                                              U[:, :, 2 * STATE:STATE + T_P], ALU.subtract)
                for a in range(4):
                    m_, u_ = (x[:, a, STATE + T_P:UW].rearrange("p (b n) -> p b n", b=NB_S)[:, :, STATE:] for x in (other, U))
                    ins = nc.gpsimd.tensor_tensor(dp[:, a, T_P:N].rearrange("p (b n) -> p b n", b=NB_S), m_, u_, ALU.subtract)
                done(ins)
                pool.dma_start(tiles(poolT, 4 * g, 4), dp).then_inc(u_st, 16)
                U_STEPS.append(n_[0] - base)

            @block.gpsimd
            def _(pool):
                pool.dma_start(scS[:], scores).then_inc(d_in, 16)
                pool.dma_start(negS[:], t["c_causal_s"]).then_inc(d_in, 16)
                pool.dma_start(cntr[:], t["c_count"]).then_inc(d_in, 16)
                pool.wait_ge(d_in, 48)
                head_load(pool, 0, 0, 0)
                for q in range(NQ):
                    head_load(pool, 0, q, 1)
                    if q:
                        pool_steps(pool, q - 1)
                    head_store(pool, 0, q, 0)
                    if q + 1 < NQ:
                        head_load(pool, 0, q + 1, 0)
                    else:
                        head_load(pool, 1, 0, 0)
                    head_store(pool, 0, q, 1)

                def group_load(q):
                    pool.wait_ge(w_pe, q * 4)
                    pool.wait_ge(u_st, q * 16 + 16)
                    alone(pool)
                    pool.dma_start(wp[:], t["w_pool"][0, ds(q, 1)].rearrange("g (a p) d -> p (g a) d", p=P)).then_inc(w_in_, 16)
                    pool.dma_start(dl[:], tiles(poolT, q * 4, 4)).then_inc(w_in_, 16)

                def group_store(q):
                    pool.wait_ge(w_ev, q * 4 + 4)
                    alone(pool)
                    pool.dma_start(tiles(mixT, q * 4, 4), obuf[:]).then_inc(w_st, 16)

                group_load(0)
                pool_steps(pool, NQ - 1)
                for m in range(2):
                    pool.dma_start(ut[m], projT[T_U + 8 * m:T_U + 8 * m + 8, :, N - P:N].rearrange("a p n -> p a n")).then_inc(ut_in, 16)

                def gate_quad(q, more):
                    head_load(pool, 1, q, 1)
                    head_store(pool, 1, q, 0)
                    if more:
                        head_load(pool, 1, q + 1, 0)
                    head_store(pool, 1, q, 1)
                    group_store(q)
                    if more:
                        group_load(q + 1)
                with pool.Fori(0, NQ - 1) as q:
                    gate_quad(q, True)
                gate_quad(NQ - 1, False)
                pool.wait_ge(ut_c, POOLW // P // 4)
                first = P - N_S - STATE
                pool.dma_start(out[5][0, 0], utN[first:first + STATE, :]).then_inc(ut_out, 16)
                for b in range(NB_S):
                    r0 = P - N_S + b * T_S
                    pool.dma_start(out[9][0, b, STATE - T_S:STATE], utN[r0:r0 + T_S, :]).then_inc(ut_out, 16)
                pool.dma_start(out[9][0, :, 0:STATE - T_S, :], t["state_pool"][0, :, T_S:STATE, :]).then_inc(ut_out, 16)
                pool.wait_ge(ut_out, 16 * (NB_S + 2))
                pool.wait_ge(w_st, 16 * NG)
                pool.wait_ge(a_st, 16 * H)

            def pe_weave(half):
                def weave(pe, q, j):
                    u, s = j // 8, j % 8
                    g = 2 * half + u
                    n = q * HPQ + (half * NQ * HPQ + u)
                    if s == 1:
                        pe.wait_ge(a_q, n * 16 + 16)
                        pe.wait_ge(a_lg, n)
                        nc.tensor.matmul(sbank[0][:, 0:L2], identb[:], maskP, start=True, stop=False)
                        nc.tensor.matmul(sbank[0][:, 0:P], qh[:, 0:P], kT[:, g, 0:P], start=False, stop=False)
                        nc.tensor.matmul(sbank[0][:, P:L2], qh[:, P:T_P], kT[:, g, 0:T_P], start=False,
                                         stop=True).then_inc(a_s, 1)
                    if s == 4:
                        pe.wait_ge(a_pr, n + 1)
                        pe.wait_ge(a_ptc, n)
                        for i in range(3):
                            tr = nc.tensor.transpose(sbank[1][:, i * P:(i + 1) * P], pr[:, i * P:(i + 1) * P], ident[:])
                        tr.then_inc(a_pt, 1)
                    if s == 6:
                        pe.wait_ge(a_ptc, n + 1)
                        pe.wait_ge(a_oh, n)
                        gv = slice(g * P, (g + 1) * P)
                        nc.tensor.matmul(sbank[2][:, 0:P], vN[:, 0, gv], pT[:, 0:P], start=True, stop=True)
                        nc.tensor.matmul(sbank[2][:, P:T_P], vN[:, 0, gv], pT[:, P:2 * P], start=True, stop=False)
                        nc.tensor.matmul(sbank[2][:, P:T_P], vN[:, 1, gv], pT[:, 2 * P:L2], start=False,
                                         stop=True).then_inc(a_pv, 1)
                    if half and j % 4 == 3:
                        dt = j // 4
                        if dt == 0:
                            pe.wait_ge(w_in_, q * 32 + 32)
                        pe.wait_ge(w_ev, q * 4 + dt)
                        for a in range(4):
                            mm = nc.tensor.matmul(sbank[3][:, 0:N], wp[:, a, dt * P:(dt + 1) * P], dl[:, a, :],
                                                  start=a == 0, stop=a == 3)
                        mm.then_inc(w_pe, 1)
                return weave

            def act_weave(half):
                def weave(act, q, j):
                    u, s = j // 8, j % 8
                    n = q * HPQ + (half * NQ * HPQ + u)
                    if s == 2:
                        act.wait_ge(a_mx, n + 1)
                        act.wait_ge(a_pt, n)
                        for i, (a, z) in enumerate(((0, P), (P, L2))):
                            ins = nc.scalar.activation(pr[:, a:z], lg[:, a:z], ACT.Exp, bias=nmx[:, i:i + 1],
                                                       accum_out=rs[:, i:i + 1])
                        ins.then_inc(a_exp, 1)
                    if s == 4:
                        act.wait_ge(a_pt, n + 1)
                        act.wait_ge(a_pv, n)
                        nc.scalar.activation(pT[:], sbank[1][:, 0:L2], ACT.Copy).then_inc(a_ptc, 1)
                    if s == 6:
                        act.wait_ge(a_pv, n + 1)
                        act.wait_ge(a_st, n * 16)
                        nc.scalar.activation(ohT[:], sbank[2][:, 0:T_P], ACT.Copy).then_inc(a_oh, 1)
                return weave

            def dve_weave(half):
                def weave(dve, q, j):
                    u, s = j // 8, j % 8
                    n = q * HPQ + (half * NQ * HPQ + u)
                    if s == 1:
                        dve.wait_ge(a_s, n + 1)
                        dve.wait_ge(a_rel, n * 32 + 32)
                        dve.wait_ge(a_exp, n)
                        nc.vector.scalar_tensor_tensor(lg[:], sbank[0][:, 0:L2], SCALE, relh[:], ALU.mult,
                                                       ALU.add).then_inc(a_lg, 1)
                        dve.wait_ge(a_lg, n + 1)
                        for i, (a, z) in enumerate(((0, P), (P, L2))):
                            ins = nc.vector.tensor_reduce(nmx[:, i:i + 1], lg[:, a:z], AX.X, ALU.max, negate=True)
                        ins.then_inc(a_mx, 1)
                    if s == 3:
                        dve.wait_ge(a_exp, n + 1)
                        nc.vector.reciprocal(ri[:], rs[:]).then_inc(a_ri, 1)
                        dve.wait_ge(a_ri, n + 1)
                        for i, (a, z) in enumerate(((0, P), (P, L2))):
                            ins = nc.vector.tensor_scalar(pr[:, a:z], pr[:, a:z], ri[:, i:i + 1], None, ALU.mult)
                        ins.then_inc(a_pr, 1)
                    if half and j % 4 == 3:
                        dt = j // 4
                        dve.wait_ge(w_pe, q * 4 + (dt + 1))
                        if dt == 0:
                            dve.wait_ge(w_st, q * 16)
                        nc.vector.tensor_scalar(obuf[:, dt, :], sbank[3][:, 0:N], poolscT[:, ds(q * 4 + dt, 1)], None,
                                                ALU.mult).then_inc(w_ev, 1)
                    if j % (QC // RQ) in (0, 2):
                        k = (q + half * NQ) * (2 * RQ) + (2 * (j // (QC // RQ)) + (j % (QC // RQ)) // 2)
                        dve.wait_ge(ts_step, k + 1)
                        alone(dve)
                        if j % (QC // RQ) == 0:
                            nc.vector.max(tops[:], scS[:]).then_inc(ts_step, 1)
                        else:
                            nc.vector.match_replace(scS[:], tops[:], scS[:], TAKEN).then_inc(ts_step, 1)
                return weave

            @block.scalar
            def _(act):
                act_segment(act, "u", act_weave(0))
                act_segment(act, "gb", act_weave(1))

            @block.vector
            def _(dve):
                dve.wait_ge(d_in, 48)
                nc.vector.memset(maskS, 0.0).then_inc(ts_fin, 1)
                nc.vector.tensor_tensor(scS[:, PAST:LS], scS[:, PAST:LS], negS[:], ALU.add).then_inc(ts_step, 1)
                dve_segment(dve, "u", dve_weave(0))
                dve_segment(dve, "gb", dve_weave(1))
                dve.wait_ge(ts_step, 2 * ROUNDS + 1)
                dve.wait_ge(ts_fin, 1)
                nc.vector.tensor_scalar(maskS[0:N_S, :], scS[:], TAKEN_EDGE, NEG, ALU.is_ge, ALU.mult).then_inc(ts_fin, 1)
                for m in range(POOLW // P // 4):
                    dve.wait_ge(ut_t, m + 1)
                    nc.vector.tensor_copy(utN[:, 4 * P * m:4 * P * (m + 1)], sbank[m]).then_inc(ut_c, 1)

            @block.tensor
            def _(pe):
                pe_segment(pe, "u", pe_weave(0))
                pe_segment(pe, "gb", pe_weave(1))
                pe.wait_ge(ut_in, 32)
                pe.wait_ge(a_oh, H)
                pe.wait_ge(w_ev, 4 * NG)
                for m in range(POOLW // P // 4):
                    for a in range(4):
                        k = 4 * m + a
                        tr = nc.tensor.transpose(sbank[m][:, a * P:(a + 1) * P], ut[k // 8][:, k % 8, :], ident[:])
                    tr.then_inc(ut_t, 1)

        with ExitStack() as ph:
            pages = sb("pages", [P, PAGES, KVW], ctx=ph)
            KTs = sb("KTs", [P, G, LS], ctx=ph)
            vnew = sb("vnew", [T_S, KVW], ctx=ph)
            rel = sb("rel", [P, LS], ctx=ph)
            lgS = sb("lgS", [P, LS], ctx=ph)
            pTs = sb("pTs", [P, PAGES + 1, P], ctx=ph)
            qb = sb("qb", [P, P], ctx=ph)
            pick = sb("pick", [P, P], BF16, ctx=ph)
            st1 = sb("st1", [P, 4], ctx=ph)
            gbt = sb("gbt", [P, N], ctx=ph)
            obt = sb("obt", [P, N], ctx=ph)
            et = sb("et", [P, N], ctx=ph)
            (e_in, e_rel, e_k, e_v, e_pick, e_kt, e_ktc, e_kn, e_qb, e_s, e_lg, e_mx, e_exp, e_ri, e_pr, e_pt, e_ptA,
             e_pv, e_o, g_in, g_exp, g_step, g_st, e_out, e_tail, e_tailc) = (sem(n) for n in (
                 "e_in", "e_rel", "e_k", "e_v", "e_pick", "e_kt", "e_ktc", "e_kn", "e_qb", "e_s", "e_lg", "e_mx", "e_exp",
                 "e_ri", "e_pr", "e_pt", "e_ptA", "e_pv", "e_o", "g_in", "g_exp", "g_step", "g_st", "e_out", "e_tail",
                 "e_tailc"))
            block = ph.enter_context(nc.Block())
            NQ = segs["ga"][2]
            BQ = NB_S // NQ
            assert BQ == 2 and PAGES == 8 and POOLW // P == 4 * NQ

            @block.sync
            def _(sp):
                load_segment(sp, "ga")

            @block.gpsimd
            def _(pool):
                pool.dma_start(qS, projT[T_Q:T_Q + H, :, T_P:N].rearrange("h p n -> p h n")).then_inc(e_in, 16)
                for h in range(H):
                    bias = biasS[h:h + 1, T_S - 1:T_S - 1 + T_S * (LS + T_S - 1)].rearrange("o (a n) -> (o a) n", n=LS + T_S - 1)
                    pool.dma_start(rel[h * T_S:(h + 1) * T_S, :], bias[:, 0:LS]).then_inc(e_rel, 16)
                with pool.Fori(0, NQ) as q:
                    for u in range(BQ):
                        b = q * BQ + u
                        pool.wait_ge(e_pv, b)
                        alone(pool)
                        for kind in (0, 1):
                            if kind:
                                pool.wait_ge(e_kt, b * PAGES + PAGES)
                                alone(pool)
                            for p in range(PAGES):
                                page = pool.value_load(ptab[0:1, ds(b * PAGES + p, 1)], min_val=0, max_val=N_PHYS - 1)
                                src = t[("cache_k", "cache_v")[kind]][0].rearrange("n r g d -> n r (g d)")
                                pool.dma_start(pages[:, p, :], tile_rows(src, page)).then_inc((e_k, e_v)[kind], 16)
                            if not kind:
                                pool.dma_start(pick[:], tile_rows(t["c_pick"], b)).then_inc(e_pick, 16)
                                pool.dma_start(vnew[:], out[7][0, ds(b, 1)].rearrange("b s g d -> (b s) (g d)")).then_inc(e_pick, 16)
                        for i in range(2):
                            k = q * 4 + (2 * u + i)
                            pool.wait_ge(g_step, k * 4)
                            pool.wait_ge(g_st, k * 16)
                            alone(pool)
                            pool.dma_start(gbt[:], tile_rows(projT, k + T_GB)).then_inc(g_in, 16)
                            pool.dma_start(obt[:], tile_rows(mixT, k)).then_inc(g_in, 16)
                            pool.wait_ge(g_step, k * 4 + 4)
                            alone(pool)
                            pool.dma_start(tile_rows(poolT, k), obt[:]).then_inc(g_st, 16)
                pool.wait_ge(e_o, NB_S)
                pool.dma_start(oT[:, :, T_P:N].rearrange("h p n -> p h n"), qS).then_inc(e_out, 16)
                pool.wait_ge(e_out, 16)
                pool.wait_ge(g_st, 16 * (POOLW // P))

            def pe_weave(pe, q, j):
                u, s = j // 8, j % 8
                b = q * BQ + u
                if s in (1, 2):
                    for p in range(4 * (s - 1), 4 * s):
                        pe.wait_ge(e_k, b * (16 * PAGES) + 16 * PAGES)
                        if p < 4:
                            pe.wait_ge(e_ptA, b)
                            pe.wait_ge(e_o, b)
                        else:
                            pe.wait_ge(e_ktc, b * PAGES + (p - 3))
                        for g in range(G):
                            tr = nc.tensor.transpose(sbank[p % 4][:, g * P:(g + 1) * P], pages[:, p, g * P:(g + 1) * P], ident[:])
                        tr.then_inc(e_kt, 1)
                if s == 4:
                    pe.wait_ge(e_pick, b * 32 + 32)
                    pe.wait_ge(e_ktc, b * PAGES + PAGES)
                    pe.wait_ge(e_kn, b + 1)
                    pe.wait_ge(e_qb, b + 1)
                    for c in range(0, LS, 512):
                        z = min(LS, c + 512)
                        nc.tensor.matmul(wide[:, c:z], pick[:], maskS[:, c:z], start=True, stop=True)
                        for g in range(G):
                            mm = nc.tensor.matmul(wide[32 * g:32 * g + 32, c:z], qb[:, 32 * g:32 * g + 32], KTs[:, g, c:z],
                                                  start=False, stop=True, skip_group_check=True)
                    mm.then_inc(e_s, 1)
                if s == 6:
                    pe.wait_ge(e_pr, b + 1)
                    for p in range(PAGES + 1):
                        r = P if p < PAGES else T_S
                        tr = nc.tensor.transpose(wide[0:r, p * P:(p + 1) * P], lgS[:, p * P:p * P + r], ident[:])
                    tr.then_inc(e_pt, 1)
                if s == 7:
                    pe.wait_ge(e_ptA, b + 1)
                    pe.wait_ge(e_v, b * (16 * PAGES) + 16 * PAGES)
                    for g in range(G):
                        for p in range(PAGES + 1):
                            lhs = pages[:, p, g * P:(g + 1) * P] if p < PAGES else vnew[:, g * P:(g + 1) * P]
                            r = P if p < PAGES else T_S
                            mm = nc.tensor.matmul(sbank[3][:, 32 * g:32 * g + 32], lhs, pTs[0:r, p, 32 * g:32 * g + 32],
                                                  start=p == 0, stop=p == PAGES)
                    mm.then_inc(e_pv, 1)

            def act_weave(act, q, j):
                u, s = j // 8, j % 8
                b = q * BQ + u
                if s == 2:
                    act.wait_ge(e_s, b)
                if s in (1, 2):
                    if s == 1:
                        act.wait_ge(e_s, b)
                    for p in range(4 * (s - 1), 4 * s):
                        act.wait_ge(e_kt, b * PAGES + (p + 1))
                        nc.scalar.activation(KTs[:, :, p * P:(p + 1) * P], sbank[p % 4].rearrange("p (g n) -> p g n", g=G),
                                             ACT.Copy).then_inc(e_ktc, 1)
                if s == 5:
                    act.wait_ge(e_mx, b + 1)
                    nc.scalar.activation(lgS[:], lgS[:], ACT.Exp, bias=st1[:, 0:1], accum_out=st1[:, 1:2]).then_inc(e_exp, 1)
                if s == 6:
                    act.wait_ge(e_pt, b + 1)
                    act.wait_ge(e_pv, b)
                    nc.scalar.activation(pTs[:, 0:PAGES, :], wide[:, 0:PAST].rearrange("p (a n) -> p a n", n=P), ACT.Copy)
                    nc.scalar.activation(pTs[0:T_S, PAGES, :], wide[0:T_S, PAST:PAST + P], ACT.Copy).then_inc(e_ptA, 1)
                if s == 7:
                    act.wait_ge(e_pv, b + 1)
                    nc.scalar.activation(qS[:, :, ds(b * T_S, T_S)], sbank[3][:, 0:P].rearrange("p (h n) -> p h n", h=H),
                                         ACT.Copy).then_inc(e_o, 1)
                if s in (5, 7):
                    k = q * 4 + (2 * u + (s - 5) // 2)
                    act.wait_ge(g_in, k * 32 + 32)
                    act.wait_ge(g_step, k * 4)
                    nc.scalar.activation(et[:], gbt[:], ACT.Exp, scale=-1.0).then_inc(g_exp, 1)

            def dve_weave(dve, q, j):
                u, s = j // 8, j % 8
                b = q * BQ + u
                if s == 2:
                    dve.wait_ge(e_in, 16)
                    dve.wait_ge(e_s, b)
                    nc.vector.tensor_copy(KTs[:, :, PAST:LS], kT[:, :, ds(b * T_S + T_P, T_S)]).then_inc(e_kn, 1)
                    nc.vector.tensor_copy(qb[:].rearrange("p (h n) -> p h n", h=H), qS[:, :, ds(b * T_S, T_S)]).then_inc(e_qb, 1)
                if s == 4:
                    dve.wait_ge(e_rel, 16 * H)
                    dve.wait_ge(e_s, b + 1)
                    dve.wait_ge(e_pt, b)
                    nc.vector.scalar_tensor_tensor(lgS[:], wide[:, 0:LS], SCALE, rel[:], ALU.mult, ALU.add).then_inc(e_lg, 1)
                    dve.wait_ge(e_lg, b + 1)
                    nc.vector.tensor_reduce(st1[:, 0:1], lgS[:], AX.X, ALU.max, negate=True).then_inc(e_mx, 1)
                if s == 5:
                    dve.wait_ge(e_exp, b + 1)
                    nc.vector.reciprocal(st1[:, 2:3], st1[:, 1:2]).then_inc(e_ri, 1)
                    dve.wait_ge(e_ri, b + 1)
                    nc.vector.tensor_scalar(lgS[:], lgS[:], st1[:, 2:3], None, ALU.mult).then_inc(e_pr, 1)
                if s in (5, 7):
                    k = q * 4 + (2 * u + (s - 5) // 2)
                    dve.wait_ge(g_exp, k + 1)
                    nc.vector.tensor_scalar(et[:], et[:], 1.0, None, ALU.add).then_inc(g_step, 1)
                    nc.vector.tensor_tensor(obt[:], obt[:], gbt[:], ALU.mult).then_inc(g_step, 1)
                    dve.wait_ge(g_step, k * 4 + 2)
                    nc.vector.reciprocal(et[:], et[:]).then_inc(g_step, 1)
                    dve.wait_ge(g_step, k * 4 + 3)
                    nc.vector.tensor_tensor(obt[:], obt[:], et[:], ALU.mult).then_inc(g_step, 1)

            @block.scalar
            def _(act):
                act_segment(act, "ga", act_weave)

            @block.vector
            def _(dve):
                dve_segment(dve, "ga", dve_weave)

            @block.tensor
            def _(pe):
                pe_segment(pe, "ga", pe_weave)

        with ExitStack() as ph:
            y = [sb(f"y{i}", [P, D], ctx=ph) for i in range(3)]
            gq = sb("gq", [P, 4 * P], ctx=ph)
            sqj = sb("sqj", [P, 4 * P], ctx=ph)
            NQ = segs["out"][2]
            sq = sb("sq", [P, 3, NQ], ctx=ph)
            sqs = sb("sqs", [P, 3], ctx=ph)
            ms = sb("ms", [P, 3], ctx=ph)
            rt = sb("rt", [P, 3], ctx=ph)
            rf = sb("rf", [P, 3], ctx=ph)
            (f_in, f_gin, f_exp, f_step, f_hi, f_lo, f_t, f_add, f_sq, f_gq, f_g, f_sum, f_ms, f_rt, f_rf, f_out,
             f_x) = (sem(n) for n in (
                 "f_in", "f_gin", "f_exp", "f_step", "f_hi", "f_lo", "f_t", "f_add", "f_sq", "f_gq", "f_g", "f_sum", "f_ms",
                 "f_rt", "f_rf", "f_out", "f_x"))
            f_y = [sem(f"f_y{i}") for i in range(3)]
            block = ph.enter_context(nc.Block())
            MIX = KT // 4
            HALF = MIX // 2
            FOUR = 4 * N
            spots = [y[i][:, k * FOUR:(k + 1) * FOUR] for i in range(3) for k in range(D // FOUR)] + [
                keep[:, k * FOUR:(k + 1) * FOUR] for k in range(4)]
            spots = [x.rearrange("p (a n) -> p a n", a=4) for x in spots]
            om = spots[0:MIX]
            gm = spots[MIX:MIX + HALF]
            em = spots[MIX + HALF]
            rows = [t["x_prompt"][0, 0:P], t["x_prompt"][0, P:T_P], t["x_sample"].rearrange("b s d -> (b s) d")]
            outs = [out[0][0, 0:P], out[0][0, P:T_P], out[1].rearrange("b s d -> (b s) d")]

            @block.sync
            def _(sp):
                load_segment(sp, "out")

            @block.gpsimd
            def _(pool):
                all_stored(pool, "ga")
                for m in range(HALF):
                    pool.dma_start(om[m], tiles(poolT, 4 * m, 4)).then_inc(f_in, 16)
                for m in range(HALF):
                    pool.dma_start(om[HALF + m], tiles(oT, 4 * m, 4)).then_inc(f_gin, 16)
                    pool.dma_start(gm[m], tiles(projT, T_GA + 4 * m, 4)).then_inc(f_gin, 16)
                pool.wait_ge(f_lo, MIX)
                for i in range(3):
                    pool.dma_start(y[i][0:TT[i][1], :], rows[i]).then_inc(f_x, 16)
                with pool.Fori(0, NQ) as q:
                    pool.wait_ge(f_g, q)
                    alone(pool)
                    pool.dma_start(gq[:], t["final_g"].rearrange("(o d) -> o d", o=1)[
                        :, ds(q * (4 * P), 4 * P)].to_broadcast([P, 4 * P])).then_inc(f_gq, 16)
                    pool.wait_ge(f_gq, q * 16 + 16)
                    pool.wait_ge(f_sq, q * 3 + 3)
                    for i in range(3):
                        cols = y[i][0:TT[i][1], ds(q * (4 * P), 4 * P)]
                        ins = nc.gpsimd.tensor_tensor(cols, cols, gq[0:TT[i][1], :], ALU.mult)
                    ins.then_inc(f_g, 1)
                for i in range(3):
                    pool.wait_ge(f_y[i], 1)
                    pool.dma_start(outs[i], y[i][0:TT[i][1], :]).then_inc(f_out, 16)
                pool.wait_ge(f_out, 48)

            def squares(act, q):
                for i in range(3):
                    r = TT[i][1]
                    act.wait_ge(f_add, q * 3 + (i + 1))
                    act.wait_ge(f_sq, q * 3 + i)
                    nc.scalar.activation(sqj[0:r, :], y[i][0:r, ds(q * (4 * P), 4 * P)], ACT.Square,
                                         accum_out=sq[0:r, i, ds(q, 1)]).then_inc(f_sq, 1)

            def act_mix(act, m):
                if m < HALF:
                    act.wait_ge(f_in, 16 * HALF)
                else:
                    act.wait_ge(f_gin, 32 * HALF)
                    act.wait_ge(f_step, 4 * (m - HALF))
                    nc.scalar.activation(em, gm[m - HALF], ACT.Exp, scale=-1.0).then_inc(f_exp, 1)
                    act.wait_ge(f_step, 4 * (m - HALF + 1))
                k0 = (4 * m + KT // 2) % KT
                nc.scalar.activation(XH[:, k0:k0 + 4, :], om[m], ACT.Copy).then_inc(f_hi, 1)

            def dve_mix(dve, m):
                if m >= HALF:
                    n = 4 * (m - HALF)
                    dve.wait_ge(f_exp, m - HALF + 1)
                    nc.vector.tensor_scalar(em, em, 1.0, None, ALU.add).then_inc(f_step, 1)
                    nc.vector.tensor_tensor(om[m], om[m], gm[m - HALF], ALU.mult).then_inc(f_step, 1)
                    dve.wait_ge(f_step, n + 2)
                    nc.vector.reciprocal(em, em).then_inc(f_step, 1)
                    dve.wait_ge(f_step, n + 3)
                    nc.vector.tensor_tensor(om[m], om[m], em, ALU.mult).then_inc(f_step, 1)
                k0 = (4 * m + KT // 2) % KT
                dve.wait_ge(f_hi, m + 1)
                nc.vector.tensor_tensor(XL[:, k0:k0 + 4, :], om[m], XH[:, k0:k0 + 4, :].bitcast(F32),
                                        ALU.subtract).then_inc(f_lo, 1)

            def mix_weave(mix):
                def weave(eng, q, j):
                    if j < HALF:
                        mix(eng, HALF + j)
                return weave

            def act_weave(act, q, j):
                if j == 4:
                    squares(act, q - 1)

            def residual(dve, q):
                for i in range(3):
                    r = TT[i][1]
                    cols = y[i][0:r, ds(q * (4 * P), 4 * P)]
                    if i == 0:
                        dve.wait_ge(f_x, 48)
                        dve.wait_ge(f_t, q + 1)
                    nc.vector.tensor_tensor(cols, sbank[i][0:r, :], cols, ALU.add).then_inc(f_add, 1)

            def dve_weave(dve, q, j):
                if j == 2:
                    residual(dve, q - 1)

            def turn(pe, q):
                quad0 = segs["out"][4]
                pe.wait_ge(evac[0], q + (quad0 + 1))
                pe.wait_ge(evac[1], q + (quad0 + 2))
                pe.wait_ge(f_add, q * 3)
                for i, (c0, r) in enumerate(TT):
                    for n in range(4):
                        tr = nc.tensor.transpose(sbank[i][0:r, n * P:(n + 1) * P], stg[n // 2][:, n % 2, c0:c0 + r], ident[:])
                tr.then_inc(f_t, 1)

            def pe_weave(pe, q, j):
                if j == 2:
                    turn(pe, q - 1)

            @block.scalar
            def _(act):
                for m in range(HALF):
                    act_mix(act, m)
                act_quad(act, "out", 0, mix_weave(act_mix), turned=f_t)
                with act.Fori(1, NQ - 1) as q:
                    act_quad(act, "out", q, act_weave, turned=f_t)
                act_quad(act, "out", NQ - 1, act_weave, True, turned=f_t)
                squares(act, NQ - 1)
                act.wait_ge(f_ms, 1)
                nc.scalar.activation(rt[0:N_S, :], ms[0:N_S, :], ACT.Sqrt)
                nc.scalar.activation(rt[N_S:P, 0:2], ms[N_S:P, 0:2], ACT.Sqrt).then_inc(f_rt, 1)
                act.wait_ge(f_rf, 1)
                act.wait_ge(f_g, NQ)
                nc.scalar.activation(y[1][:], y[1][:], ACT.Copy, scale=rf[:, 1:2]).then_inc(f_y[1], 1)

            @block.vector
            def _(dve):
                for m in range(HALF):
                    dve_mix(dve, m)
                dve_quad(dve, "out", 0, mix_weave(dve_mix))
                with dve.Fori(1, NQ - 1) as q:
                    dve_quad(dve, "out", q, dve_weave)
                dve_quad(dve, "out", NQ - 1, dve_weave, True)
                residual(dve, NQ - 1)
                dve.wait_ge(f_sq, 3 * NQ)
                for i in range(3):
                    r = TT[i][1]
                    ins = nc.vector.tensor_reduce(sqs[0:r, i:i + 1], sq[0:r, i, :], AX.X, ALU.add)
                ins.then_inc(f_sum, 1)
                dve.wait_ge(f_sum, 1)
                for i in range(3):
                    r = TT[i][1]
                    ins = nc.vector.tensor_scalar(ms[0:r, i:i + 1], sqs[0:r, i:i + 1], 1.0 / D, EPS, ALU.mult, ALU.add)
                ins.then_inc(f_ms, 1)
                dve.wait_ge(f_rt, 1)
                nc.vector.reciprocal(rf[0:N_S, :], rt[0:N_S, :])
                nc.vector.reciprocal(rf[N_S:P, 0:2], rt[N_S:P, 0:2]).then_inc(f_rf, 1)
                dve.wait_ge(f_rf, 1)
                dve.wait_ge(f_g, NQ)
                for i in (0, 2):
                    r = TT[i][1]
                    nc.vector.tensor_scalar(y[i][0:r, :], y[i][0:r, :], rf[0:r, i:i + 1], None, ALU.mult).then_inc(f_y[i], 1)

            @block.tensor
            def _(pe):
                pe_quad(pe, "out", 0, before=lambda pe, j: pe.wait_ge(f_lo, min(j, CH - 1) + 1))
                with pe.Fori(1, NQ) as q:
                    pe_quad(pe, "out", q, pe_weave)
                turn(pe, NQ - 1)


_INS = ["x_prompt", "x_sample", "cache_k", "cache_v", "cache_idx_k", "state_pool", "page_table", "rel_bias", "ln_g",
        "w_in", "w_pool", "pool_scale", "w_out", "final_g"]


def kernel(**inputs):
    import math

    import ml_dtypes
    import concourse.bacc as _bacc
    from concourse.bass_utils import run_bass_kernel_spmd as _run

    nc = _bacc.Bacc("TRN2", target_bir_lowering=False, num_devices=1, dynamic_dma_scratch_size=8192)
    arrays, t = {}, {}

    def give(name, a):
        a = np.ascontiguousarray(a)
        arrays[name] = a
        t[name] = nc.dram_tensor(name, a.shape, mybir.dt.from_np(a.dtype), kind="ExternalInput").ap()

    for name in _INS:
        give(name, inputs[name])
    _, t_p, d = inputs["x_prompt"].shape
    b_s, t_s, _ = inputs["x_sample"].shape
    depth, n_phys, page, g, hd = inputs["cache_k"].shape
    idd = inputs["cache_idx_k"].shape[-1]
    past = inputs["page_table"].shape[1] * page
    nbk, h = inputs["rel_bias"].shape
    poolw, state = inputs["pool_scale"].shape[1], inputs["state_pool"].shape[2]

    f32, p = np.float32, P
    give("c_ident", np.eye(p, dtype=f32))
    rows = np.arange(p)[:, None]
    causal = np.concatenate([np.arange(p)[None] > rows, np.arange(t_p)[None] > rows + p], axis=1)
    give("c_causal", np.where(causal, f32(NEG), f32(0)))
    give("c_causal_s", np.where(np.arange(t_s)[None] > (np.arange(b_s * t_s) % t_s)[:, None], f32(NEG), f32(0)))
    dist = np.maximum(past + t_s - 1 - np.arange(past + t_s + p), 0)
    exact = nbk // 2
    far = exact + (np.log(np.maximum(dist, 1).astype(f32) / f32(exact)) / f32(math.log(128 / exact))
                   * f32(nbk - exact)).astype(np.int32)
    bucket = np.where(dist < exact, dist, np.minimum(far, nbk - 1))
    give("c_onehot", (np.arange(nbk)[:, None] == bucket[None]).astype(f32))
    pos = np.arange(state + 1)
    count = np.stack([1.0 / np.minimum(pos + 1, w) for w in (2, 4, 8, 16)]).astype(f32)
    give("c_count", np.broadcast_to(count[None], (p,) + count.shape))
    k, m = np.arange(p)[None, :, None], np.arange(p)[None, None, :]
    pick = (k == np.arange(b_s)[:, None, None] * t_s + m % t_s)
    give("c_pick", pick.astype(ml_dtypes.bfloat16))

    shapes = [(1, t_p, d), (b_s, t_s, d), (depth, 1, t_p, g, hd), (depth, 1, t_p, g, hd), (depth, 1, t_p, idd),
              (depth, 1, state, poolw), (depth, b_s, t_s, g, hd), (depth, b_s, t_s, g, hd), (depth, b_s, t_s, idd),
              (depth, b_s, state, poolw)]
    out = [nc.dram_tensor(f"out_{i}", s, F32, kind="ExternalOutput").ap() for i, s in enumerate(shapes)]
    hybrid_layer(nc, t, out)
    r = _run(nc, [arrays], core_ids=[0])
    return tuple(r.results[0][f"out_{i}"] for i in range(len(shapes)))
```

```python
from contextlib import ExitStack

import numpy as np
import concourse.bass as bass
from concourse import mybir

F32 = mybir.dt.float32
F32R = mybir.dt.float32r
BF16 = mybir.dt.bfloat16
I32 = mybir.dt.int32
ALU = mybir.AluOpType
ACT = mybir.ActivationFunctionType
AX = mybir.AxisListType
ds = bass.ds

P = 128
SLOTS = 4
KK = 4
AHEAD_SPLIT = 3
AHEAD_LOAD = 7
NEG = -1e30
TAKEN = -3e38
TAKEN_EDGE = -2e38


def hybrid_layer(nc, t, out):
    _, T_P, D = t["x_prompt"].shape
    NB_S, T_S, _ = t["x_sample"].shape
    N_PHYS, PAGE, G, HD = t["cache_k"].shape[1:]
    PAGES = t["page_table"].shape[1]
    PAST = PAGES * PAGE
    NBK, H = t["rel_bias"].shape
    POOLW = t["pool_scale"].shape[1]
    STATE = t["state_pool"].shape[2]
    NG = t["w_pool"].shape[1]
    ID = t["cache_idx_k"].shape[-1]
    AW, KVW = H * HD, G * HD
    IH = (t["w_in"].shape[2] - 2 * AW - 2 * KVW - ID - 2 * POOLW) // (ID + 1)
    R = H // G
    N_S = NB_S * T_S
    N = T_P + N_S
    TT = [(0, P), (P, P), (T_P, N_S)]
    KT = D // P
    CH = KT // KK
    QC = 2 * CH
    LS = PAST + T_S
    TOPK_P, TOPK_S = min(256, T_P // 4), min(256, LS // 4)
    SCALE = float(HD) ** -0.5
    W_SCALE = float(ID * IH) ** -0.5
    EPS = 1e-6
    TQ = T_S * IH
    L2 = P + T_P
    NEG_AT = PAST + T_S - 1
    VEC = NEG_AT + P + 1
    WINS = (2, 4, 8, 16)
    UW = STATE + T_P + NB_S * (STATE + T_S)
    assert T_P == 2 * P and HD == P and ID == P and PAGE == P and R * T_S == 32 and CH == 8

    C_Q, C_K = 0, AW
    C_GA = AW + 2 * KVW
    C_QI = C_GA + AW
    C_WI = C_QI + IH * ID
    C_KI = C_WI + IH
    C_U = C_KI + ID
    C_GB = C_U + POOLW
    W0 = IH + ID
    T_Q, T_K, T_V, T_GA = 0, AW // P, (AW + KVW) // P, C_GA // P
    T_QI = C_QI // P
    T_U = C_WI // P
    T_GB = T_U + POOLW // P
    N_TILES = T_GB + POOLW // P

    segs, chunk0, quad0 = {}, CH, 0
    for name, w, col, width, tile0 in (
            ("qi", "w_in", C_QI, IH * ID, T_QI), ("q", "w_in", C_Q, AW, T_Q), ("kv", "w_in", C_K, 2 * KVW, T_K),
            ("u", "w_in", C_U, POOLW, T_U), ("gb", "w_in", C_GB, POOLW, T_GB), ("ga", "w_in", C_GA, AW, T_GA),
            ("out", "w_out", 0, D, 0)):
        n = width // (4 * P)
        segs[name] = (w, col, n, chunk0, quad0, tile0)
        chunk0 += n * QC
        quad0 += n
    order = list(segs)
    CHUNKS = chunk0

    w_rows = {n: t[n][0].rearrange("(k p) n -> p k n", p=P) for n in ("w_in", "w_out")}

    def dram(name, shape):
        return nc.dram_tensor(name, shape, F32).ap()

    projT = dram("projT", (N_TILES, P, N))
    oT = dram("oT", (H, P, N))
    poolT = dram("poolT", (POOLW // P, P, N))
    mixT = dram("mixT", (POOLW // P, P, N))
    wsc = dram("wsc", (1, N_S * IH))
    scores = dram("scores", (N_S, LS))
    BIAS_W = T_P + P
    biasP = dram("biasP", (H, P * BIAS_W))
    biasS = dram("biasS", (H, T_S * (LS + T_S)))

    def tile_rows(ap, i):
        return ap[ds(i, 1)].rearrange("a p n -> (a p) n")

    def tiles(ap, i, n):
        return ap[ds(i, n)].rearrange("a p n -> p a n")

    root = ExitStack()
    with root:
        names = set()

        def sem(name):
            assert name not in names
            names.add(name)
            return root.enter_context(nc.semaphore(name))

        def sb(name, shape, dt=F32, ctx=root):
            return ctx.enter_context(nc.sbuf_tensor(name, shape, dt))

        bank = [root.enter_context(nc.psum_tensor(f"bank{i}", [P, 512], F32)) for i in range(4)]
        wide = root.enter_context(nc.psum_tensor("wide", [P, 4 * 512], F32))
        sbank = [wide[:, 512 * i:512 * i + 512] for i in range(4)]

        XH = sb("XH", [P, KT, N], F32R)
        XL = sb("XL", [P, KT, N], F32R)
        raw = sb("raw", [P, SLOTS, KK, 2 * P])
        hi = sb("hi", [P, SLOTS, KK, 2 * P], F32R)
        lo = sb("lo", [P, SLOTS, KK, 2 * P], F32R)
        stg = [sb(f"stg{i}", [P, 2, N]) for i in range(2)]
        ident = sb("ident", [P, P])
        identb = sb("identb", [P, P], BF16)
        gT = sb("gT", [P, KT])
        poolscT = sb("poolscT", [P, POOLW // P])
        rstdB = sb("rstdB", [P, N])
        kiT = sb("kiT", [P, N])
        wN = sb("wN", [P, 3, IH])
        ptab = sb("ptab", [1, NB_S * PAGES], I32)
        keep = sb("keep", [P, G * N + (LS + 1) // 2 + L2 + L2 // 2 + 3 * KVW + POOLW // P * NB_S * STATE])
        at = [0]

        def cut(n, dt=F32, back=None):
            if back is not None:
                at[0] = back
            ap = keep[:, at[0]:at[0] + n]
            at[0] += n
            return ap if dt == F32 else ap.bitcast(dt)

        kT = cut(G * N).rearrange("p (g n) -> p g n", g=G)
        maskS = cut((LS + 1) // 2, BF16)
        era = at[0]
        scP = cut(L2)
        maskP = cut(L2 // 2, BF16)
        vN = cut(3 * KVW).rearrange("p (a n) -> p a n", a=3)
        stT = cut(POOLW // P * NB_S * STATE).rearrange("p (a n) -> p a n", a=POOLW // P)
        qS = cut(H * N_S, back=era).rearrange("p (h n) -> p h n", h=H)

        stood = {e: sem(f"stood_{e}") for e in ("Pool", "DVE", "SP", "PE")}

        def alone(eng):
            eng.sem_inc(stood[eng.engine.name], 1)

        raw_in = [sem(f"raw_in{i}") for i in range(SLOTS)]
        hi_ready, lo_ready, chunk_used = sem("hi_ready"), sem("lo_ready"), sem("chunk_used")
        evac = [sem("evac0"), sem("evac1")]
        stored = [sem("stored0"), sem("stored1")]

        def load_chunk(sp, c, slot, src, width, guard=True):
            if guard:
                sp.wait_ge(lo_ready, c - (SLOTS - 1))
                alone(sp)
            sp.dma_start(raw[:, slot, :, 0:width], src).then_inc(raw_in[slot], 16)

        def chunk_src(name, q, j):
            w, col = segs[name][:2]
            return w_rows[w][:, KK * (j % CH) if name != "out" else (KK * (j % CH) + KT // 2) % KT:, :][
                :, 0:KK, ds(q * (4 * P) + (col + (j // CH) * 2 * P), 2 * P)]

        def load_segment(sp, name):
            _, _, n, c0, _, _ = segs[name]
            nxt = order[order.index(name) + 1] if name != "out" else None

            def quad(q, last):
                for j in range(QC):
                    k = j + AHEAD_LOAD
                    if k < QC:
                        src = chunk_src(name, q, k)
                    elif not last:
                        src = chunk_src(name, q + 1, k - QC)
                    elif nxt:
                        src = chunk_src(nxt, 0, k - QC)
                    else:
                        continue
                    load_chunk(sp, q * QC + (c0 + k), (c0 + k) % SLOTS, src, 2 * P)
            with sp.Fori(0, n - 1) as q:
                quad(q, False)
            quad(n - 1, True)

        def hi_chunk(act, c, slot, uses, width=2 * P, guard=True):
            act.wait_ge(raw_in[slot], uses)
            if guard:
                act.wait_ge(chunk_used, c - (SLOTS - 1))
            nc.scalar.activation(hi[:, slot, :, 0:width], raw[:, slot, :, 0:width], ACT.Copy).then_inc(hi_ready, 1)

        def lo_chunk(dve, c, slot, width=2 * P):
            dve.wait_ge(hi_ready, c + 1)
            nc.vector.tensor_tensor(lo[:, slot, :, 0:width], raw[:, slot, :, 0:width],
                                    hi[:, slot, :, 0:width].bitcast(F32), ALU.subtract).then_inc(lo_ready, 1)

        def products(pe, c, slot, j, banks, cols, rot=0):
            pe.wait_ge(lo_ready, c + 1)
            for kk in range(KK):
                k = (KK * j + kk + rot) % KT
                for n in range(2):
                    wh, wl = (w[:, slot, kk, cols[n]:cols[n] + P] for w in (hi, lo))
                    first, last = j == 0 and kk == 0, j == CH - 1 and kk == KK - 1
                    nc.tensor.matmul(bank[banks[n]][:, 0:N], wh, XH[:, k, :], start=first, stop=False)
                    nc.tensor.matmul(bank[banks[n]][:, 0:N], wh, XL[:, k, :], start=False, stop=False)
                    mm = nc.tensor.matmul(bank[banks[n]][:, 0:N], wl, XH[:, k, :], start=False, stop=last)
            mm.then_inc(chunk_used, 1)

        def pe_quad(pe, name, q, weave=None, before=None):
            _, _, _, c0, quad0, _ = segs[name]
            rot = KT // 2 if name == "out" else 0
            for j in range(QC):
                half = j // CH
                if j % CH == 0:
                    pe.wait_ge(evac[half], q + (quad0 + half))
                if before:
                    before(pe, j)
                products(pe, q * QC + (c0 + j), (c0 + j) % SLOTS, j % CH, (2 * half, 2 * half + 1), (0, P), rot)
                if weave:
                    weave(pe, q, j)

        def pe_segment(pe, name, weave=None):
            with pe.Fori(0, segs[name][2]) as q:
                pe_quad(pe, name, q, weave)

        def act_quad(act, name, q, weave=None, last=False, turned=None, gate=None):
            _, _, _, c0, quad0, tile0 = segs[name]
            for j in range(QC):
                k = j + AHEAD_SPLIT
                half = j // CH
                if not (last and k >= QC):
                    hi_chunk(act, q * QC + (c0 + k), (c0 + k) % SLOTS,
                             q * (QC // SLOTS * 16) + 16 * ((c0 + k) // SLOTS + 1))
                if j % CH == CH - 1 and turned is None:
                    act.wait_ge(evac[half], q + (quad0 + half + 1))
                    if gate:
                        ex, exped, _ = gate
                        nc.scalar.activation(ex, stg[half][:], ACT.Exp, scale=-1.0).then_inc(exped, 1)
                    else:
                        act.dma_start(tiles(projT, q * 4 + (tile0 + 2 * half), 2), stg[half][:]).then_inc(stored[half], 16)
                if weave:
                    weave(act, q, j)
                if gate and j % CH == CH - 1:
                    act.wait_ge(gate[2], q * 6 + (3 * half + 3))
                    act.dma_start(tiles(projT, q * 4 + (tile0 + 2 * half), 2), stg[half][:]).then_inc(stored[half], 16)

        def act_segment(act, name, weave=None, gate=None):
            with act.Fori(0, segs[name][2]) as q:
                act_quad(act, name, q, weave, gate=gate)

        def dve_quad(dve, name, q, weave=None, last=False, turned=None, gate=None):
            _, _, _, c0, quad0, _ = segs[name]
            for j in range(QC):
                k = j + AHEAD_SPLIT
                if not (last and k >= QC):
                    lo_chunk(dve, q * QC + (c0 + k), (c0 + k) % SLOTS)
                if j % CH == CH - 1:
                    half = j // CH
                    dve.wait_ge(chunk_used, q * QC + (c0 + j + 1))
                    if turned is None:
                        dve.wait_ge(stored[half], q * 16 + 16 * quad0)
                    else:
                        dve.wait_ge(stored[half], 16 * quad0)
                        dve.wait_ge(turned, q)
                    for n_ in range(2):
                        sums = bank[2 * half + n_][:, 0:N]
                        if turned is None:
                            copy = nc.vector.tensor_tensor(stg[half][:, n_, :], sums, rstdB[:], ALU.mult)
                        else:
                            copy = nc.vector.tensor_copy(stg[half][:, n_, :], sums)
                    copy.then_inc(evac[half], 1)
                if gate and j % CH == CH - 1:
                    ex, exped, gated = gate
                    n = q * 6 + 3 * half
                    dve.wait_ge(exped, q * 2 + (half + 1))
                    nc.vector.tensor_scalar(ex, ex, 1.0, None, ALU.add).then_inc(gated, 1)
                    dve.wait_ge(gated, n + 1)
                    nc.vector.reciprocal(ex, ex).then_inc(gated, 1)
                    dve.wait_ge(gated, n + 2)
                    nc.vector.tensor_tensor(stg[half][:], stg[half][:], ex, ALU.mult).then_inc(gated, 1)
                if weave:
                    weave(dve, q, j)

        def dve_segment(dve, name, weave=None, gate=None):
            with dve.Fori(0, segs[name][2]) as q:
                dve_quad(dve, name, q, weave, gate=gate)

        def all_stored(eng, name):
            for half in range(2):
                eng.wait_ge(stored[half], 16 * (segs[name][4] + segs[name][2]))

        with ExitStack() as ph:
            xN = [sb(f"xN{i}", [P, D], ctx=ph) for i in range(3)]
            ssq = sb("ssq", [P, 3], ctx=ph)
            var = sb("var", [P, 3], ctx=ph)
            rstd = sb("rstd", [P, 3], ctx=ph)
            root_ = sb("root_", [P, 3], ctx=ph)
            newt = sb("newt", [P, 3], ctx=ph)
            onehot = keep[0:NBK, D:D + VEC]
            relb = sb("relb", [NBK, H], ctx=ph)
            bvec = sb("bvec", [H, VEC], ctx=ph)
            s_step, s_bias = sem("s_step"), sem("s_bias")
            gN = sb("gN", [KT, P], ctx=ph)
            pscN = sb("pscN", [POOLW // P, P], ctx=ph)
            wiT = sb("wiT", [IH, N], ctx=ph)
            kiN = keep[:, 0:3 * P].rearrange("p (a n) -> p a n", a=3)
            ones = keep[:, D + VEC:D + VEC + P]
            diag = keep[:, D + VEC + P:D + VEC + 4 * P].rearrange("p (a n) -> p a n", a=3)
            XPARTS = 4
            XW = D // XPARTS
            s_x = [sem(f"s_x{i}") for i in range(XPARTS)]
            s_small, s_sq, s_root, s_rstd = (sem(n) for n in ("s_small", "s_sq", "s_root", "s_rstd"))
            s_gT, s_gcopy, s_xT, s_xh, s_xl = (sem(n) for n in ("s_gT", "s_gcopy", "s_xT", "s_xh", "s_xl"))
            s_diag, s_rb = sem("s_diag"), sem("s_rb")
            s_kin, s_kinc, s_bvec, s_bvecc, s_outA, s_identb = (sem(n) for n in (
                "s_kin", "s_kinc", "s_bvec", "s_bvecc", "s_outA", "s_identb"))
            s_onehot = sem("s_onehot")
            SQUARES = range(3, 6)
            block = ph.enter_context(nc.Block())

            @block.sync
            def _(sp):
                sp.dma_start(ident[:], t["c_ident"]).then_inc(s_small, 16)
                sp.dma_start(gN[:], t["ln_g"][0].rearrange("(k p) -> k p", p=P)).then_inc(s_small, 16)
                sp.dma_start(pscN[:], t["pool_scale"][0].rearrange("(k p) -> k p", p=P)).then_inc(s_small, 16)
                sp.dma_start(relb[:], t["rel_bias"]).then_inc(s_onehot, 16)
                sp.dma_start(onehot, t["c_onehot"]).then_inc(s_onehot, 16)
                sp.wait_ge(s_x[0], 48)
                for c in range(AHEAD_LOAD):
                    load_chunk(sp, c, c % SLOTS, w_rows["w_in"][:, KK * c:KK * c + KK, C_WI:C_WI + W0], W0, c >= SLOTS)
                for c in range(AHEAD_LOAD, AHEAD_LOAD + CH):
                    if c < CH:
                        load_chunk(sp, c, c % SLOTS, w_rows["w_in"][:, KK * c:KK * c + KK, C_WI:C_WI + W0], W0)
                    else:
                        load_chunk(sp, c, c % SLOTS, chunk_src("qi", 0, c - CH), 2 * P)
                load_segment(sp, "qi")

            @block.gpsimd
            def _(pool):
                pool.dma_start(ptab[:], t["page_table"].rearrange("(o b) p -> o (b p)", o=1)).then_inc(s_outA, 16)
                pool.wait_ge(s_kinc, 1)
                pool.dma_start(out[4][0, 0].rearrange("(a p) d -> p a d", p=P), kiN[:, 0:2, :]).then_inc(s_outA, 16)
                pool.dma_start(out[8][0].rearrange("b s d -> (b s) d"), kiN[0:N_S, 2, :]).then_inc(s_outA, 16)
                pool.dma_start(wsc.rearrange("o (p h) -> (o p) h", h=IH), wN[0:N_S, 2, :]).then_inc(s_outA, 16)
                pool.wait_ge(s_bvecc, 1)
                pool.dma_start(biasP.rearrange("h (c n) -> h c n", n=BIAS_W),
                               bvec[:, VEC - BIAS_W:VEC].unsqueeze(1).to_broadcast([H, P, BIAS_W])).then_inc(s_bias, 16)
                pool.dma_start(biasS.rearrange("h (c n) -> h c n", n=LS + T_S),
                               bvec[:, 0:LS + T_S].unsqueeze(1).to_broadcast([H, T_S, LS + T_S])).then_inc(s_bias, 16)
                pool.wait_ge(s_bias, 32)
                pool.wait_ge(s_outA, 64)

            @block.scalar
            def _(act):
                rows = [t["x_prompt"][0, 0:P], t["x_prompt"][0, P:T_P], t["x_sample"].rearrange("b s d -> (b s) d")]
                for part in range(XPARTS):
                    for i in range(3):
                        cols = slice(part * XW, (part + 1) * XW)
                        act.dma_start(xN[i][0:TT[i][1], cols], rows[i][:, cols]).then_inc(s_x[part], 16)
                for c in range(AHEAD_SPLIT):
                    hi_chunk(act, c, c, 16, W0, False)
                act.wait_ge(s_gcopy, 1)
                for c in range(CH):
                    for k in range(KK * c, KK * c + KK):
                        act.wait_ge(s_xT, k + 1)
                        nc.scalar.activation(XH[:, k, :], sbank[k % 4][:, 0:N], ACT.Copy,
                                             scale=gT[:, k:k + 1]).then_inc(s_xh, 1)
                    a = c + AHEAD_SPLIT
                    hi_chunk(act, a, a % SLOTS, 16 * (a // SLOTS + 1), W0 if a < CH else 2 * P, a >= SLOTS)
                    if c in SQUARES:
                        i = c - SQUARES[0]
                        r = TT[i][1]
                        for part in range(XPARTS):
                            act.wait_ge(s_x[part], 48)
                        act.wait_ge(s_step, 1)
                        if i:
                            act.wait_ge(s_sq, i)
                        nc.scalar.activation(keep[0:r, 0:D], xN[i][0:r, :], ACT.Square,
                                             accum_out=ssq[0:r, i:i + 1]).then_inc(s_sq, 1)
                    if c == SQUARES[-1] + 1:
                        act.wait_ge(s_step, 2)
                        nc.scalar.activation(root_[:], var[:], ACT.Sqrt).then_inc(s_root, 1)
                act_segment(act, "qi")

            @block.vector
            def _(dve):
                nc.vector.memset(ssq[:], 1.0).then_inc(s_step, 1)
                dve.wait_ge(s_bvec, 1)
                nc.vector.tensor_copy(bvec[:], wide[0:H, 512:512 + VEC]).then_inc(s_bvecc, 1)
                nc.vector.memset(ones, 1.0)
                for c in range(AHEAD_SPLIT):
                    lo_chunk(dve, c, c, W0)
                dve.wait_ge(s_gT, 1)
                nc.vector.tensor_copy(gT[:], sbank[0][:, 0:KT])
                nc.vector.tensor_copy(identb[:], ident[:])
                nc.vector.tensor_copy(poolscT[:], sbank[0][:, KT:KT + POOLW // P]).then_inc(s_gcopy, 1)
                dve.wait_ge(s_gcopy, 1)
                for c in range(CH):
                    for k in range(KK * c, KK * c + KK):
                        dve.wait_ge(s_xh, k + 1)
                        nc.vector.scalar_tensor_tensor(XL[:, k, :], sbank[k % 4][:, 0:N], gT[:, k:k + 1],
                                                       XH[:, k, :].bitcast(F32), ALU.mult, ALU.subtract).then_inc(s_xl, 1)
                    a = c + AHEAD_SPLIT
                    lo_chunk(dve, a, a % SLOTS, W0 if a < CH else 2 * P)
                    if c == SQUARES[-1]:
                        dve.wait_ge(s_sq, 3)
                        nc.vector.tensor_scalar(var[:], ssq[:], 1.0 / D, EPS, ALU.mult, ALU.add).then_inc(s_step, 1)
                    if c == SQUARES[-1] + 1:
                        dve.wait_ge(s_root, 1)
                        nc.vector.reciprocal(root_[:], root_[:]).then_inc(s_step, 1)
                        dve.wait_ge(s_step, 3)
                        nc.vector.tensor_tensor(newt[:], root_[:], root_[:], ALU.mult).then_inc(s_step, 1)
                        dve.wait_ge(s_step, 4)
                        nc.vector.tensor_tensor(newt[:], newt[:], var[:], ALU.mult).then_inc(s_step, 1)
                        dve.wait_ge(s_step, 5)
                        nc.vector.tensor_scalar(newt[:], newt[:], -0.5, 1.5, ALU.mult, ALU.add).then_inc(s_step, 1)
                        dve.wait_ge(s_step, 6)
                        nc.vector.tensor_tensor(rstd[:], root_[:], newt[:], ALU.mult).then_inc(s_rstd, 1)
                        dve.wait_ge(s_rstd, 1)
                        for i, (_, r) in enumerate(TT):
                            ins = nc.vector.tensor_scalar(diag[0:r, i, 0:r], ident[0:r, 0:r], rstd[0:r, i:i + 1], None, ALU.mult)
                        ins.then_inc(s_diag, 1)
                dve.wait_ge(s_rb, 1)
                nc.vector.tensor_copy(rstdB[:], sbank[0][:, 0:N]).then_inc(s_rstd, 1)
                dve.wait_ge(s_rstd, 2)
                dve.wait_ge(chunk_used, CH)
                nc.vector.scalar_tensor_tensor(wiT[:], bank[2][0:IH, 0:N], W_SCALE, rstdB[0:IH, :], ALU.mult, ALU.mult)
                nc.vector.tensor_tensor(kiT[:], bank[3][:, 0:N], rstdB[:], ALU.mult).then_inc(evac[1], 1)
                dve.wait_ge(s_kin, 1)
                nc.vector.tensor_copy(wN[:, 0:2, :], sbank[0][:, 0:2 * IH].rearrange("p (a h) -> p a h", a=2))
                nc.vector.tensor_copy(wN[0:N_S, 2, :], sbank[0][0:N_S, 2 * IH:3 * IH])
                nc.vector.tensor_copy(kiN[:, 0:2, :], sbank[1][:, 0:2 * P].rearrange("p (a h) -> p a h", a=2))
                nc.vector.tensor_copy(kiN[0:N_S, 2, :], sbank[1][0:N_S, 2 * P:3 * P]).then_inc(s_kinc, 1)
                dve_segment(dve, "qi")

            @block.tensor
            def _(pe):
                pe.wait_ge(s_onehot, 32)
                for c in range(0, VEC, 512):
                    z = min(VEC, c + 512)
                    mm = nc.tensor.matmul(wide[0:H, 512 + c:512 + z], relb[:], onehot[:, c:z], start=True, stop=True)
                mm.then_inc(s_bvec, 1)
                pe.wait_ge(s_small, 48)
                nc.tensor.transpose(sbank[0][:, 0:KT], gN[:], ident[0:KT, 0:KT])
                nc.tensor.transpose(sbank[0][:, KT:KT + POOLW // P], pscN[:],
                                    ident[0:POOLW // P, 0:POOLW // P]).then_inc(s_gT, 1)
                pe.wait_ge(s_gcopy, 1)
                pe.wait_ge(s_bvecc, 1)

                def turn_tokens(c):
                    for k in range(KK * c, KK * c + KK):
                        pe.wait_ge(s_x[k * P // XW], 48)
                        if k >= 4:
                            pe.wait_ge(s_xl, k - 3)
                        for i, (c0, r) in enumerate(TT):
                            tr = nc.tensor.transpose(sbank[k % 4][:, c0:c0 + r], xN[i][0:r, k * P:k * P + P],
                                                     ident[0:r, 0:r])
                        tr.then_inc(s_xT, 1)

                turn_tokens(0)
                for c in range(CH):
                    if c + 1 < CH:
                        turn_tokens(c + 1)
                    else:
                        pe.wait_ge(s_diag, 1)
                        pe.wait_ge(s_xl, KT - 3)
                        for i, (c0, r) in enumerate(TT):
                            mm = nc.tensor.matmul(sbank[0][:, c0:c0 + r], ones[0:r, :], diag[0:r, i, 0:r], start=True, stop=True)
                        mm.then_inc(s_rb, 1)
                    pe.wait_ge(s_xl, KK * (c + 1))
                    products(pe, c, c % SLOTS, c, (2, 3), (0, IH))
                pe.wait_ge(evac[1], 1)
                for i, (c0, r) in enumerate(TT):
                    nc.tensor.transpose(sbank[0][0:r, i * IH:(i + 1) * IH], wiT[:, c0:c0 + r], ident[0:IH, 0:IH])
                for i, (c0, r) in enumerate(TT):
                    tr = nc.tensor.transpose(sbank[1][0:r, i * P:(i + 1) * P], kiT[:, c0:c0 + r], ident[:])
                tr.then_inc(s_kin, 1)
                pe_segment(pe, "qi")

        HQ = IH // segs["q"][2]
        BQ = NB_S // segs["q"][2]
        with ExitStack() as ph:
            qiH = [sb(f"qiH{i}", [P, HQ // 2, T_P], ctx=ph) for i in range(2)]
            qiS = sb("qiS", [P, IH, N_S], ctx=ph)
            wbc = sb("wbc", [P, N_S * IH], ctx=ph)
            ipg = sb("ipg", [P, PAGES, ID], ctx=ph)
            ikT = sb("ikT", [P, LS], ctx=ph)
            prod = sb("prod", [P, 2, TQ], ctx=ph)
            scT = sb("scT", [P, PAGES + 1, T_S], ctx=ph)
            sc8 = sb("sc8", [T_S, LS], ctx=ph)
            relu = sb("relu", [P, L2], ctx=ph)
            s_qiH = [sem("s_qiH0"), sem("s_qiH1")]
            (s_qiS, s_wbc, p_scored, p_relu, p_sum, s_ipg, s_itr, s_ikA, s_ikD, s_iks, s_sc, s_prod, s_red,
             s_bt, s_sc8, s_scst, s_zero) = (sem(n) for n in (
                 "s_qiS", "s_wbc", "p_scored", "p_relu", "p_sum", "s_ipg", "s_itr", "s_ikA", "s_ikD", "s_iks",
                 "s_sc", "s_prod", "s_red", "s_bt", "s_sc8", "s_scst", "s_zero"))
            block = ph.enter_context(nc.Block())
            PAIRS = [(p, min(2, PAGES - p)) for p in range(0, PAGES, 2)] + [(PAGES, 1)]
            NPAIR = len(PAIRS)

            @block.sync
            def _(sp):
                load_segment(sp, "q")

            @block.gpsimd
            def _(pool):
                def index_pages(b):
                    pool.wait_ge(s_itr, b)
                    alone(pool)
                    for p in range(PAGES):
                        page = pool.value_load(ptab[0:1, ds(b * PAGES + p, 1)], min_val=0, max_val=N_PHYS - 1)
                        pool.dma_start(ipg[:, p, :], tile_rows(t["cache_idx_k"][0], page)).then_inc(s_ipg, 16)

                def store_scores(b):
                    pool.wait_ge(s_sc8, b + 1)
                    alone(pool)
                    pool.dma_start(scores[ds(b * T_S, T_S), :], sc8[:]).then_inc(s_scst, 16)

                def quad(q, more):
                    index_pages(q * BQ + 1)
                    if more:
                        pool.wait_ge(p_scored, q * HQ + HQ // 2)
                        alone(pool)
                        load_heads(q + 1, 0)
                    store_scores(q * BQ)
                    if more:
                        index_pages(q * BQ + 2)
                        pool.wait_ge(p_scored, q * HQ + HQ)
                        alone(pool)
                        load_heads(q + 1, 1)
                    store_scores(q * BQ + 1)

                def load_heads(q, i):
                    pool.dma_start(qiH[i][:], projT[ds(q * HQ + (T_QI + i * (HQ // 2)), HQ // 2), :, 0:T_P].rearrange(
                        "h p n -> p h n")).then_inc(s_qiH[i], 16)

                all_stored(pool, "qi")
                load_heads(0, 0)
                index_pages(0)
                pool.dma_start(qiS[:], projT[T_QI:T_QI + IH, :, T_P:N].rearrange("h p n -> p h n")).then_inc(s_qiS, 16)
                pool.dma_start(wbc[:], wsc.to_broadcast([P, N_S * IH])).then_inc(s_wbc, 16)
                load_heads(0, 1)
                NQ = segs["q"][2]
                with pool.Fori(0, NQ - 1) as q:
                    quad(q, True)
                quad(NQ - 1, False)
                pool.wait_ge(s_scst, 16 * NB_S)

            def pe_weave(pe, q, j):
                if j % 2 == 1:
                    h = j // 2
                    part = h // (HQ // 2)
                    if h % (HQ // 2) == 0:
                        pe.wait_ge(s_qiH[part], q * 16 + 16)
                    pe.wait_ge(p_relu, q * HQ + h)
                    nc.tensor.matmul(sbank[0][:, 0:P], qiH[part][:, h % (HQ // 2), 0:P], kiT[:, 0:P], start=True, stop=True)
                    nc.tensor.matmul(sbank[0][:, P:L2], qiH[part][:, h % (HQ // 2), P:T_P], kiT[:, 0:T_P], start=True,
                                     stop=True).then_inc(p_scored, 1)
                u, s = j // 8, j % 8
                b = q * BQ + u
                if s == 1:
                    pe.wait_ge(s_ipg, b * (16 * PAGES) + 16 * PAGES)
                    pe.wait_ge(s_sc8, b)
                    for p in range(PAGES):
                        tr = nc.tensor.transpose(sbank[1 + p // 4][:, (p % 4) * P:(p % 4 + 1) * P], ipg[:, p, :], ident[:])
                    tr.then_inc(s_itr, 1)
                for i, (p, n) in enumerate(PAIRS):
                    if s != 3 + i // 2:
                        continue
                    if i == 0:
                        pe.wait_ge(s_ikA, b + 1)
                        pe.wait_ge(s_iks, b + 1)
                    if i >= 2:
                        pe.wait_ge(s_prod, b * NPAIR + (i - 1))
                    pe.wait_ge(s_qiS, 16)
                    alone(pe)
                    for m in range(n):
                        cols = P if p < PAGES else T_S
                        mm = nc.tensor.matmul(sbank[1 + i % 2][0:cols, m * TQ:(m + 1) * TQ],
                                              ikT[:, (p + m) * P:(p + m) * P + cols],
                                              qiS[:, :, ds(b * T_S, T_S)].rearrange("p h t -> p t h"),
                                              start=True, stop=True)
                    mm.then_inc(s_sc, 1)
                if s == 7:
                    pe.wait_ge(s_red, b * NPAIR + NPAIR)
                    for p in range(PAGES):
                        nc.tensor.transpose(wide[0:T_S, 512 + p * P:512 + (p + 1) * P], scT[:, p, :], ident[:])
                    nc.tensor.transpose(wide[0:T_S, 512 + PAST:512 + LS], scT[0:T_S, PAGES, :],
                                        ident[0:T_S, 0:T_S]).then_inc(s_bt, 1)

            def act_weave(act, q, j):
                if j % 2 == 1:
                    h = j // 2
                    act.wait_ge(p_scored, q * HQ + (h + 1))
                    act.wait_ge(p_sum, q * HQ + h)
                    nc.scalar.activation(relu[:], sbank[0][:, 0:L2], ACT.Relu).then_inc(p_relu, 1)
                u, s = j // 8, j % 8
                b = q * BQ + u
                if s == 1:
                    act.wait_ge(s_itr, b + 1)
                    act.wait_ge(s_sc, b * NPAIR)
                    nc.scalar.activation(ikT[:, 0:PAST], wide[:, 512:512 + PAST], ACT.Copy).then_inc(s_ikA, 1)

            def dve_weave(dve, q, j):
                u, s = j // 8, j % 8
                b = q * BQ + u
                if s == 1:
                    dve.wait_ge(s_sc, b * NPAIR)
                    nc.vector.tensor_copy(ikT[:, PAST:LS], kiT[:, ds(b * T_S + T_P, T_S)]).then_inc(s_iks, 1)
                if j % 2 == 1:
                    h = q * HQ + j // 2
                    dve.wait_ge(p_relu, h + 1)
                    dve.wait_ge(p_sum, h)
                    for i, (a, z) in enumerate(((0, P), (P, L2))):
                        ins = nc.vector.scalar_tensor_tensor(scP[:, a:z], relu[:, a:z], wN[:, i, ds(h, 1)], scP[:, a:z],
                                                             ALU.mult, ALU.add)
                    ins.then_inc(p_sum, 1)
                for i, (p, n) in enumerate(PAIRS):
                    if s != 3 + i // 2:
                        continue
                    cols = P if p < PAGES else T_S
                    dve.wait_ge(s_sc, b * NPAIR + (i + 1))
                    dve.wait_ge(s_red, b * NPAIR + i)
                    if i == 0:
                        dve.wait_ge(s_wbc, 16)
                        dve.wait_ge(s_bt, b)
                    nc.vector.scalar_tensor_tensor(
                        prod[0:cols, 0:n, :], sbank[1 + i % 2][0:cols, 0:n * TQ].rearrange("p (a c) -> p a c", a=n), 0.0,
                        wbc[0:cols, ds(b * TQ, TQ)].unsqueeze(1).to_broadcast([cols, n, TQ]),
                        ALU.max, ALU.mult).then_inc(s_prod, 1)
                    dve.wait_ge(s_prod, b * NPAIR + (i + 1))
                    nc.vector.tensor_reduce(scT[0:cols, p:p + n, :].rearrange("p a t -> p (a t)"),
                                            prod[0:cols, 0:n, :].rearrange("p a (t h) -> p (a t) h", h=IH),
                                            AX.X, ALU.add).then_inc(s_red, 1)
                if s == 7:
                    dve.wait_ge(s_bt, b + 1)
                    dve.wait_ge(s_scst, b * 16)
                    nc.vector.tensor_copy(sc8[:], wide[0:T_S, 512:512 + LS]).then_inc(s_sc8, 1)

            @block.scalar
            def _(act):
                act.wait_ge(s_zero, 1)
                act_segment(act, "q", act_weave)

            @block.vector
            def _(dve):
                nc.vector.memset(scP, 0.0).then_inc(s_zero, 1)
                dve.wait_ge(s_zero, 1)
                dve_segment(dve, "q", dve_weave)

            @block.tensor
            def _(pe):
                pe_segment(pe, "q", pe_weave)

        with ExitStack() as ph:
            vT = sb("vT", [P, G, N], ctx=ph)
            kN = sb("kN", [P, 3, KVW], ctx=ph)
            negP = sb("negP", [P, L2], ctx=ph)
            top8 = sb("top8", [P, 2, 8], ctx=ph)
            keepP = sb("keepP", [P, L2], ctx=ph)
            stN = sb("stN", [NB_S * STATE, POOLW], ctx=ph)
            s_cin, t_step, s_kvT, s_kvt, s_kvc, s_outC, s_stt, s_stc = (sem(n) for n in (
                "s_cin", "t_step", "s_kvT", "s_kvt", "s_kvc", "s_outC", "s_stt", "s_stc"))
            block = ph.enter_context(nc.Block())
            NQ = segs["kv"][2]
            ROUNDS = TOPK_P // 8
            RQ = ROUNDS // NQ
            FILLS = [(src, i) for src in (0, 1) for i in range(3)]
            ST_FILLS = POOLW // P // 4

            @block.sync
            def _(sp):
                load_segment(sp, "kv")

            @block.gpsimd
            def _(pool):
                pool.dma_start(negP[:], t["c_causal"]).then_inc(s_cin, 16)
                pool.dma_start(stN[:], t["state_pool"][0].rearrange("b s c -> (b s) c")).then_inc(s_cin, 16)
                all_stored(pool, "kv")
                pool.dma_start(kT, tiles(projT, T_K, G)).then_inc(s_kvT, 16)
                pool.dma_start(vT[:], tiles(projT, T_V, G)).then_inc(s_kvT, 16)
                pool.wait_ge(s_kvc, len(FILLS))
                for o, src in ((2, kN), (3, vN)):
                    pool.dma_start(out[o][0, 0].rearrange("(a p) g d -> p a (g d)", p=P), src[:, 0:2, :]).then_inc(s_outC, 16)
                    pool.dma_start(out[o + 4][0].rearrange("b s g d -> (b s) (g d)"), src[0:N_S, 2, :]).then_inc(s_outC, 16)
                pool.wait_ge(s_outC, 64)

            def dve_weave(dve, q, j):
                per = QC // RQ
                r, s = j // per, j % per
                base = q * (4 * RQ) + 4 * r
                for i, (a, z) in enumerate(((0, P), (P, L2))):
                    if s == 2 * i:
                        dve.wait_ge(t_step, base + (2 * i + 1))
                        alone(dve)
                        nc.vector.max(top8[:, i, :], scP[:, a:z]).then_inc(t_step, 1)
                    if s == 2 * i + 1:
                        dve.wait_ge(t_step, base + (2 * i + 2))
                        alone(dve)
                        nc.vector.match_replace(scP[:, a:z], top8[:, i, :], scP[:, a:z], TAKEN).then_inc(t_step, 1)

            @block.scalar
            def _(act):
                act_segment(act, "kv")

            @block.vector
            def _(dve):
                dve.wait_ge(s_cin, 32)
                nc.vector.tensor_tensor(scP, scP, negP[:], ALU.add).then_inc(t_step, 1)
                dve_segment(dve, "kv", dve_weave)
                steps = 4 * ROUNDS + 1
                dve.wait_ge(t_step, steps)
                nc.vector.tensor_scalar(keepP[:], scP, TAKEN_EDGE, NEG, ALU.is_ge, ALU.mult).then_inc(t_step, 1)
                dve.wait_ge(t_step, steps + 1)
                nc.vector.tensor_tensor(maskP, keepP[:], negP[:], ALU.min).then_inc(t_step, 1)
                for f, (src, i) in enumerate(FILLS):
                    r = TT[i][1]
                    dve.wait_ge(s_kvt, f + 1)
                    nc.vector.tensor_copy((kN, vN)[src][0:r, i, :], sbank[f % 4][0:r, 0:KVW]).then_inc(s_kvc, 1)
                for f in range(ST_FILLS):
                    dve.wait_ge(s_stt, f + 1)
                    nc.vector.tensor_copy(stT[:, 4 * f:4 * f + 4, :], sbank[(f + 2) % 4][:, 0:4 * NB_S * STATE].rearrange(
                        "p (a n) -> p a n", a=4)).then_inc(s_stc, 1)

            @block.tensor
            def _(pe):
                pe_segment(pe, "kv")
                pe.wait_ge(s_kvT, 32)
                for f, (src, i) in enumerate(FILLS):
                    c0, r = TT[i]
                    if f >= 4:
                        pe.wait_ge(s_kvc, f - 3)
                    for g in range(G):
                        tr = nc.tensor.transpose(sbank[f % 4][0:r, g * P:(g + 1) * P], (kT, vT)[src][:, g, c0:c0 + r], ident[:])
                    tr.then_inc(s_kvt, 1)
                pe.wait_ge(s_cin, 32)
                for f in range(ST_FILLS):
                    if f < 2:
                        pe.wait_ge(s_kvc, f + 3)
                    else:
                        pe.wait_ge(s_kvc, 6)
                        pe.wait_ge(s_stc, f - 1) if f >= 4 else None
                    for a in range(4):
                        tr = nc.tensor.transpose(sbank[(f + 2) % 4][:, a * NB_S * STATE:(a + 1) * NB_S * STATE],
                                                 stN[:, (4 * f + a) * P:(4 * f + a + 1) * P],
                                                 ident[0:NB_S * STATE, 0:NB_S * STATE])
                    tr.then_inc(s_stt, 1)

        with ExitStack() as ph:
            qh = sb("qh", [P, T_P], ctx=ph)
            relh = sb("relh", [P, L2], ctx=ph)
            lg = sb("lg", [P, L2], ctx=ph)
            pT = sb("pT", [P, L2], ctx=ph)
            ohT = sb("ohT", [P, T_P], ctx=ph)
            nmx = sb("nmx", [P, 2], ctx=ph)
            rs = sb("rs", [P, 2], ctx=ph)
            ri = sb("ri", [P, 2], ctx=ph)
            scS = sb("scS", [N_S, LS], ctx=ph)
            negS = sb("negS", [N_S, T_S], ctx=ph)
            tops = sb("tops", [N_S, 8], ctx=ph)
            uin = sb("uin", [P, 4, N], ctx=ph)
            ubuf = [sb(f"ubuf{i}", [P, 4, UW], ctx=ph) for i in range(3)]
            cntr = sb("cntr", [P, NG, STATE + 1], ctx=ph)
            fix = sb("fix", [P, 4, STATE + 1], ctx=ph)
            dl = sb("dl", [P, 4, N], ctx=ph)
            wp = sb("wp", [P, 4, 4 * P], ctx=ph)
            obuf = sb("obuf", [P, 4, N], ctx=ph)
            ut = ubuf[0][:].rearrange("p a n -> p (a n)")[:, 0:4 * P].rearrange("p (a n) -> p a n", a=4)
            utN = ubuf[1][:].rearrange("p a n -> p (a n)")[:, 0:4 * P]
            gex = keep[:, G * N:G * N + 2 * N].rearrange("p (a n) -> p a n", a=2)
            gated_b, exped_b = sem("gated_b"), sem("exped_b")
            ut_in, ut_t, ut_c, ut_out = (sem(n) for n in ("ut_in", "ut_t", "ut_c", "ut_out"))
            (d_in, a_q, a_rel, a_s, a_lg, a_mx, a_exp, a_ri, a_pr, a_pt, a_ptc, a_pv, a_oh, a_st, ts_step, ts_fin,
             u_in, u_step, u_st, w_in_, w_pe, w_ev, w_st) = (sem(n) for n in (
                 "d_in", "a_q", "a_rel", "a_s", "a_lg", "a_mx", "a_exp", "a_ri", "a_pr", "a_pt", "a_ptc", "a_pv", "a_oh",
                 "a_st", "ts_step", "ts_fin", "u_in", "u_step", "u_st", "w_in_", "w_pe", "w_ev", "w_st"))
            block = ph.enter_context(nc.Block())
            NQ = segs["u"][2]
            HPQ = H // (2 * NQ)
            ROUNDS = TOPK_S // 8
            RQ = ROUNDS // (2 * NQ)
            UN = UW - STATE - T_P
            assert HPQ == 2 and NQ == R and NG == NQ and G == 4

            @block.sync
            def _(sp):
                load_segment(sp, "u")
                load_segment(sp, "gb")

            def head_number(half, q, u):
                return q * HPQ + (half * NQ * HPQ + u)

            def head_load(pool, half, q, u):
                h, n = q + (2 * half + u) * R, head_number(half, q, u)
                pool.wait_ge(a_s, n)
                alone(pool)
                pool.dma_start(qh[:], tile_rows(projT, h)[:, 0:T_P]).then_inc(a_q, 16)
                pool.wait_ge(a_lg, n)
                alone(pool)
                bias = biasP[ds(h, 1), P - 1:P - 1 + P * (BIAS_W - 1)].rearrange("o (a n) -> (o a) n", n=BIAS_W - 1)
                pool.dma_start(relh[:, P:L2], bias[:, 0:T_P]).then_inc(a_rel, 16)
                pool.dma_start(relh[:, 0:P], bias[:, P:T_P]).then_inc(a_rel, 16)

            def head_store(pool, half, q, u):
                h, n = q + (2 * half + u) * R, head_number(half, q, u)
                pool.wait_ge(a_oh, n + 1)
                alone(pool)
                pool.dma_start(tile_rows(oT, h)[:, 0:T_P], ohT[:]).then_inc(a_st, 16)

            U_STEPS = [0]

            def pool_steps(pool, g, between=None):
                win = WINS[g]
                base = sum(U_STEPS)
                n_ = [base]

                def done(ins):
                    n_[0] += 1
                    ins.then_inc(u_step, 1)
                    pool.wait_ge(u_step, n_[0])

                pool.wait_ge(stored[0], 16 * (segs["u"][4] + g + 1))
                pool.wait_ge(stored[1], 16 * (segs["u"][4] + g + 1))
                pool.dma_start(uin[:], tiles(projT, T_U + 4 * g, 4)).then_inc(u_in, 16)
                pool.wait_ge(u_in, 16 * (g + 1))
                U, A, B = ubuf
                if g:
                    pool.wait_ge(u_st, 16 * g)
                nc.gpsimd.memset(U[:, :, 0:STATE], 0.0)
                nc.gpsimd.tensor_copy(U[:, :, STATE:STATE + T_P], uin[:, :, 0:T_P])
                for a in range(4):
                    rows = U[:, a, STATE + T_P:UW].rearrange("p (b n) -> p b n", b=NB_S)
                    nc.gpsimd.tensor_copy(rows[:, :, 0:STATE], stT[:, 4 * g + a, :].rearrange("p (b n) -> p b n", b=NB_S))
                    ins = nc.gpsimd.tensor_copy(rows[:, :, STATE:], uin[:, a, T_P:N].rearrange("p (b n) -> p b n", b=NB_S))
                done(ins)
                src, w, lost = U, 1, 0
                while w < win:
                    dst = A if src is not A else B
                    done(nc.gpsimd.tensor_tensor(dst[:, :, lost + w:UW], src[:, :, lost + w:UW], src[:, :, lost:UW - w], ALU.add))
                    src, lost, w = dst, lost + w, 2 * w
                if between:
                    between()
                other = A if src is B else B
                done(nc.gpsimd.tensor_tensor(fix[:, :, 0:STATE], src[:, :, STATE:2 * STATE],
                                             cntr[:, g:g + 1, 0:STATE].to_broadcast([P, 4, STATE]), ALU.mult))
                done(nc.gpsimd.tensor_scalar(other[:, :, STATE:UW], src[:, :, STATE:UW], 1.0 / win, None, ALU.mult))
                dp = src[:].rearrange("p a n -> p (a n)")[:, 0:4 * N].rearrange("p (a n) -> p a n", a=4)
                nc.gpsimd.tensor_tensor(dp[:, :, 0:STATE], fix[:, :, 0:STATE], U[:, :, STATE:2 * STATE], ALU.subtract)
                ins = nc.gpsimd.tensor_tensor(dp[:, :, STATE:T_P], other[:, :, 2 * STATE:STATE + T_P],
                                              U[:, :, 2 * STATE:STATE + T_P], ALU.subtract)
                for a in range(4):
                    m_, u_ = (x[:, a, STATE + T_P:UW].rearrange("p (b n) -> p b n", b=NB_S)[:, :, STATE:] for x in (other, U))
                    ins = nc.gpsimd.tensor_tensor(dp[:, a, T_P:N].rearrange("p (b n) -> p b n", b=NB_S), m_, u_, ALU.subtract)
                done(ins)
                pool.dma_start(tiles(poolT, 4 * g, 4), dp).then_inc(u_st, 16)
                U_STEPS.append(n_[0] - base)

            @block.gpsimd
            def _(pool):
                pool.dma_start(scS[:], scores).then_inc(d_in, 16)
                pool.dma_start(negS[:], t["c_causal_s"]).then_inc(d_in, 16)
                pool.dma_start(cntr[:], t["c_count"]).then_inc(d_in, 16)
                pool.wait_ge(d_in, 48)
                head_load(pool, 0, 0, 0)
                pool.dma_start(out[9][0, :, 0:STATE - T_S, :], t["state_pool"][0, :, T_S:STATE, :]).then_inc(ut_out, 16)
                for q in range(NQ):
                    head_load(pool, 0, q, 1)
                    if q:
                        pool_steps(pool, q - 1)
                    head_store(pool, 0, q, 0)
                    if q + 1 < NQ:
                        head_load(pool, 0, q + 1, 0)
                    else:
                        head_load(pool, 1, 0, 0)
                    head_store(pool, 0, q, 1)

                def group_load(q):
                    pool.wait_ge(w_pe, q * 4)
                    pool.wait_ge(u_st, q * 16 + 16)
                    alone(pool)
                    pool.dma_start(wp[:], t["w_pool"][0, ds(q, 1)].rearrange("g (a p) d -> p (g a) d", p=P)).then_inc(w_in_, 16)
                    pool.dma_start(dl[:], tiles(poolT, q * 4, 4)).then_inc(w_in_, 16)

                def group_store(q):
                    pool.wait_ge(w_ev, q * 4 + 4)
                    alone(pool)
                    pool.dma_start(tiles(mixT, q * 4, 4), obuf[:]).then_inc(w_st, 16)

                group_load(0)
                pool_steps(pool, NQ - 1, lambda: head_load(pool, 1, 0, 1))
                pool.wait_ge(u_st, 16 * NG)

                def gate_quad(q, more):
                    pool.dma_start(ut, projT[ds(q * 4 + T_U, 4), :, N - P:N].rearrange("a p n -> p a n")).then_inc(ut_in, 16)
                    head_store(pool, 1, q, 0)
                    if more:
                        head_load(pool, 1, q + 1, 0)
                    head_store(pool, 1, q, 1)
                    if more:
                        group_load(q + 1)
                        group_store(q)
                    pool.wait_ge(ut_c, q + 1)
                    alone(pool)
                    first, cols = P - N_S - STATE, ds(q * (4 * P), 4 * P)
                    pool.dma_start(out[5][0, 0][:, cols], utN[first:first + STATE, :]).then_inc(ut_out, 16)
                    for b in range(NB_S):
                        r0 = P - N_S + b * T_S
                        pool.dma_start(out[9][0, b, STATE - T_S:STATE][:, cols], utN[r0:r0 + T_S, :]).then_inc(ut_out, 16)
                    if more:
                        head_load(pool, 1, q + 1, 1)
                    else:
                        group_store(q)
                with pool.Fori(0, NQ - 1) as q:
                    gate_quad(q, True)
                gate_quad(NQ - 1, False)
                pool.wait_ge(ut_out, 16 * (NQ * (NB_S + 1) + 1))
                pool.wait_ge(w_st, 16 * NG)
                pool.wait_ge(a_st, 16 * H)

            def pe_weave(half):
                def weave(pe, q, j):
                    u, s = j // 8, j % 8
                    g = 2 * half + u
                    n = q * HPQ + (half * NQ * HPQ + u)
                    if s == 1:
                        pe.wait_ge(a_q, n * 16 + 16)
                        pe.wait_ge(a_lg, n)
                        nc.tensor.matmul(sbank[0][:, 0:L2], identb[:], maskP, start=True, stop=False)
                        nc.tensor.matmul(sbank[0][:, 0:P], qh[:, 0:P], kT[:, g, 0:P], start=False, stop=False)
                        nc.tensor.matmul(sbank[0][:, P:L2], qh[:, P:T_P], kT[:, g, 0:T_P], start=False,
                                         stop=True).then_inc(a_s, 1)
                    if s == 4:
                        pe.wait_ge(a_pr, n + 1)
                        pe.wait_ge(a_ptc, n)
                        for i in range(3):
                            tr = nc.tensor.transpose(sbank[1][:, i * P:(i + 1) * P], lg[:, i * P:(i + 1) * P], ident[:])
                        tr.then_inc(a_pt, 1)
                    if s == 6:
                        pe.wait_ge(a_ptc, n + 1)
                        pe.wait_ge(a_oh, n)
                        gv = slice(g * P, (g + 1) * P)
                        nc.tensor.matmul(sbank[2][:, 0:P], vN[:, 0, gv], pT[:, 0:P], start=True, stop=True)
                        nc.tensor.matmul(sbank[2][:, P:T_P], vN[:, 0, gv], pT[:, P:2 * P], start=True, stop=False)
                        nc.tensor.matmul(sbank[2][:, P:T_P], vN[:, 1, gv], pT[:, 2 * P:L2], start=False,
                                         stop=True).then_inc(a_pv, 1)
                    if half and j % 4 == 3:
                        dt = j // 4
                        if dt == 0:
                            pe.wait_ge(w_in_, q * 32 + 32)
                        pe.wait_ge(w_ev, q * 4 + dt)
                        if dt == 3:
                            pe.wait_ge(ut_c, q + 1)
                        for a in range(4):
                            mm = nc.tensor.matmul(sbank[3][:, 0:N], wp[:, a, dt * P:(dt + 1) * P], dl[:, a, :],
                                                  start=a == 0, stop=a == 3)
                        mm.then_inc(w_pe, 1)
                    if half and j == 13:
                        pe.wait_ge(ut_in, q * 16 + 16)
                        pe.wait_ge(w_ev, q * 4 + 3)
                        for a in range(4):
                            tr = nc.tensor.transpose(sbank[3][:, a * P:(a + 1) * P], ut[:, a, :], ident[:])
                        tr.then_inc(ut_t, 1)
                return weave

            def act_weave(half):
                def weave(act, q, j):
                    u, s = j // 8, j % 8
                    n = q * HPQ + (half * NQ * HPQ + u)
                    if s == 2:
                        act.wait_ge(a_mx, n + 1)
                        for i, (a, z) in enumerate(((0, P), (P, L2))):
                            ins = nc.scalar.activation(lg[:, a:z], lg[:, a:z], ACT.Exp, bias=nmx[:, i:i + 1],
                                                       accum_out=rs[:, i:i + 1])
                        ins.then_inc(a_exp, 1)
                    if s == 4:
                        act.wait_ge(a_pt, n + 1)
                        act.wait_ge(a_pv, n)
                        nc.scalar.activation(pT[:], sbank[1][:, 0:L2], ACT.Copy).then_inc(a_ptc, 1)
                    if s == 6:
                        act.wait_ge(a_pv, n + 1)
                        act.wait_ge(a_st, n * 16)
                        nc.scalar.activation(ohT[:], sbank[2][:, 0:T_P], ACT.Copy).then_inc(a_oh, 1)
                return weave

            def dve_weave(half):
                def weave(dve, q, j):
                    u, s = j // 8, j % 8
                    n = q * HPQ + (half * NQ * HPQ + u)
                    if s == 1:
                        dve.wait_ge(a_s, n + 1)
                        dve.wait_ge(a_rel, n * 32 + 32)
                        dve.wait_ge(a_pt, n)
                        nc.vector.scalar_tensor_tensor(lg[:], sbank[0][:, 0:L2], SCALE, relh[:], ALU.mult,
                                                       ALU.add).then_inc(a_lg, 1)
                        dve.wait_ge(a_lg, n + 1)
                        for i, (a, z) in enumerate(((0, P), (P, L2))):
                            ins = nc.vector.tensor_reduce(nmx[:, i:i + 1], lg[:, a:z], AX.X, ALU.max, negate=True)
                        ins.then_inc(a_mx, 1)
                    if s == 3:
                        dve.wait_ge(a_exp, n + 1)
                        nc.vector.reciprocal(ri[:], rs[:]).then_inc(a_ri, 1)
                        dve.wait_ge(a_ri, n + 1)
                        for i, (a, z) in enumerate(((0, P), (P, L2))):
                            ins = nc.vector.tensor_scalar(lg[:, a:z], lg[:, a:z], ri[:, i:i + 1], None, ALU.mult)
                        ins.then_inc(a_pr, 1)
                    if half and j % 4 == 3:
                        dt = j // 4
                        dve.wait_ge(w_pe, q * 4 + (dt + 1))
                        if dt == 0:
                            dve.wait_ge(w_st, q * 16)
                        nc.vector.tensor_scalar(obuf[:, dt, :], sbank[3][:, 0:N], poolscT[:, ds(q * 4 + dt, 1)], None,
                                                ALU.mult).then_inc(w_ev, 1)
                    if half and j == 13:
                        dve.wait_ge(ut_t, q + 1)
                        dve.wait_ge(ut_out, q * (16 * (NB_S + 1)) + 16)
                        nc.vector.tensor_copy(utN, sbank[3]).then_inc(ut_c, 1)
                    if j % (QC // RQ) in (0, 2):
                        k = (q + half * NQ) * (2 * RQ) + (2 * (j // (QC // RQ)) + (j % (QC // RQ)) // 2)
                        dve.wait_ge(ts_step, k + 1)
                        alone(dve)
                        if j % (QC // RQ) == 0:
                            nc.vector.max(tops[:], scS[:]).then_inc(ts_step, 1)
                        else:
                            nc.vector.match_replace(scS[:], tops[:], scS[:], TAKEN).then_inc(ts_step, 1)
                return weave

            @block.scalar
            def _(act):
                act_segment(act, "u", act_weave(0))
                act_segment(act, "gb", act_weave(1), gate=(gex, exped_b, gated_b))

            @block.vector
            def _(dve):
                dve.wait_ge(d_in, 48)
                nc.vector.tensor_tensor(scS[:, PAST:LS], scS[:, PAST:LS], negS[:], ALU.add).then_inc(ts_step, 1)
                dve_segment(dve, "u", dve_weave(0))
                dve_segment(dve, "gb", dve_weave(1), gate=(gex, exped_b, gated_b))
                dve.wait_ge(gated_b, 6 * NQ)
                nc.vector.memset(maskS, 0.0).then_inc(ts_fin, 1)
                dve.wait_ge(ts_step, 2 * ROUNDS + 1)
                dve.wait_ge(ts_fin, 1)
                nc.vector.tensor_scalar(maskS[0:N_S, :], scS[:], TAKEN_EDGE, NEG, ALU.is_ge, ALU.mult).then_inc(ts_fin, 1)

            @block.tensor
            def _(pe):
                pe_segment(pe, "u", pe_weave(0))
                pe_segment(pe, "gb", pe_weave(1))

        with ExitStack() as ph:
            KEPT = 5
            after_qS = era + H * N_S
            kpg = sb("kpg", [P, PAGES, KVW], ctx=ph)
            vpg_own = sb("vpg_own", [P, PAGES - KEPT, KVW], ctx=ph)
            vpg = [keep[:, after_qS + p * KVW:after_qS + (p + 1) * KVW] for p in range(KEPT)] + [
                vpg_own[:, p, :] for p in range(PAGES - KEPT)]
            KTs = sb("KTs", [P, G, LS], ctx=ph)
            vnew = sb("vnew", [T_S, KVW], ctx=ph)
            rel = sb("rel", [P, LS], ctx=ph)
            lgS = sb("lgS", [P, LS], ctx=ph)
            pTs = sb("pTs", [P, PAGES + 1, P], ctx=ph)
            free = after_qS + KEPT * KVW
            qb = keep[:, free:free + P]
            oN = keep[:, free + P:free + P + HD]
            pick = sb("pick", [P, P], BF16, ctx=ph)
            st1 = sb("st1", [P, 4], ctx=ph)
            gexE = sb("gexE", [P, 2, N], ctx=ph)
            gated_a, exped_a = sem("gated_a"), sem("exped_a")
            (e_in, e_rel, e_k, e_v, e_pick, e_vnew, e_kt, e_kcA, e_kcD, e_kn, e_s, e_lg, e_mx, e_exp, e_ri, e_pt,
             e_ptA, e_pv, e_on, e_ot, e_o) = (sem(n) for n in (
                 "e_in", "e_rel", "e_k", "e_v", "e_pick", "e_vnew", "e_kt", "e_kcA", "e_kcD", "e_kn", "e_s", "e_lg",
                 "e_mx", "e_exp", "e_ri", "e_pt", "e_ptA", "e_pv", "e_on", "e_ot", "e_o"))
            f_in = [sem(f"f_in{m}") for m in range(KT // 4)]
            block = ph.enter_context(nc.Block())
            NQ = segs["ga"][2]
            BQ = NB_S // NQ
            FOUR = 4 * N
            kept_spots = [keep[:, after_qS + k * FOUR:after_qS + (k + 1) * FOUR].rearrange("p (a n) -> p a n", a=4)
                          for k in range(2)]
            assert BQ == 2 and PAGES == 8 and KVW == 512 and LS <= 3 * 512

            @block.sync
            def _(sp):
                for h in range(H):
                    bias = biasS[h:h + 1, T_S - 1:T_S - 1 + T_S * (LS + T_S - 1)].rearrange("o (a n) -> (o a) n", n=LS + T_S - 1)
                    sp.dma_start(rel[h * T_S:(h + 1) * T_S, :], bias[:, 0:LS]).then_inc(e_rel, 16)
                load_segment(sp, "ga")

            @block.gpsimd
            def _(pool):
                def load_pages(b, cache, dst, landed):
                    src = t[cache][0].rearrange("n r g d -> n r (g d)")
                    for p in range(PAGES):
                        page = pool.value_load(ptab[0:1, ds(b * PAGES + p, 1)], min_val=0, max_val=N_PHYS - 1)
                        pool.dma_start(dst[p], tile_rows(src, page)).then_inc(landed, 16)

                def load_pick(b):
                    pool.dma_start(pick[:], tile_rows(t["c_pick"], b)).then_inc(e_pick, 16)

                def load_vnew(b):
                    pool.dma_start(vnew[:], out[7][0, ds(b, 1)].rearrange("b s g d -> (b s) (g d)")).then_inc(e_vnew, 16)

                keys = [kpg[:, p, :] for p in range(PAGES)]
                load_pages(0, "cache_k", keys, e_k)
                pool.dma_start(qS, projT[T_Q:T_Q + H, :, T_P:N].rearrange("h p n -> p h n")).then_inc(e_in, 16)
                load_pick(0)
                load_pages(0, "cache_v", vpg, e_v)
                load_vnew(0)
                with pool.Fori(1, NB_S) as b:
                    pool.wait_ge(e_kt, b * PAGES)
                    alone(pool)
                    load_pages(b, "cache_k", keys, e_k)
                    pool.wait_ge(e_s, b)
                    alone(pool)
                    load_pick(b)
                    pool.wait_ge(e_pv, b)
                    alone(pool)
                    load_pages(b, "cache_v", vpg, e_v)
                    load_vnew(b)
                pool.wait_ge(e_pv, NB_S)
                pool.dma_start(kept_spots[0], tiles(mixT, 0, 4)).then_inc(f_in[0], 16)
                pool.dma_start(kept_spots[1], tiles(projT, T_GB, 4)).then_inc(f_in[0], 16)

            def pe_weave(pe, q, j):
                u, s = j // 8, j % 8
                b = q * BQ + u
                if s in (0, 1):
                    for p in range(4 * s, 4 * s + 4):
                        if p == 0:
                            pe.wait_ge(e_k, b * (16 * PAGES) + 16 * PAGES)
                            pe.wait_ge(e_ptA, b)
                        if p == 3:
                            pe.wait_ge(e_o, b)
                        if p >= 4:
                            pe.wait_ge((e_kcA, e_kcD)[p % 2], b * (PAGES // 2) + (p - 4) // 2 + 1)
                        for g in range(G):
                            tr = nc.tensor.transpose(sbank[p % 4][:, g * P:(g + 1) * P], kpg[:, p, g * P:(g + 1) * P], ident[:])
                        tr.then_inc(e_kt, 1)
                if s == 3:
                    pe.wait_ge(e_pick, b * 16 + 16)
                    pe.wait_ge(e_kcA, b * (PAGES // 2) + PAGES // 2)
                    pe.wait_ge(e_kcD, b * (PAGES // 2) + PAGES // 2)
                    pe.wait_ge(e_kn, b * 2 + 2)
                    for c in range(0, LS, 512):
                        z = min(LS, c + 512)
                        nc.tensor.matmul(wide[:, c:z], pick[:], maskS[:, c:z], start=True, stop=True)
                        for g in range(G):
                            mm = nc.tensor.matmul(wide[32 * g:32 * g + 32, c:z], qb[:, 32 * g:32 * g + 32], KTs[:, g, c:z],
                                                  start=False, stop=True, skip_group_check=True)
                    mm.then_inc(e_s, 1)
                if s == 5:
                    pe.wait_ge(e_exp, b + 1)
                    for p in range(PAGES + 1):
                        r = P if p < PAGES else T_S
                        tr = nc.tensor.transpose(wide[0:r, p * P:(p + 1) * P], lgS[:, p * P:p * P + r], ident[:])
                    tr.then_inc(e_pt, 1)
                if s == 6:
                    pe.wait_ge(e_ptA, b + 1)
                    pe.wait_ge(e_v, b * (16 * PAGES) + 16 * PAGES)
                    pe.wait_ge(e_vnew, b * 16 + 16)
                    for p in range(PAGES + 1):
                        r = P if p < PAGES else T_S
                        v = vpg[p] if p < PAGES else vnew[:]
                        for g in range(G):
                            mm = nc.tensor.matmul(sbank[3][32 * g:32 * g + 32, 0:HD], pTs[0:r, p, 32 * g:32 * g + 32],
                                                  v[:, g * P:(g + 1) * P], start=p == 0, stop=p == PAGES,
                                                  skip_group_check=True)
                    mm.then_inc(e_pv, 1)
                if s == 7:
                    pe.wait_ge(e_on, b + 1)
                    nc.tensor.transpose(sbank[3][:, P:2 * P], oN, ident[:]).then_inc(e_ot, 1)

            def turned_keys(eng, copy, s, b, even, done):
                eng.wait_ge(e_s, b)
                for p in range(4 * s + (0 if even else 1), 4 * s + 4, 2):
                    eng.wait_ge(e_kt, b * PAGES + (p + 1))
                    copy(KTs[:, :, p * P:(p + 1) * P], sbank[p % 4].rearrange("p (g n) -> p g n", g=G)).then_inc(done, 1)

            def act_weave(act, q, j):
                u, s = j // 8, j % 8
                b = q * BQ + u
                if s in (0, 1):
                    turned_keys(act, lambda o, i: nc.scalar.activation(o, i, ACT.Copy), s, b, True, e_kcA)
                if s == 4:
                    act.wait_ge(e_mx, b + 1)
                    nc.scalar.activation(lgS[:], lgS[:], ACT.Exp, bias=st1[:, 0:1], accum_out=st1[:, 1:2]).then_inc(e_exp, 1)
                if s == 5:
                    act.wait_ge(e_pt, b + 1)
                    act.wait_ge(e_pv, b)
                    nc.scalar.activation(pTs[:, 0:PAGES, :], wide[:, 0:PAST].rearrange("p (a n) -> p a n", n=P), ACT.Copy)
                    nc.scalar.activation(pTs[0:T_S, PAGES, :], wide[0:T_S, PAST:PAST + P], ACT.Copy).then_inc(e_ptA, 1)
                if s == 7:
                    act.wait_ge(e_ot, b + 1)
                    nc.scalar.activation(qS[:, :, ds(b * T_S, T_S)], sbank[3][:, P:2 * P].rearrange("p (h n) -> p h n", h=H),
                                         ACT.Copy).then_inc(e_o, 1)

            def dve_weave(dve, q, j):
                u, s = j // 8, j % 8
                b = q * BQ + u
                if s in (0, 1):
                    turned_keys(dve, nc.vector.tensor_copy, s, b, False, e_kcD)
                if s == 2:
                    dve.wait_ge(e_in, 16)
                    nc.vector.tensor_copy(KTs[:, :, PAST:LS], kT[:, :, ds(b * T_S + T_P, T_S)]).then_inc(e_kn, 1)
                    nc.vector.tensor_copy(qb.rearrange("p (h n) -> p h n", h=H), qS[:, :, ds(b * T_S, T_S)]).then_inc(e_kn, 1)
                if s == 3:
                    dve.wait_ge(e_rel, 16 * H)
                    dve.wait_ge(e_s, b + 1)
                    dve.wait_ge(e_pt, b)
                    nc.vector.scalar_tensor_tensor(lgS[:], wide[:, 0:LS], SCALE, rel[:], ALU.mult, ALU.add).then_inc(e_lg, 1)
                    dve.wait_ge(e_lg, b + 1)
                    nc.vector.tensor_reduce(st1[:, 0:1], lgS[:], AX.X, ALU.max, negate=True).then_inc(e_mx, 1)
                if s == 5:
                    dve.wait_ge(e_exp, b + 1)
                    nc.vector.reciprocal(st1[:, 2:3], st1[:, 1:2]).then_inc(e_ri, 1)
                if s == 6:
                    dve.wait_ge(e_ri, b + 1)
                    dve.wait_ge(e_pv, b + 1)
                    dve.wait_ge(e_ot, b)
                    nc.vector.tensor_scalar(oN, sbank[3][:, 0:HD], st1[:, 2:3], None, ALU.mult).then_inc(e_on, 1)

            @block.scalar
            def _(act):
                act_segment(act, "ga", act_weave, gate=(gexE[:], exped_a, gated_a))

            @block.vector
            def _(dve):
                dve_segment(dve, "ga", dve_weave, gate=(gexE[:], exped_a, gated_a))

            @block.tensor
            def _(pe):
                pe_segment(pe, "ga", pe_weave)

        with ExitStack() as ph:
            y = [sb(f"y{i}", [P, D], ctx=ph) for i in range(3)]
            gq = sb("gq", [P, 4 * P], ctx=ph)
            sqj = sb("sqj", [P, 4 * P], ctx=ph)
            NQ = segs["out"][2]
            sq = sb("sq", [P, 3, NQ], ctx=ph)
            ms = sb("ms", [P, 3], ctx=ph)
            rt = sb("rt", [P, 3], ctx=ph)
            nt = sb("nt", [P, 3], ctx=ph)
            rf = sb("rf", [P, 3], ctx=ph)
            (f_mul, f_hi, f_lo, f_t, f_add, f_sq, f_gq, f_g, f_sum, f_rt, f_rf, f_x, f_gd) = (sem(n) for n in (
                 "f_mul", "f_hi", "f_lo", "f_t", "f_add", "f_sq", "f_gq", "f_g", "f_sum", "f_rt", "f_rf", "f_x", "f_gd"))
            f_y = {e: sem(f"f_y_{e}") for e in ("act", "dve")}
            f_out = {e: sem(f"f_out_{e}") for e in ("act", "dve")}
            block = ph.enter_context(nc.Block())
            MIX = KT // 4
            HALF = MIX // 2
            spots = kept_spots + [keep[:, 0:FOUR].rearrange("p (a n) -> p a n", a=4)] + [
                y[i][:, k * FOUR:(k + 1) * FOUR].rearrange("p (a n) -> p a n", a=4)
                for i in range(3) for k in range(D // FOUR)]
            STEPS = len(spots) // 2
            om = [spots[2 * (m % STEPS)] for m in range(MIX)]
            gm = [spots[2 * (m % STEPS) + 1] for m in range(MIX)]
            UP_FRONT = 3
            rows = [t["x_prompt"][0, 0:P], t["x_prompt"][0, P:T_P], t["x_sample"].rearrange("b s d -> (b s) d")]
            outs = [out[0][0, 0:P], out[0][0, P:T_P], out[1].rearrange("b s d -> (b s) d")]

            def load_mix(eng, m):
                if m < HALF:
                    eng.dma_start(om[m], tiles(mixT, 4 * m, 4)).then_inc(f_in[m], 16)
                    eng.dma_start(gm[m], tiles(projT, T_GB + 4 * m, 4)).then_inc(f_in[m], 16)
                else:
                    k = 4 * (m - HALF)
                    eng.dma_start(om[m][:, :, 0:T_P], tiles(oT, k, 4)[:, :, 0:T_P]).then_inc(f_in[m], 16)
                    eng.dma_start(gm[m], tiles(projT, T_GA + k, 4)).then_inc(f_in[m], 16)

            CUTS = {"dve": ((0, 0, D // 2), (0, D // 2, D), (2, 0, D // 2), (2, D // 2, D)),
                    "act": ((1, 0, D // 4), (1, D // 4, D // 2), (1, D // 2, 3 * D // 4), (1, 3 * D // 4, D))}

            def scaled(eng, name, mul):
                eng.wait_ge(f_rf, 1)
                eng.wait_ge(f_g, NQ)
                eng.wait_ge(f_gd, 1)
                for n, (i, a, z) in enumerate(CUTS[name]):
                    r = TT[i][1]
                    mul(y[i][0:r, a:z], rf[0:r, i:i + 1]).then_inc(f_y[name], 1)
                    if name != "dve":
                        eng.wait_ge(f_y[name], n + 1)
                        eng.dma_start(outs[i][:, a:z], y[i][0:r, a:z]).then_inc(f_out[name], 16)
                if name != "dve":
                    eng.wait_ge(f_out[name], 16 * len(CUTS[name]))

            @block.sync
            def _(sp):
                for m in range(1, HALF):
                    load_mix(sp, m)
                all_stored(sp, "ga")
                for m in range(HALF, STEPS):
                    load_mix(sp, m)
                load_segment(sp, "out")
                for n, (i, a, z) in enumerate(CUTS["dve"]):
                    sp.wait_ge(f_y["dve"], n + 1)
                    sp.dma_start(outs[i][:, a:z], y[i][0:TT[i][1], a:z]).then_inc(f_out["dve"], 16)
                sp.wait_ge(f_out["dve"], 16 * len(CUTS["dve"]))

            @block.gpsimd
            def _(pool):
                all_stored(pool, "ga")
                for m in range(MIX):
                    if 0 < m <= MIX - STEPS:
                        pool.wait_ge(f_lo, m)
                        load_mix(pool, STEPS + m - 1)
                    pool.wait_ge(f_in[m], 32)
                    if m < HALF:
                        ins = nc.gpsimd.tensor_tensor(om[m], om[m], gm[m], ALU.mult)
                    else:
                        k = 4 * (m - HALF)
                        nc.gpsimd.tensor_tensor(om[m][:, :, 0:T_P], om[m][:, :, 0:T_P], gm[m][:, :, 0:T_P], ALU.mult)
                        ins = nc.gpsimd.tensor_tensor(om[m][:, :, T_P:N], qS[:, k:k + 4, :], gm[m][:, :, T_P:N], ALU.mult)
                    ins.then_inc(f_mul, 1)
                pool.wait_ge(f_lo, MIX)
                for i in range(3):
                    pool.dma_start(y[i][0:TT[i][1], :], rows[i]).then_inc(f_x, 16)
                def weigh(q, tiles_):
                    pool.wait_ge(f_g, q)
                    alone(pool)
                    pool.dma_start(gq[:], t["final_g"].rearrange("(o d) -> o d", o=1)[
                        :, ds(q * (4 * P), 4 * P)].to_broadcast([P, 4 * P])).then_inc(f_gq, 16)
                    pool.wait_ge(f_gq, q * 16 + 16)
                    pool.wait_ge(f_sq, q * 3 + 3)
                    for i in tiles_:
                        cols = y[i][0:TT[i][1], ds(q * (4 * P), 4 * P)]
                        ins = nc.gpsimd.tensor_tensor(cols, cols, gq[0:TT[i][1], :], ALU.mult)
                    ins.then_inc(f_g, 1)
                with pool.Fori(0, NQ - 1) as q:
                    weigh(q, (0, 1, 2))
                weigh(NQ - 1, (0, ))
                pool.wait_ge(f_g, NQ)

            def squares(act, q):
                for i in range(3):
                    r = TT[i][1]
                    act.wait_ge(f_sum, 1)
                    act.wait_ge(f_add, q * 3 + (i + 1))
                    act.wait_ge(f_sq, q * 3 + i)
                    nc.scalar.activation(sqj[0:r, :], y[i][0:r, ds(q * (4 * P), 4 * P)], ACT.Square,
                                         accum_out=sq[0:r, i, ds(q, 1)]).then_inc(f_sq, 1)

            def act_mix(act, m):
                k0 = (4 * m + KT // 2) % KT
                act.wait_ge(f_mul, m + 1)
                nc.scalar.activation(XH[:, k0:k0 + 4, :], om[m], ACT.Copy).then_inc(f_hi, 1)

            def dve_mix(dve, m):
                k0 = (4 * m + KT // 2) % KT
                dve.wait_ge(f_hi, m + 1)
                nc.vector.tensor_tensor(XL[:, k0:k0 + 4, :], om[m], XH[:, k0:k0 + 4, :].bitcast(F32),
                                        ALU.subtract).then_inc(f_lo, 1)

            def mix_weave(mix):
                def weave(eng, q, j):
                    if j < MIX - UP_FRONT:
                        mix(eng, UP_FRONT + j)
                return weave

            def act_weave(act, q, j):
                if j == 4:
                    squares(act, q - 1)

            def residual(dve, q):
                for i in range(3):
                    r = TT[i][1]
                    cols = y[i][0:r, ds(q * (4 * P), 4 * P)]
                    if i == 0:
                        dve.wait_ge(f_x, 48)
                        dve.wait_ge(f_t, q + 1)
                    nc.vector.tensor_tensor(cols, sbank[i][0:r, :], cols, ALU.add).then_inc(f_add, 1)

            def dve_weave(dve, q, j):
                if j == 2:
                    residual(dve, q - 1)

            def turn(pe, q):
                quad0 = segs["out"][4]
                pe.wait_ge(evac[0], q + (quad0 + 1))
                pe.wait_ge(evac[1], q + (quad0 + 2))
                pe.wait_ge(f_add, q * 3)
                for i, (c0, r) in enumerate(TT):
                    for n in range(4):
                        tr = nc.tensor.transpose(sbank[i][0:r, n * P:(n + 1) * P], stg[n // 2][:, n % 2, c0:c0 + r], ident[:])
                tr.then_inc(f_t, 1)

            def pe_weave(pe, q, j):
                if j == 2:
                    turn(pe, q - 1)

            @block.scalar
            def _(act):
                for m in range(UP_FRONT):
                    act_mix(act, m)
                act_quad(act, "out", 0, mix_weave(act_mix), turned=f_t)
                with act.Fori(1, NQ - 1) as q:
                    act_quad(act, "out", q, act_weave, turned=f_t)
                act_quad(act, "out", NQ - 1, act_weave, True, turned=f_t)
                squares(act, NQ - 1)
                act.wait_ge(f_sum, 3)
                nc.scalar.activation(rt[:], ms[:], ACT.Sqrt).then_inc(f_rt, 1)
                scaled(act, "act", lambda o, r: nc.scalar.activation(o, o, ACT.Copy, scale=r))

            @block.vector
            def _(dve):
                for m in range(UP_FRONT):
                    dve_mix(dve, m)
                dve_quad(dve, "out", 0, mix_weave(dve_mix), turned=f_t)
                nc.vector.memset(sq[:], 1.0).then_inc(f_sum, 1)
                with dve.Fori(1, NQ - 1) as q:
                    dve_quad(dve, "out", q, dve_weave, turned=f_t)
                dve_quad(dve, "out", NQ - 1, dve_weave, True, turned=f_t)
                residual(dve, NQ - 1)
                dve.wait_ge(f_sq, 3 * NQ)
                nc.vector.tensor_reduce(ms[:], sq[:], AX.X, ALU.add).then_inc(f_sum, 1)
                dve.wait_ge(f_sum, 2)
                nc.vector.tensor_scalar(ms[:], ms[:], 1.0 / D, EPS, ALU.mult, ALU.add).then_inc(f_sum, 1)
                dve.wait_ge(f_gq, 16 * NQ)
                for i in (1, 2):
                    cols = y[i][0:TT[i][1], D - 4 * P:D]
                    ins = nc.vector.tensor_tensor(cols, cols, gq[0:TT[i][1], :], ALU.mult)
                ins.then_inc(f_gd, 1)
                dve.wait_ge(f_rt, 1)
                nc.vector.reciprocal(rt[:], rt[:]).then_inc(f_sum, 1)
                dve.wait_ge(f_sum, 4)
                nc.vector.tensor_tensor(nt[:], rt[:], rt[:], ALU.mult).then_inc(f_sum, 1)
                dve.wait_ge(f_sum, 5)
                nc.vector.tensor_tensor(nt[:], nt[:], ms[:], ALU.mult).then_inc(f_sum, 1)
                dve.wait_ge(f_sum, 6)
                nc.vector.tensor_scalar(nt[:], nt[:], -0.5, 1.5, ALU.mult, ALU.add).then_inc(f_sum, 1)
                dve.wait_ge(f_sum, 7)
                nc.vector.tensor_tensor(rf[:], rt[:], nt[:], ALU.mult).then_inc(f_rf, 1)
                scaled(dve, "dve", lambda o, r: nc.vector.tensor_scalar(o, o, r, None, ALU.mult))

            @block.tensor
            def _(pe):
                pe_quad(pe, "out", 0, before=lambda pe, j: pe.wait_ge(f_lo, min(j, CH - 1) + 1))
                with pe.Fori(1, NQ) as q:
                    pe_quad(pe, "out", q, pe_weave)
                turn(pe, NQ - 1)


_INS = ["x_prompt", "x_sample", "cache_k", "cache_v", "cache_idx_k", "state_pool", "page_table", "rel_bias", "ln_g",
        "w_in", "w_pool", "pool_scale", "w_out", "final_g"]


def kernel(**inputs):
    import math

    import ml_dtypes
    import concourse.bacc as _bacc
    from concourse.bass_utils import run_bass_kernel_spmd as _run

    nc = _bacc.Bacc("TRN2", target_bir_lowering=False, num_devices=1, dynamic_dma_scratch_size=8192)
    arrays, t = {}, {}

    def give(name, a):
        a = np.ascontiguousarray(a)
        arrays[name] = a
        t[name] = nc.dram_tensor(name, a.shape, mybir.dt.from_np(a.dtype), kind="ExternalInput").ap()

    for name in _INS:
        give(name, inputs[name])
    _, t_p, d = inputs["x_prompt"].shape
    b_s, t_s, _ = inputs["x_sample"].shape
    depth, n_phys, page, g, hd = inputs["cache_k"].shape
    idd = inputs["cache_idx_k"].shape[-1]
    past = inputs["page_table"].shape[1] * page
    nbk, h = inputs["rel_bias"].shape
    poolw, state = inputs["pool_scale"].shape[1], inputs["state_pool"].shape[2]

    f32, p = np.float32, P
    give("c_ident", np.eye(p, dtype=f32))
    rows = np.arange(p)[:, None]
    causal = np.concatenate([np.arange(p)[None] > rows, np.arange(t_p)[None] > rows + p], axis=1)
    give("c_causal", np.where(causal, f32(NEG), f32(0)))
    give("c_causal_s", np.where(np.arange(t_s)[None] > (np.arange(b_s * t_s) % t_s)[:, None], f32(NEG), f32(0)))
    dist = np.maximum(past + t_s - 1 - np.arange(past + t_s + p), 0)
    exact = nbk // 2
    far = exact + (np.log(np.maximum(dist, 1).astype(f32) / f32(exact)) / f32(math.log(128 / exact))
                   * f32(nbk - exact)).astype(np.int32)
    bucket = np.where(dist < exact, dist, np.minimum(far, nbk - 1))
    give("c_onehot", (np.arange(nbk)[:, None] == bucket[None]).astype(f32))
    pos = np.arange(state + 1)
    count = np.stack([1.0 / np.minimum(pos + 1, w) for w in (2, 4, 8, 16)]).astype(f32)
    give("c_count", np.broadcast_to(count[None], (p,) + count.shape))
    k, m = np.arange(p)[None, :, None], np.arange(p)[None, None, :]
    pick = (k == np.arange(b_s)[:, None, None] * t_s + m % t_s)
    give("c_pick", pick.astype(ml_dtypes.bfloat16))

    shapes = [(1, t_p, d), (b_s, t_s, d), (depth, 1, t_p, g, hd), (depth, 1, t_p, g, hd), (depth, 1, t_p, idd),
              (depth, 1, state, poolw), (depth, b_s, t_s, g, hd), (depth, b_s, t_s, g, hd), (depth, b_s, t_s, idd),
              (depth, b_s, state, poolw)]
    out = [nc.dram_tensor(f"out_{i}", s, F32, kind="ExternalOutput").ap() for i, s in enumerate(shapes)]
    hybrid_layer(nc, t, out)
    r = _run(nc, [arrays], core_ids=[0])
    return tuple(r.results[0][f"out_{i}"] for i in range(len(shapes)))
```

```python
from contextlib import ExitStack

import numpy as np
import concourse.bass as bass
from concourse import mybir

F32 = mybir.dt.float32
F32R = mybir.dt.float32r
BF16 = mybir.dt.bfloat16
I32 = mybir.dt.int32
ALU = mybir.AluOpType
ACT = mybir.ActivationFunctionType
AX = mybir.AxisListType
ds = bass.ds

P = 128
SLOTS = 4
KK = 4
AHEAD_SPLIT = 3
AHEAD_LOAD = 7
NEG = -1e30
TAKEN = -3e38
TAKEN_EDGE = -2e38


def hybrid_layer(nc, t, out):
    _, T_P, D = t["x_prompt"].shape
    NB_S, T_S, _ = t["x_sample"].shape
    N_PHYS, PAGE, G, HD = t["cache_k"].shape[1:]
    PAGES = t["page_table"].shape[1]
    PAST = PAGES * PAGE
    NBK, H = t["rel_bias"].shape
    POOLW = t["pool_scale"].shape[1]
    STATE = t["state_pool"].shape[2]
    NG = t["w_pool"].shape[1]
    ID = t["cache_idx_k"].shape[-1]
    AW, KVW = H * HD, G * HD
    IH = (t["w_in"].shape[2] - 2 * AW - 2 * KVW - ID - 2 * POOLW) // (ID + 1)
    R = H // G
    N_S = NB_S * T_S
    N = T_P + N_S
    TT = [(0, P), (P, P), (T_P, N_S)]
    KT = D // P
    CH = KT // KK
    QC = 2 * CH
    LS = PAST + T_S
    TOPK_P, TOPK_S = min(256, T_P // 4), min(256, LS // 4)
    SCALE = float(HD) ** -0.5
    W_SCALE = float(ID * IH) ** -0.5
    EPS = 1e-6
    TQ = T_S * IH
    L2 = P + T_P
    NEG_AT = PAST + T_S - 1
    VEC = NEG_AT + P + 1
    WINS = (2, 4, 8, 16)
    UW = STATE + T_P + NB_S * (STATE + T_S)
    assert T_P == 2 * P and HD == P and ID == P and PAGE == P and R * T_S == 32 and CH == 8

    C_Q = 0
    C_GA = AW + 2 * KVW
    C_QI = C_GA + AW
    C_WI = C_QI + IH * ID
    C_KI = C_WI + IH
    C_U = C_KI + ID
    C_GB = C_U + POOLW
    W0 = IH + ID
    T_Q, T_K, T_V, T_GA = 0, AW // P, (AW + KVW) // P, C_GA // P
    T_QI = C_QI // P
    T_U = C_WI // P
    T_GB = T_U + POOLW // P
    N_TILES = T_GB + POOLW // P

    segs, chunk0, quad0 = {}, CH, 0
    for name, w, col, width, tile0 in (
            ("qi", "w_in", C_QI, IH * ID, T_QI), ("qkv", "w_in", C_Q + AW // 2, AW // 2 + 2 * KVW, T_Q + AW // 2 // P),
            ("q", "w_in", C_Q, AW // 2, T_Q),
            ("u", "w_in", C_U, POOLW, T_U), ("gb", "w_in", C_GB, POOLW, T_GB), ("ga", "w_in", C_GA, AW, T_GA),
            ("out", "w_out", 0, D, 0)):
        n = width // (4 * P)
        segs[name] = (w, col, n, chunk0, quad0, tile0)
        chunk0 += n * QC
        quad0 += n
    order = list(segs)

    w_rows = {n: t[n][0].rearrange("(k p) n -> p k n", p=P) for n in ("w_in", "w_out")}

    def dram(name, shape):
        return nc.dram_tensor(name, shape, F32).ap()

    projT = dram("projT", (N_TILES, P, N))
    oT = dram("oT", (H, P, N))
    poolT = dram("poolT", (POOLW // P, P, N))
    mixT = dram("mixT", (POOLW // P, P, N))
    wsc = dram("wsc", (1, N_S * IH))
    scores = dram("scores", (N_S, LS))
    BIAS_W = T_P + P
    biasP = dram("biasP", (H, P * BIAS_W))
    biasS = dram("biasS", (H, T_S * (LS + T_S)))

    def tile_rows(ap, i):
        return ap[ds(i, 1)].rearrange("a p n -> (a p) n")

    def tiles(ap, i, n):
        return ap[ds(i, n)].rearrange("a p n -> p a n")

    root = ExitStack()
    with root:
        names = set()

        def sem(name):
            assert name not in names
            names.add(name)
            return root.enter_context(nc.semaphore(name))

        def sb(name, shape, dt=F32, ctx=root):
            return ctx.enter_context(nc.sbuf_tensor(name, shape, dt))

        bank = [root.enter_context(nc.psum_tensor(f"bank{i}", [P, 512], F32)) for i in range(4)]
        wide = root.enter_context(nc.psum_tensor("wide", [P, 4 * 512], F32))
        sbank = [wide[:, 512 * i:512 * i + 512] for i in range(4)]

        XH = sb("XH", [P, KT, N], F32R)
        XL = sb("XL", [P, KT, N], F32R)
        raw = sb("raw", [P, SLOTS, KK, 2 * P])
        hi = sb("hi", [P, SLOTS, KK, 2 * P], F32R)
        lo = sb("lo", [P, SLOTS, KK, 2 * P], F32R)
        stg = [sb(f"stg{i}", [P, 2, N]) for i in range(2)]
        ident = sb("ident", [P, P])
        identb = sb("identb", [P, P], BF16)
        gT = sb("gT", [P, KT])
        poolscT = sb("poolscT", [P, POOLW // P])
        rstdB = sb("rstdB", [P, N])
        kiT = sb("kiT", [P, N])
        wN = sb("wN", [P, 3, IH])
        ptab = sb("ptab", [1, NB_S * PAGES], I32)
        keep = sb("keep", [P, G * N + (LS + 1) // 2 + L2 + L2 // 2 + 3 * KVW + POOLW // P * NB_S * STATE])
        at = [0]

        def cut(n, dt=F32, back=None):
            if back is not None:
                at[0] = back
            ap = keep[:, at[0]:at[0] + n]
            at[0] += n
            return ap if dt == F32 else ap.bitcast(dt)

        kT = cut(G * N).rearrange("p (g n) -> p g n", g=G)
        maskS = cut((LS + 1) // 2, BF16)
        era = at[0]
        scP = cut(L2)
        maskP = cut(L2 // 2, BF16)
        vN = cut(3 * KVW).rearrange("p (a n) -> p a n", a=3)
        stT = cut(POOLW // P * NB_S * STATE).rearrange("p (a n) -> p a n", a=POOLW // P)
        qS = cut(H * N_S, back=era).rearrange("p (h n) -> p h n", h=H)

        stood = {e: sem(f"stood_{e}") for e in ("Pool", "DVE", "SP", "PE")}

        def alone(eng):
            eng.sem_inc(stood[eng.engine.name], 1)

        raw_in = [sem(f"raw_in{i}") for i in range(SLOTS)]
        hi_ready, lo_ready, chunk_used = sem("hi_ready"), sem("lo_ready"), sem("chunk_used")
        evac = [sem("evac0"), sem("evac1")]
        stored = [sem("stored0"), sem("stored1")]

        def load_chunk(sp, c, slot, src, width, guard=True):
            if guard:
                sp.wait_ge(lo_ready, c - (SLOTS - 1))
                alone(sp)
            sp.dma_start(raw[:, slot, :, 0:width], src).then_inc(raw_in[slot], 16)

        def chunk_src(name, q, j):
            w, col = segs[name][:2]
            return w_rows[w][:, KK * (j % CH) if name != "out" else (KK * (j % CH) + KT // 2) % KT:, :][
                :, 0:KK, ds(q * (4 * P) + (col + (j // CH) * 2 * P), 2 * P)]

        def load_segment(sp, name, weave=None):
            _, _, n, c0, _, _ = segs[name]
            nxt = order[order.index(name) + 1] if name != "out" else None

            def quad(q, last):
                for j in range(QC):
                    k = j + AHEAD_LOAD
                    if k < QC:
                        src = chunk_src(name, q, k)
                    elif not last:
                        src = chunk_src(name, q + 1, k - QC)
                    elif nxt:
                        src = chunk_src(nxt, 0, k - QC)
                    else:
                        continue
                    load_chunk(sp, q * QC + (c0 + k), (c0 + k) % SLOTS, src, 2 * P)
                    if weave:
                        weave(sp, q, j)
            with sp.Fori(0, n - 1) as q:
                quad(q, False)
            quad(n - 1, True)

        def hi_chunk(act, c, slot, uses, width=2 * P, guard=True):
            act.wait_ge(raw_in[slot], uses)
            if guard:
                act.wait_ge(chunk_used, c - (SLOTS - 1))
            nc.scalar.activation(hi[:, slot, :, 0:width], raw[:, slot, :, 0:width], ACT.Copy).then_inc(hi_ready, 1)

        def lo_chunk(dve, c, slot, width=2 * P):
            dve.wait_ge(hi_ready, c + 1)
            nc.vector.tensor_tensor(lo[:, slot, :, 0:width], raw[:, slot, :, 0:width],
                                    hi[:, slot, :, 0:width].bitcast(F32), ALU.subtract).then_inc(lo_ready, 1)

        def products(pe, c, slot, j, banks, cols, rot=0):
            pe.wait_ge(lo_ready, c + 1)
            for kk in range(KK):
                k = (KK * j + kk + rot) % KT
                for n in range(2):
                    wh, wl = (w[:, slot, kk, cols[n]:cols[n] + P] for w in (hi, lo))
                    first, last = j == 0 and kk == 0, j == CH - 1 and kk == KK - 1
                    nc.tensor.matmul(bank[banks[n]][:, 0:N], wh, XH[:, k, :], start=first, stop=False)
                    nc.tensor.matmul(bank[banks[n]][:, 0:N], wh, XL[:, k, :], start=False, stop=False)
                    mm = nc.tensor.matmul(bank[banks[n]][:, 0:N], wl, XH[:, k, :], start=False, stop=last)
            mm.then_inc(chunk_used, 1)

        def pe_quad(pe, name, q, weave=None, before=None):
            _, _, _, c0, quad0, _ = segs[name]
            rot = KT // 2 if name == "out" else 0
            for j in range(QC):
                half = j // CH
                if j % CH == 0:
                    pe.wait_ge(evac[half], q + (quad0 + half))
                if before:
                    before(pe, j)
                products(pe, q * QC + (c0 + j), (c0 + j) % SLOTS, j % CH, (2 * half, 2 * half + 1), (0, P), rot)
                if weave:
                    weave(pe, q, j)

        def pe_segment(pe, name, weave=None):
            with pe.Fori(0, segs[name][2]) as q:
                pe_quad(pe, name, q, weave)

        def act_quad(act, name, q, weave=None, last=False, turned=None, gate=None, early=None):
            _, _, _, c0, quad0, tile0 = segs[name]
            for j in range(QC):
                k = j + AHEAD_SPLIT
                half = j // CH
                if not (last and k >= QC):
                    hi_chunk(act, q * QC + (c0 + k), (c0 + k) % SLOTS,
                             q * (QC // SLOTS * 16) + 16 * ((c0 + k) // SLOTS + 1))
                if early and j == QC - 1:
                    early(act)
                if j % CH == CH - 1 and turned is None:
                    act.wait_ge(evac[half], q + (quad0 + half + 1))
                    if gate:
                        ex, exped, _ = gate
                        nc.scalar.activation(ex, stg[half][:], ACT.Exp, scale=-1.0).then_inc(exped, 1)
                    else:
                        act.dma_start(tiles(projT, q * 4 + (tile0 + 2 * half), 2), stg[half][:]).then_inc(stored[half], 16)
                if weave:
                    weave(act, q, j)
                if gate and j % CH == CH - 1:
                    act.wait_ge(gate[2], q * 6 + (3 * half + 3))
                    act.dma_start(tiles(projT, q * 4 + (tile0 + 2 * half), 2), stg[half][:]).then_inc(stored[half], 16)

        def act_segment(act, name, weave=None, gate=None):
            with act.Fori(0, segs[name][2]) as q:
                act_quad(act, name, q, weave, gate=gate)

        def dve_quad(dve, name, q, weave=None, last=False, turned=None, gate=None):
            _, _, _, c0, quad0, _ = segs[name]
            for j in range(QC):
                k = j + AHEAD_SPLIT
                if not (last and k >= QC):
                    lo_chunk(dve, q * QC + (c0 + k), (c0 + k) % SLOTS)
                if j % CH == CH - 1:
                    half = j // CH
                    dve.wait_ge(chunk_used, q * QC + (c0 + j + 1))
                    if turned is None:
                        dve.wait_ge(stored[half], q * 16 + 16 * quad0)
                    else:
                        dve.wait_ge(stored[half], 16 * quad0)
                        dve.wait_ge(turned, q)
                    for n_ in range(2):
                        sums = bank[2 * half + n_][:, 0:N]
                        if turned is None:
                            copy = nc.vector.tensor_tensor(stg[half][:, n_, :], sums, rstdB[:], ALU.mult)
                        else:
                            copy = nc.vector.tensor_copy(stg[half][:, n_, :], sums)
                    copy.then_inc(evac[half], 1)
                if weave:
                    weave(dve, q, j)
                if gate and j % CH == CH - 1:
                    ex, exped, gated = gate
                    n = q * 6 + 3 * half
                    dve.wait_ge(exped, q * 2 + (half + 1))
                    nc.vector.tensor_scalar(ex, ex, 1.0, None, ALU.add).then_inc(gated, 1)
                    dve.wait_ge(gated, n + 1)
                    nc.vector.reciprocal(ex, ex).then_inc(gated, 1)
                    dve.wait_ge(gated, n + 2)
                    nc.vector.tensor_tensor(stg[half][:], stg[half][:], ex, ALU.mult).then_inc(gated, 1)

        def dve_segment(dve, name, weave=None, gate=None):
            with dve.Fori(0, segs[name][2]) as q:
                dve_quad(dve, name, q, weave, gate=gate)

        def all_stored(eng, name):
            for half in range(2):
                eng.wait_ge(stored[half], 16 * (segs[name][4] + segs[name][2]))

        with ExitStack() as ph:
            xN = [sb(f"xN{i}", [P, D], ctx=ph) for i in range(3)]
            ssq = sb("ssq", [P, 3], ctx=ph)
            var = sb("var", [P, 3], ctx=ph)
            rstd = sb("rstd", [P, 3], ctx=ph)
            root_ = sb("root_", [P, 3], ctx=ph)
            newt = sb("newt", [P, 3], ctx=ph)
            onehot = keep[0:NBK, D:D + VEC]
            relb = sb("relb", [NBK, H], ctx=ph)
            bvec = sb("bvec", [H, VEC], ctx=ph)
            s_step, s_bias = sem("s_step"), sem("s_bias")
            gN = sb("gN", [KT, P], ctx=ph)
            pscN = sb("pscN", [POOLW // P, P], ctx=ph)
            wiT = sb("wiT", [IH, N], ctx=ph)
            kiN = keep[:, 0:3 * P].rearrange("p (a n) -> p a n", a=3)
            ones = keep[:, D + VEC:D + VEC + P]
            diag = keep[:, D + VEC + P:D + VEC + 4 * P].rearrange("p (a n) -> p a n", a=3)
            XPARTS = 4
            XW = D // XPARTS
            s_x = [sem(f"s_x{i}") for i in range(XPARTS)]
            s_small, s_sq, s_root, s_rstd = (sem(n) for n in ("s_small", "s_sq", "s_root", "s_rstd"))
            s_gT, s_gcopy, s_xT, s_xh, s_xl = (sem(n) for n in ("s_gT", "s_gcopy", "s_xT", "s_xh", "s_xl"))
            s_diag, s_rb = sem("s_diag"), sem("s_rb")
            s_kin, s_kinc, s_bvec, s_bvecc, s_outA = (sem(n) for n in (
                "s_kin", "s_kinc", "s_bvec", "s_bvecc", "s_outA"))
            s_onehot = sem("s_onehot")
            SPLIT_AFTER = [(0, ), (1, 2), (3, 4), (5, 6)] + [(c + AHEAD_SPLIT, ) for c in range(4, CH)]
            SQUARES = range(3, 6)
            block = ph.enter_context(nc.Block())

            @block.sync
            def _(sp):
                sp.dma_start(ident[:], t["c_ident"]).then_inc(s_small, 16)
                sp.dma_start(gN[:], t["ln_g"][0].rearrange("(k p) -> k p", p=P)).then_inc(s_small, 16)
                sp.dma_start(pscN[:], t["pool_scale"][0].rearrange("(k p) -> k p", p=P)).then_inc(s_small, 16)
                sp.dma_start(relb[:], t["rel_bias"]).then_inc(s_onehot, 16)
                sp.dma_start(onehot, t["c_onehot"]).then_inc(s_onehot, 16)
                sp.wait_ge(s_x[0], 48)
                for c in range(AHEAD_LOAD):
                    load_chunk(sp, c, c % SLOTS, w_rows["w_in"][:, KK * c:KK * c + KK, C_WI:C_WI + W0], W0, c >= SLOTS)
                for c in range(AHEAD_LOAD, AHEAD_LOAD + CH):
                    if c < CH:
                        load_chunk(sp, c, c % SLOTS, w_rows["w_in"][:, KK * c:KK * c + KK, C_WI:C_WI + W0], W0)
                    else:
                        load_chunk(sp, c, c % SLOTS, chunk_src("qi", 0, c - CH), 2 * P)
                load_segment(sp, "qi")

            @block.gpsimd
            def _(pool):
                pool.dma_start(ptab[:], t["page_table"].rearrange("(o b) p -> o (b p)", o=1)).then_inc(s_outA, 16)
                pool.wait_ge(s_kinc, 1)
                pool.dma_start(out[4][0, 0].rearrange("(a p) d -> p a d", p=P), kiN[:, 0:2, :]).then_inc(s_outA, 16)
                pool.dma_start(out[8][0].rearrange("b s d -> (b s) d"), kiN[0:N_S, 2, :]).then_inc(s_outA, 16)
                pool.dma_start(wsc.rearrange("o (p h) -> (o p) h", h=IH), wN[0:N_S, 2, :]).then_inc(s_outA, 16)
                pool.wait_ge(s_bvecc, 1)
                pool.dma_start(biasP.rearrange("h (c n) -> h c n", n=BIAS_W),
                               bvec[:, VEC - BIAS_W:VEC].unsqueeze(1).to_broadcast([H, P, BIAS_W])).then_inc(s_bias, 16)
                pool.dma_start(biasS.rearrange("h (c n) -> h c n", n=LS + T_S),
                               bvec[:, 0:LS + T_S].unsqueeze(1).to_broadcast([H, T_S, LS + T_S])).then_inc(s_bias, 16)
                pool.wait_ge(s_bias, 32)
                pool.wait_ge(s_outA, 64)

            @block.scalar
            def _(act):
                rows = [t["x_prompt"][0, 0:P], t["x_prompt"][0, P:T_P], t["x_sample"].rearrange("b s d -> (b s) d")]
                for part in range(XPARTS):
                    for i in range(3):
                        cols = slice(part * XW, (part + 1) * XW)
                        act.dma_start(xN[i][0:TT[i][1], cols], rows[i][:, cols]).then_inc(s_x[part], 16)
                act.wait_ge(s_gcopy, 1)
                for c in range(CH):
                    for k in range(KK * c, KK * c + KK):
                        act.wait_ge(s_xT, k + 1)
                        nc.scalar.activation(XH[:, k, :], sbank[k % 4][:, 0:N], ACT.Copy,
                                             scale=gT[:, k:k + 1]).then_inc(s_xh, 1)
                    for a in SPLIT_AFTER[c]:
                        hi_chunk(act, a, a % SLOTS, 16 * (a // SLOTS + 1), W0 if a < CH else 2 * P, a >= SLOTS)
                    if c in SQUARES:
                        i = c - SQUARES[0]
                        r = TT[i][1]
                        for part in range(XPARTS):
                            act.wait_ge(s_x[part], 48)
                        act.wait_ge(s_step, 1)
                        if i:
                            act.wait_ge(s_sq, i)
                        nc.scalar.activation(keep[0:r, 0:D], xN[i][0:r, :], ACT.Square,
                                             accum_out=ssq[0:r, i:i + 1]).then_inc(s_sq, 1)
                    if c == SQUARES[-1] + 1:
                        act.wait_ge(s_step, 2)
                        nc.scalar.activation(root_[:], var[:], ACT.Sqrt).then_inc(s_root, 1)
                act_segment(act, "qi")

            @block.vector
            def _(dve):
                nc.vector.memset(ssq[:], 1.0).then_inc(s_step, 1)
                dve.wait_ge(s_bvec, 1)
                nc.vector.tensor_copy(bvec[:], wide[0:H, 512:512 + VEC]).then_inc(s_bvecc, 1)
                nc.vector.memset(ones, 1.0)
                dve.wait_ge(s_gT, 1)
                nc.vector.tensor_copy(gT[:], sbank[0][:, 0:KT])
                nc.vector.tensor_copy(identb[:], ident[:])
                nc.vector.tensor_copy(poolscT[:], sbank[0][:, KT:KT + POOLW // P]).then_inc(s_gcopy, 1)
                dve.wait_ge(s_gcopy, 1)
                for c in range(CH):
                    for k in range(KK * c, KK * c + KK):
                        dve.wait_ge(s_xh, k + 1)
                        nc.vector.scalar_tensor_tensor(XL[:, k, :], sbank[k % 4][:, 0:N], gT[:, k:k + 1],
                                                       XH[:, k, :].bitcast(F32), ALU.mult, ALU.subtract).then_inc(s_xl, 1)
                    for a in SPLIT_AFTER[c]:
                        lo_chunk(dve, a, a % SLOTS, W0 if a < CH else 2 * P)
                    if c == SQUARES[-1]:
                        dve.wait_ge(s_sq, 3)
                        nc.vector.tensor_scalar(var[:], ssq[:], 1.0 / D, EPS, ALU.mult, ALU.add).then_inc(s_step, 1)
                    if c == SQUARES[-1] + 1:
                        dve.wait_ge(s_root, 1)
                        nc.vector.reciprocal(root_[:], root_[:]).then_inc(s_step, 1)
                        dve.wait_ge(s_step, 3)
                        nc.vector.tensor_tensor(newt[:], root_[:], root_[:], ALU.mult).then_inc(s_step, 1)
                        dve.wait_ge(s_step, 4)
                        nc.vector.tensor_tensor(newt[:], newt[:], var[:], ALU.mult).then_inc(s_step, 1)
                        dve.wait_ge(s_step, 5)
                        nc.vector.tensor_scalar(newt[:], newt[:], -0.5, 1.5, ALU.mult, ALU.add).then_inc(s_step, 1)
                        dve.wait_ge(s_step, 6)
                        nc.vector.tensor_tensor(rstd[:], root_[:], newt[:], ALU.mult).then_inc(s_rstd, 1)
                        dve.wait_ge(s_rstd, 1)
                        for i, (_, r) in enumerate(TT):
                            ins = nc.vector.tensor_scalar(diag[0:r, i, 0:r], ident[0:r, 0:r], rstd[0:r, i:i + 1], None, ALU.mult)
                        ins.then_inc(s_diag, 1)
                dve.wait_ge(s_rb, 1)
                nc.vector.tensor_copy(rstdB[:], sbank[0][:, 0:N]).then_inc(s_rstd, 1)
                dve.wait_ge(s_rstd, 2)
                dve.wait_ge(chunk_used, CH)
                nc.vector.scalar_tensor_tensor(wiT[:], bank[2][0:IH, 0:N], W_SCALE, rstdB[0:IH, :], ALU.mult, ALU.mult)
                nc.vector.tensor_tensor(kiT[:], bank[3][:, 0:N], rstdB[:], ALU.mult).then_inc(evac[1], 1)
                dve.wait_ge(s_kin, 1)
                nc.vector.tensor_copy(wN[:, 0:2, :], sbank[0][:, 0:2 * IH].rearrange("p (a h) -> p a h", a=2))
                nc.vector.tensor_copy(wN[0:N_S, 2, :], sbank[0][0:N_S, 2 * IH:3 * IH])
                nc.vector.tensor_copy(kiN[:, 0:2, :], sbank[1][:, 0:2 * P].rearrange("p (a h) -> p a h", a=2))
                nc.vector.tensor_copy(kiN[0:N_S, 2, :], sbank[1][0:N_S, 2 * P:3 * P]).then_inc(s_kinc, 1)
                dve_segment(dve, "qi")

            @block.tensor
            def _(pe):
                pe.wait_ge(s_onehot, 32)
                for c in range(0, VEC, 512):
                    z = min(VEC, c + 512)
                    mm = nc.tensor.matmul(wide[0:H, 512 + c:512 + z], relb[:], onehot[:, c:z], start=True, stop=True)
                mm.then_inc(s_bvec, 1)
                pe.wait_ge(s_small, 48)
                nc.tensor.transpose(sbank[0][:, 0:KT], gN[:], ident[0:KT, 0:KT])
                nc.tensor.transpose(sbank[0][:, KT:KT + POOLW // P], pscN[:],
                                    ident[0:POOLW // P, 0:POOLW // P]).then_inc(s_gT, 1)
                pe.wait_ge(s_gcopy, 1)
                pe.wait_ge(s_bvecc, 1)

                def turn_tokens(c):
                    for k in range(KK * c, KK * c + KK):
                        pe.wait_ge(s_x[k * P // XW], 48)
                        if k >= 4:
                            pe.wait_ge(s_xl, k - 3)
                        for i, (c0, r) in enumerate(TT):
                            tr = nc.tensor.transpose(sbank[k % 4][:, c0:c0 + r], xN[i][0:r, k * P:k * P + P],
                                                     ident[0:r, 0:r])
                        tr.then_inc(s_xT, 1)

                turn_tokens(0)
                for c in range(CH):
                    if c + 1 < CH:
                        turn_tokens(c + 1)
                    else:
                        pe.wait_ge(s_diag, 1)
                        pe.wait_ge(s_xl, KT - 3)
                        for i, (c0, r) in enumerate(TT):
                            mm = nc.tensor.matmul(sbank[0][:, c0:c0 + r], ones[0:r, :], diag[0:r, i, 0:r], start=True, stop=True)
                        mm.then_inc(s_rb, 1)
                    pe.wait_ge(s_xl, KK * (c + 1))
                    products(pe, c, c % SLOTS, c, (2, 3), (0, IH))
                pe.wait_ge(evac[1], 1)
                for i, (c0, r) in enumerate(TT):
                    nc.tensor.transpose(sbank[0][0:r, i * IH:(i + 1) * IH], wiT[:, c0:c0 + r], ident[0:IH, 0:IH])
                for i, (c0, r) in enumerate(TT):
                    tr = nc.tensor.transpose(sbank[1][0:r, i * P:(i + 1) * P], kiT[:, c0:c0 + r], ident[:])
                tr.then_inc(s_kin, 1)
                pe_segment(pe, "qi")

        HQ = IH // segs["qkv"][2]
        BQ = NB_S // segs["qkv"][2]
        with ExitStack() as ph:
            qiH = [sb(f"qiH{i}", [P, HQ // 2, T_P], ctx=ph) for i in range(2)]
            qiS = sb("qiS", [P, IH, N_S], ctx=ph)
            wbc = sb("wbc", [P, N_S * IH], ctx=ph)
            ipg = sb("ipg", [P, PAGES, ID], ctx=ph)
            ikT = sb("ikT", [P, LS], ctx=ph)
            prod = sb("prod", [P, 2, TQ], ctx=ph)
            scT = sb("scT", [P, PAGES + 1, T_S], ctx=ph)
            sc8 = sb("sc8", [T_S, LS], ctx=ph)
            relu = sb("relu", [P, L2], ctx=ph)
            s_qiH = [sem("s_qiH0"), sem("s_qiH1")]
            (s_qiS, s_wbc, p_scored, p_relu, p_sum, s_ipg, s_itr, s_ikA, s_iks, s_sc, s_prod, s_red,
             s_bt, s_sc8, s_scst, s_zero) = (sem(n) for n in (
                 "s_qiS", "s_wbc", "p_scored", "p_relu", "p_sum", "s_ipg", "s_itr", "s_ikA", "s_iks",
                 "s_sc", "s_prod", "s_red", "s_bt", "s_sc8", "s_scst", "s_zero"))
            block = ph.enter_context(nc.Block())
            PAIRS = [(p, min(2, PAGES - p)) for p in range(0, PAGES, 2)] + [(PAGES, 1)]
            NPAIR = len(PAIRS)

            @block.sync
            def _(sp):
                load_segment(sp, "qkv")

            @block.gpsimd
            def _(pool):
                def index_pages(b):
                    pool.wait_ge(s_itr, b)
                    alone(pool)
                    for p in range(PAGES):
                        page = pool.value_load(ptab[0:1, ds(b * PAGES + p, 1)], min_val=0, max_val=N_PHYS - 1)
                        pool.dma_start(ipg[:, p, :], tile_rows(t["cache_idx_k"][0], page)).then_inc(s_ipg, 16)

                def store_scores(b):
                    pool.wait_ge(s_sc8, b + 1)
                    alone(pool)
                    pool.dma_start(scores[ds(b * T_S, T_S), :], sc8[:]).then_inc(s_scst, 16)

                def quad(q, more):
                    index_pages(q * BQ + 1)
                    if more:
                        pool.wait_ge(p_scored, q * HQ + HQ // 2)
                        alone(pool)
                        load_heads(q + 1, 0)
                    store_scores(q * BQ)
                    if more:
                        index_pages(q * BQ + 2)
                        pool.wait_ge(p_scored, q * HQ + HQ)
                        alone(pool)
                        load_heads(q + 1, 1)
                    if more:
                        store_scores(q * BQ + 1)

                def load_heads(q, i):
                    pool.dma_start(qiH[i][:], projT[ds(q * HQ + (T_QI + i * (HQ // 2)), HQ // 2), :, 0:T_P].rearrange(
                        "h p n -> p h n")).then_inc(s_qiH[i], 16)

                for half in range(2):
                    pool.wait_ge(stored[half], 16 * (segs["qi"][4] + 1))
                load_heads(0, 0)
                index_pages(0)
                all_stored(pool, "qi")
                pool.dma_start(qiS[:], projT[T_QI:T_QI + IH, :, T_P:N].rearrange("h p n -> p h n")).then_inc(s_qiS, 16)
                pool.dma_start(wbc[:], wsc.to_broadcast([P, N_S * IH])).then_inc(s_wbc, 16)
                load_heads(0, 1)
                NQ = segs["qkv"][2]
                with pool.Fori(0, NQ - 1) as q:
                    quad(q, True)
                quad(NQ - 1, False)

            def pe_weave(pe, q, j):
                if j % 2 == 1:
                    h = j // 2
                    part = h // (HQ // 2)
                    if h % (HQ // 2) == 0:
                        pe.wait_ge(s_qiH[part], q * 16 + 16)
                    pe.wait_ge(p_relu, q * HQ + h)
                    nc.tensor.matmul(sbank[0][:, 0:P], qiH[part][:, h % (HQ // 2), 0:P], kiT[:, 0:P], start=True, stop=True)
                    nc.tensor.matmul(sbank[0][:, P:L2], qiH[part][:, h % (HQ // 2), P:T_P], kiT[:, 0:T_P], start=True,
                                     stop=True).then_inc(p_scored, 1)
                u, s = j // 8, j % 8
                b = q * BQ + u
                if s == 1:
                    pe.wait_ge(s_ipg, b * (16 * PAGES) + 16 * PAGES)
                    pe.wait_ge(s_sc8, b)
                    for p in range(PAGES):
                        tr = nc.tensor.transpose(sbank[1 + p // 4][:, (p % 4) * P:(p % 4 + 1) * P], ipg[:, p, :], ident[:])
                    tr.then_inc(s_itr, 1)
                for i, (p, n) in enumerate(PAIRS):
                    if s != 3 + i // 2:
                        continue
                    if i == 0:
                        pe.wait_ge(s_ikA, b + 1)
                        pe.wait_ge(s_iks, b + 1)
                    if i >= 2:
                        pe.wait_ge(s_prod, b * NPAIR + (i - 1))
                    pe.wait_ge(s_qiS, 16)
                    alone(pe)
                    for m in range(n):
                        cols = P if p < PAGES else T_S
                        mm = nc.tensor.matmul(sbank[1 + i % 2][0:cols, m * TQ:(m + 1) * TQ],
                                              ikT[:, (p + m) * P:(p + m) * P + cols],
                                              qiS[:, :, ds(b * T_S, T_S)].rearrange("p h t -> p t h"),
                                              start=True, stop=True)
                    mm.then_inc(s_sc, 1)
                if s == 7:
                    pe.wait_ge(s_red, b * NPAIR + NPAIR)
                    for p in range(PAGES):
                        nc.tensor.transpose(wide[0:T_S, 512 + p * P:512 + (p + 1) * P], scT[:, p, :], ident[:])
                    nc.tensor.transpose(wide[0:T_S, 512 + PAST:512 + LS], scT[0:T_S, PAGES, :],
                                        ident[0:T_S, 0:T_S]).then_inc(s_bt, 1)

            def act_weave(act, q, j):
                if j % 2 == 1:
                    h = j // 2
                    act.wait_ge(p_scored, q * HQ + (h + 1))
                    act.wait_ge(p_sum, q * HQ + h)
                    nc.scalar.activation(relu[:], sbank[0][:, 0:L2], ACT.Relu).then_inc(p_relu, 1)
                u, s = j // 8, j % 8
                b = q * BQ + u
                if s == 1:
                    act.wait_ge(s_itr, b + 1)
                    act.wait_ge(s_sc, b * NPAIR)
                    nc.scalar.activation(ikT[:, 0:PAST], wide[:, 512:512 + PAST], ACT.Copy).then_inc(s_ikA, 1)

            def dve_weave(dve, q, j):
                u, s = j // 8, j % 8
                b = q * BQ + u
                if s == 1:
                    dve.wait_ge(s_sc, b * NPAIR)
                    nc.vector.tensor_copy(ikT[:, PAST:LS], kiT[:, ds(b * T_S + T_P, T_S)]).then_inc(s_iks, 1)
                if j % 2 == 1:
                    h = q * HQ + j // 2
                    dve.wait_ge(p_relu, h + 1)
                    dve.wait_ge(p_sum, h)
                    for i, (a, z) in enumerate(((0, P), (P, L2))):
                        ins = nc.vector.scalar_tensor_tensor(scP[:, a:z], relu[:, a:z], wN[:, i, ds(h, 1)], scP[:, a:z],
                                                             ALU.mult, ALU.add)
                    ins.then_inc(p_sum, 1)
                for i, (p, n) in enumerate(PAIRS):
                    if s != 3 + i // 2:
                        continue
                    cols = P if p < PAGES else T_S
                    dve.wait_ge(s_sc, b * NPAIR + (i + 1))
                    dve.wait_ge(s_red, b * NPAIR + i)
                    if i == 0:
                        dve.wait_ge(s_wbc, 16)
                        dve.wait_ge(s_bt, b)
                    nc.vector.scalar_tensor_tensor(
                        prod[0:cols, 0:n, :], sbank[1 + i % 2][0:cols, 0:n * TQ].rearrange("p (a c) -> p a c", a=n), 0.0,
                        wbc[0:cols, ds(b * TQ, TQ)].unsqueeze(1).to_broadcast([cols, n, TQ]),
                        ALU.max, ALU.mult).then_inc(s_prod, 1)
                    dve.wait_ge(s_prod, b * NPAIR + (i + 1))
                    nc.vector.tensor_reduce(scT[0:cols, p:p + n, :].rearrange("p a t -> p (a t)"),
                                            prod[0:cols, 0:n, :].rearrange("p a (t h) -> p (a t) h", h=IH),
                                            AX.X, ALU.add).then_inc(s_red, 1)
                if s == 7:
                    dve.wait_ge(s_bt, b + 1)
                    dve.wait_ge(s_scst, b * 16)
                    nc.vector.tensor_copy(sc8[:], wide[0:T_S, 512:512 + LS]).then_inc(s_sc8, 1)

            @block.scalar
            def _(act):
                act.wait_ge(s_zero, 1)
                act_segment(act, "qkv", act_weave)

            @block.vector
            def _(dve):
                nc.vector.memset(scP, 0.0).then_inc(s_zero, 1)
                dve.wait_ge(s_zero, 1)
                dve_segment(dve, "qkv", dve_weave)

            @block.tensor
            def _(pe):
                pe_segment(pe, "qkv", pe_weave)

        with ExitStack() as ph:
            vT = sb("vT", [P, G, N], ctx=ph)
            kN = sb("kN", [P, 3, KVW], ctx=ph)
            negP = sb("negP", [P, L2], ctx=ph)
            top8 = sb("top8", [P, 2, 8], ctx=ph)
            keepP = sb("keepP", [P, L2], ctx=ph)
            stN = sb("stN", [NB_S * STATE, POOLW], ctx=ph)
            s_cin, t_step, s_kvT, s_kvt, s_kvc, s_outC, s_stt = (sem(n) for n in (
                "s_cin", "t_step", "s_kvT", "s_kvt", "s_kvc", "s_outC", "s_stt"))
            block = ph.enter_context(nc.Block())
            NQ = segs["q"][2]
            ROUNDS = TOPK_P // 8
            RQ = ROUNDS // NQ
            FILLS = [(src, i) for src in (0, 1) for i in range(3)]
            ST_FILLS = POOLW // P // 4
            assert NQ == 2 and len(FILLS) == QC // 2 - 2 and ST_FILLS == 4

            @block.sync
            def _(sp):
                load_segment(sp, "q")

            @block.gpsimd
            def _(pool):
                pool.wait_ge(s_sc8, NB_S)
                pool.dma_start(scores[(NB_S - 1) * T_S:NB_S * T_S, :], sc8[:]).then_inc(s_scst, 16)
                pool.dma_start(negP[:], t["c_causal"]).then_inc(s_cin, 16)
                pool.dma_start(stN[:], t["state_pool"][0].rearrange("b s c -> (b s) c")).then_inc(s_cin, 16)
                all_stored(pool, "qkv")
                pool.dma_start(kT, tiles(projT, T_K, G)).then_inc(s_kvT, 16)
                pool.dma_start(vT[:], tiles(projT, T_V, G)).then_inc(s_kvT, 16)
                pool.wait_ge(s_kvc, len(FILLS))
                for o, src in ((2, kN), (3, vN)):
                    pool.dma_start(out[o][0, 0].rearrange("(a p) g d -> p a (g d)", p=P), src[:, 0:2, :]).then_inc(s_outC, 16)
                    pool.dma_start(out[o + 4][0].rearrange("b s g d -> (b s) (g d)"), src[0:N_S, 2, :]).then_inc(s_outC, 16)
                pool.wait_ge(s_outC, 64)
                pool.wait_ge(s_scst, 16 * NB_S)

            def turning(q, j):
                if j % 2 or not 2 <= j < QC:
                    return None, None
                if q == 0:
                    return (j - 4) // 2 if j >= 4 else None, None
                return None, (j - 2) // 2 if j < 2 + 2 * ST_FILLS else None

            def pe_weave(pe, q, j):
                f, st = turning(q, j)
                if f is not None:
                    src, i = FILLS[f]
                    c0, r = TT[i]
                    pe.wait_ge(s_kvT, 32)
                    if f >= 4:
                        pe.wait_ge(s_kvc, f - 3)
                    for g in range(G):
                        tr = nc.tensor.transpose(sbank[f % 4][0:r, g * P:(g + 1) * P], (kT, vT)[src][:, g, c0:c0 + r], ident[:])
                    tr.then_inc(s_kvt, 1)
                if st is not None:
                    pe.wait_ge(s_cin, 32)
                    pe.wait_ge(s_kvc, len(FILLS))
                    for a in range(4):
                        tr = nc.tensor.transpose(sbank[st][:, a * NB_S * STATE:(a + 1) * NB_S * STATE],
                                                 stN[:, (4 * st + a) * P:(4 * st + a + 1) * P],
                                                 ident[0:NB_S * STATE, 0:NB_S * STATE])
                    tr.then_inc(s_stt, 1)

            def act_weave(act, q, j):
                f, st = turning(q, j)
                if f is not None:
                    src, i = FILLS[f]
                    r = TT[i][1]
                    act.wait_ge(s_kvt, f + 1)
                    nc.scalar.activation((kN, vN)[src][0:r, i, :], sbank[f % 4][0:r, 0:KVW], ACT.Copy).then_inc(s_kvc, 1)
                if st is not None:
                    act.wait_ge(s_stt, st + 1)
                    nc.scalar.activation(stT[:, 4 * st:4 * st + 4, :], sbank[st][:, 0:4 * NB_S * STATE].rearrange(
                        "p (a n) -> p a n", a=4), ACT.Copy)

            def dve_weave(dve, q, j):
                per = QC // RQ
                r, s = j // per, j % per
                base = q * (4 * RQ) + 4 * r
                for i, (a, z) in enumerate(((0, P), (P, L2))):
                    if s == 2 * i:
                        dve.wait_ge(t_step, base + (2 * i + 1))
                        alone(dve)
                        nc.vector.max(top8[:, i, :], scP[:, a:z]).then_inc(t_step, 1)
                    if s == 2 * i + 1:
                        dve.wait_ge(t_step, base + (2 * i + 2))
                        alone(dve)
                        nc.vector.match_replace(scP[:, a:z], top8[:, i, :], scP[:, a:z], TAKEN).then_inc(t_step, 1)

            @block.scalar
            def _(act):
                for q in range(NQ):
                    act_quad(act, "q", q, act_weave)

            @block.vector
            def _(dve):
                dve.wait_ge(s_cin, 32)
                nc.vector.tensor_tensor(scP, scP, negP[:], ALU.add).then_inc(t_step, 1)
                dve_segment(dve, "q", dve_weave)
                steps = 4 * ROUNDS + 1
                dve.wait_ge(t_step, steps)
                nc.vector.tensor_scalar(keepP[:], scP, TAKEN_EDGE, NEG, ALU.is_ge, ALU.mult).then_inc(t_step, 1)
                dve.wait_ge(t_step, steps + 1)
                nc.vector.tensor_tensor(maskP, keepP[:], negP[:], ALU.min).then_inc(t_step, 1)

            @block.tensor
            def _(pe):
                for q in range(NQ):
                    pe_quad(pe, "q", q, pe_weave)

        with ExitStack() as ph:
            qh = sb("qh", [P, T_P], ctx=ph)
            relh = sb("relh", [P, L2], ctx=ph)
            lg = sb("lg", [P, L2], ctx=ph)
            pT = sb("pT", [P, L2], ctx=ph)
            ohT = sb("ohT", [P, T_P], ctx=ph)
            nmx = sb("nmx", [P, 2], ctx=ph)
            rs = sb("rs", [P, 2], ctx=ph)
            ri = sb("ri", [P, 2], ctx=ph)
            scS = sb("scS", [N_S, LS], ctx=ph)
            negS = sb("negS", [N_S, T_S], ctx=ph)
            tops = sb("tops", [N_S, 8], ctx=ph)
            uin = sb("uin", [P, 4, N], ctx=ph)
            ubuf = [sb(f"ubuf{i}", [P, 4, UW], ctx=ph) for i in range(3)]
            cntr = sb("cntr", [P, NG, STATE + 1], ctx=ph)
            fix = sb("fix", [P, 4, STATE + 1], ctx=ph)
            dl = sb("dl", [P, 4, N], ctx=ph)
            wp = sb("wp", [P, 4, 4 * P], ctx=ph)
            obuf = sb("obuf", [P, 4, N], ctx=ph)
            ut = ubuf[0][:].rearrange("p a n -> p (a n)")[:, 0:4 * P].rearrange("p (a n) -> p a n", a=4)
            utN = ubuf[1][:].rearrange("p a n -> p (a n)")[:, 0:4 * P]
            gex = keep[:, G * N:G * N + 2 * N].rearrange("p (a n) -> p a n", a=2)
            gated_b, exped_b = sem("gated_b"), sem("exped_b")
            ut_in, ut_t, ut_c, ut_out, u_old = (sem(n) for n in ("ut_in", "ut_t", "ut_c", "ut_out", "u_old"))
            (d_in, a_q, a_rel, a_s, a_lg, a_mx, a_exp, a_ri, a_pr, a_pt, a_ptc, a_pv, a_oh, a_st, ts_step, ts_fin,
             u_in, u_step, u_st, w_in_, w_pe, w_ev, w_st) = (sem(n) for n in (
                 "d_in", "a_q", "a_rel", "a_s", "a_lg", "a_mx", "a_exp", "a_ri", "a_pr", "a_pt", "a_ptc", "a_pv", "a_oh",
                 "a_st", "ts_step", "ts_fin", "u_in", "u_step", "u_st", "w_in_", "w_pe", "w_ev", "w_st"))
            block = ph.enter_context(nc.Block())
            NQ = segs["u"][2]
            HPQ = H // (2 * NQ)
            ROUNDS = TOPK_S // 8
            RQ = ROUNDS // (2 * NQ)
            assert HPQ == 2 and NQ == R and NG == NQ and G == 4

            def tail_tokens(sp, q, j):
                if j != 14:
                    return
                sp.wait_ge(ut_c, q + 1)
                alone(sp)
                first, cols = P - N_S - STATE, ds(q * (4 * P), 4 * P)
                sp.dma_start(out[5][0, 0][:, cols], utN[first:first + STATE, :]).then_inc(ut_out, 16)
                for b in range(NB_S):
                    r0 = P - N_S + b * T_S
                    sp.dma_start(out[9][0, b, STATE - T_S:STATE][:, cols], utN[r0:r0 + T_S, :]).then_inc(ut_out, 16)

            @block.sync
            def _(sp):
                load_segment(sp, "u")
                load_segment(sp, "gb", tail_tokens)

            def head_number(half, q, u):
                return q * HPQ + (half * NQ * HPQ + u)

            def head_load(pool, half, q, u):
                h, n = q + (2 * half + u) * R, head_number(half, q, u)
                pool.wait_ge(a_s, n)
                alone(pool)
                pool.dma_start(qh[:], tile_rows(projT, h)[:, 0:T_P]).then_inc(a_q, 16)
                pool.wait_ge(a_lg, n)
                alone(pool)
                bias = biasP[ds(h, 1), P - 1:P - 1 + P * (BIAS_W - 1)].rearrange("o (a n) -> (o a) n", n=BIAS_W - 1)
                pool.dma_start(relh[:, P:L2], bias[:, 0:T_P]).then_inc(a_rel, 16)
                pool.dma_start(relh[:, 0:P], bias[:, P:T_P]).then_inc(a_rel, 16)

            def head_store(pool, half, q, u):
                h, n = q + (2 * half + u) * R, head_number(half, q, u)
                pool.wait_ge(a_oh, n + 1)
                alone(pool)
                pool.dma_start(tile_rows(oT, h)[:, 0:T_P], ohT[:]).then_inc(a_st, 16)

            U_STEPS = [0]

            def pool_steps(pool, g, between=None):
                win = WINS[g]
                base = sum(U_STEPS)
                n_ = [base]

                def done(ins):
                    n_[0] += 1
                    ins.then_inc(u_step, 1)
                    pool.wait_ge(u_step, n_[0])

                pool.wait_ge(stored[0], 16 * (segs["u"][4] + g + 1))
                pool.wait_ge(stored[1], 16 * (segs["u"][4] + g + 1))
                pool.dma_start(uin[:], tiles(projT, T_U + 4 * g, 4)).then_inc(u_in, 16)
                pool.wait_ge(u_in, 16 * (g + 1))
                U, A, B = ubuf
                if g:
                    pool.wait_ge(u_st, 16 * g)
                nc.gpsimd.memset(U[:, :, 0:STATE], 0.0)
                nc.gpsimd.tensor_copy(U[:, :, STATE:STATE + T_P], uin[:, :, 0:T_P])
                for a in range(4):
                    rows = U[:, a, STATE + T_P:UW].rearrange("p (b n) -> p b n", b=NB_S)
                    nc.gpsimd.tensor_copy(rows[:, :, 0:STATE], stT[:, 4 * g + a, :].rearrange("p (b n) -> p b n", b=NB_S))
                    ins = nc.gpsimd.tensor_copy(rows[:, :, STATE:], uin[:, a, T_P:N].rearrange("p (b n) -> p b n", b=NB_S))
                done(ins)
                src, w, lost = U, 1, 0
                while w < win:
                    dst = A if src is not A else B
                    done(nc.gpsimd.tensor_tensor(dst[:, :, lost + w:UW], src[:, :, lost + w:UW], src[:, :, lost:UW - w], ALU.add))
                    src, lost, w = dst, lost + w, 2 * w
                if between:
                    between()
                other = A if src is B else B
                done(nc.gpsimd.tensor_tensor(fix[:, :, 0:STATE], src[:, :, STATE:2 * STATE],
                                             cntr[:, g:g + 1, 0:STATE].to_broadcast([P, 4, STATE]), ALU.mult))
                done(nc.gpsimd.tensor_scalar(other[:, :, STATE:UW], src[:, :, STATE:UW], 1.0 / win, None, ALU.mult))
                dp = src[:].rearrange("p a n -> p (a n)")[:, 0:4 * N].rearrange("p (a n) -> p a n", a=4)
                nc.gpsimd.tensor_tensor(dp[:, :, 0:STATE], fix[:, :, 0:STATE], U[:, :, STATE:2 * STATE], ALU.subtract)
                ins = nc.gpsimd.tensor_tensor(dp[:, :, STATE:T_P], other[:, :, 2 * STATE:STATE + T_P],
                                              U[:, :, 2 * STATE:STATE + T_P], ALU.subtract)
                for a in range(4):
                    m_, u_ = (x[:, a, STATE + T_P:UW].rearrange("p (b n) -> p b n", b=NB_S)[:, :, STATE:] for x in (other, U))
                    ins = nc.gpsimd.tensor_tensor(dp[:, a, T_P:N].rearrange("p (b n) -> p b n", b=NB_S), m_, u_, ALU.subtract)
                done(ins)
                pool.dma_start(tiles(poolT, 4 * g, 4), dp).then_inc(u_st, 16)
                U_STEPS.append(n_[0] - base)

            @block.gpsimd
            def _(pool):
                pool.dma_start(scS[:], scores).then_inc(d_in, 16)
                pool.dma_start(negS[:], t["c_causal_s"]).then_inc(d_in, 16)
                pool.dma_start(cntr[:], t["c_count"]).then_inc(d_in, 16)
                pool.wait_ge(d_in, 48)
                for half in range(2):
                    pool.wait_ge(stored[half], 16 * (segs["q"][4] + 1))
                head_load(pool, 0, 0, 0)
                all_stored(pool, "q")
                pool.dma_start(out[9][0, :, 0:STATE - T_S, :], t["state_pool"][0, :, T_S:STATE, :]).then_inc(u_old, 16)
                for q in range(NQ):
                    head_load(pool, 0, q, 1)
                    if q:
                        pool_steps(pool, q - 1)
                    head_store(pool, 0, q, 0)
                    if q + 1 < NQ:
                        head_load(pool, 0, q + 1, 0)
                    else:
                        head_load(pool, 1, 0, 0)
                    head_store(pool, 0, q, 1)

                def group_load(q):
                    pool.wait_ge(w_pe, q * 4)
                    pool.wait_ge(u_st, q * 16 + 16)
                    alone(pool)
                    pool.dma_start(wp[:], t["w_pool"][0, ds(q, 1)].rearrange("g (a p) d -> p (g a) d", p=P)).then_inc(w_in_, 16)
                    pool.dma_start(dl[:], tiles(poolT, q * 4, 4)).then_inc(w_in_, 16)

                def group_store(q):
                    pool.wait_ge(w_ev, q * 4 + 4)
                    alone(pool)
                    pool.dma_start(tiles(mixT, q * 4, 4), obuf[:]).then_inc(w_st, 16)

                group_load(0)
                pool_steps(pool, NQ - 1, lambda: head_load(pool, 1, 0, 1))
                pool.wait_ge(u_st, 16 * NG)

                def gate_quad(q, more):
                    pool.dma_start(ut, projT[ds(q * 4 + T_U, 4), :, N - P:N].rearrange("a p n -> p a n")).then_inc(ut_in, 16)
                    head_store(pool, 1, q, 0)
                    if more:
                        head_load(pool, 1, q + 1, 0)
                    head_store(pool, 1, q, 1)
                    if more:
                        group_load(q + 1)
                    group_store(q)
                    if more:
                        head_load(pool, 1, q + 1, 1)
                with pool.Fori(0, NQ - 1) as q:
                    gate_quad(q, True)
                gate_quad(NQ - 1, False)

            def pe_weave(half):
                def weave(pe, q, j):
                    u, s = j // 8, j % 8
                    g = 2 * half + u
                    n = q * HPQ + (half * NQ * HPQ + u)
                    if s == 1:
                        pe.wait_ge(a_q, n * 16 + 16)
                        pe.wait_ge(a_lg, n)
                        nc.tensor.matmul(sbank[0][:, 0:L2], identb[:], maskP, start=True, stop=False)
                        nc.tensor.matmul(sbank[0][:, 0:P], qh[:, 0:P], kT[:, g, 0:P], start=False, stop=False)
                        nc.tensor.matmul(sbank[0][:, P:L2], qh[:, P:T_P], kT[:, g, 0:T_P], start=False,
                                         stop=True).then_inc(a_s, 1)
                    if s == 4:
                        pe.wait_ge(a_pr, n + 1)
                        pe.wait_ge(a_ptc, n)
                        for i in range(3):
                            tr = nc.tensor.transpose(sbank[1][:, i * P:(i + 1) * P], lg[:, i * P:(i + 1) * P], ident[:])
                        tr.then_inc(a_pt, 1)
                    if s == 6:
                        pe.wait_ge(a_ptc, n + 1)
                        pe.wait_ge(a_oh, n)
                        gv = slice(g * P, (g + 1) * P)
                        nc.tensor.matmul(sbank[2][:, 0:P], vN[:, 0, gv], pT[:, 0:P], start=True, stop=True)
                        nc.tensor.matmul(sbank[2][:, P:T_P], vN[:, 0, gv], pT[:, P:2 * P], start=True, stop=False)
                        nc.tensor.matmul(sbank[2][:, P:T_P], vN[:, 1, gv], pT[:, 2 * P:L2], start=False,
                                         stop=True).then_inc(a_pv, 1)
                    if half and j % 4 == 3:
                        dt = j // 4
                        if dt == 0:
                            pe.wait_ge(w_in_, q * 32 + 32)
                        pe.wait_ge(w_ev, q * 4 + dt)
                        if dt == 3:
                            pe.wait_ge(ut_c, q + 1)
                        for a in range(4):
                            mm = nc.tensor.matmul(sbank[3][:, 0:N], wp[:, a, dt * P:(dt + 1) * P], dl[:, a, :],
                                                  start=a == 0, stop=a == 3)
                        mm.then_inc(w_pe, 1)
                    if half and j == 13:
                        pe.wait_ge(ut_in, q * 16 + 16)
                        pe.wait_ge(w_ev, q * 4 + 3)
                        for a in range(4):
                            tr = nc.tensor.transpose(sbank[3][:, a * P:(a + 1) * P], ut[:, a, :], ident[:])
                        tr.then_inc(ut_t, 1)
                return weave

            def act_weave(half):
                def weave(act, q, j):
                    u, s = j // 8, j % 8
                    n = q * HPQ + (half * NQ * HPQ + u)
                    if s == 2:
                        act.wait_ge(a_mx, n + 1)
                        for i, (a, z) in enumerate(((0, P), (P, L2))):
                            ins = nc.scalar.activation(lg[:, a:z], lg[:, a:z], ACT.Exp, bias=nmx[:, i:i + 1],
                                                       accum_out=rs[:, i:i + 1])
                        ins.then_inc(a_exp, 1)
                    if s == 4:
                        act.wait_ge(a_pt, n + 1)
                        act.wait_ge(a_pv, n)
                        nc.scalar.activation(pT[:], sbank[1][:, 0:L2], ACT.Copy).then_inc(a_ptc, 1)
                    if s == 6:
                        act.wait_ge(a_pv, n + 1)
                        act.wait_ge(a_st, n * 16)
                        nc.scalar.activation(ohT[:], sbank[2][:, 0:T_P], ACT.Copy).then_inc(a_oh, 1)
                return weave

            def dve_weave(half):
                def weave(dve, q, j):
                    u, s = j // 8, j % 8
                    n = q * HPQ + (half * NQ * HPQ + u)
                    if s == 1:
                        dve.wait_ge(a_s, n + 1)
                        dve.wait_ge(a_rel, n * 32 + 32)
                        dve.wait_ge(a_pt, n)
                        nc.vector.scalar_tensor_tensor(lg[:], sbank[0][:, 0:L2], SCALE, relh[:], ALU.mult,
                                                       ALU.add).then_inc(a_lg, 1)
                        dve.wait_ge(a_lg, n + 1)
                        for i, (a, z) in enumerate(((0, P), (P, L2))):
                            ins = nc.vector.tensor_reduce(nmx[:, i:i + 1], lg[:, a:z], AX.X, ALU.max, negate=True)
                        ins.then_inc(a_mx, 1)
                    if s == 3:
                        dve.wait_ge(a_exp, n + 1)
                        nc.vector.reciprocal(ri[:], rs[:]).then_inc(a_ri, 1)
                        dve.wait_ge(a_ri, n + 1)
                        for i, (a, z) in enumerate(((0, P), (P, L2))):
                            ins = nc.vector.tensor_scalar(lg[:, a:z], lg[:, a:z], ri[:, i:i + 1], None, ALU.mult)
                        ins.then_inc(a_pr, 1)
                    if half and j % 4 == 3:
                        dt = j // 4
                        dve.wait_ge(w_pe, q * 4 + (dt + 1))
                        if dt == 0:
                            dve.wait_ge(w_st, q * 16)
                        nc.vector.tensor_scalar(obuf[:, dt, :], sbank[3][:, 0:N], poolscT[:, ds(q * 4 + dt, 1)], None,
                                                ALU.mult).then_inc(w_ev, 1)
                    if half and j == 13:
                        dve.wait_ge(ut_t, q + 1)
                        dve.wait_ge(ut_out, q * (16 * (NB_S + 1)))
                        nc.vector.tensor_copy(utN, sbank[3]).then_inc(ut_c, 1)
                    if j % (QC // RQ) in (0, 2):
                        k = (q + half * NQ) * (2 * RQ) + (2 * (j // (QC // RQ)) + (j % (QC // RQ)) // 2)
                        dve.wait_ge(ts_step, k + 1)
                        alone(dve)
                        if j % (QC // RQ) == 0:
                            nc.vector.max(tops[:], scS[:]).then_inc(ts_step, 1)
                        else:
                            nc.vector.match_replace(scS[:], tops[:], scS[:], TAKEN).then_inc(ts_step, 1)
                return weave

            @block.scalar
            def _(act):
                act_segment(act, "u", act_weave(0))
                act_segment(act, "gb", act_weave(1), gate=(gex, exped_b, gated_b))

            @block.vector
            def _(dve):
                dve.wait_ge(d_in, 48)
                nc.vector.tensor_tensor(scS[:, PAST:LS], scS[:, PAST:LS], negS[:], ALU.add).then_inc(ts_step, 1)
                dve_segment(dve, "u", dve_weave(0))
                dve_segment(dve, "gb", dve_weave(1), gate=(gex, exped_b, gated_b))
                dve.wait_ge(gated_b, 6 * NQ)
                nc.vector.memset(maskS, 0.0).then_inc(ts_fin, 1)
                dve.wait_ge(ts_step, 2 * ROUNDS + 1)
                dve.wait_ge(ts_fin, 1)
                nc.vector.tensor_scalar(maskS[0:N_S, :], scS[:], TAKEN_EDGE, NEG, ALU.is_ge, ALU.mult).then_inc(ts_fin, 1)

            @block.tensor
            def _(pe):
                pe_segment(pe, "u", pe_weave(0))
                pe_segment(pe, "gb", pe_weave(1))

        with ExitStack() as ph:
            KEPT = 5
            after_qS = era + H * N_S
            DECK = PAGES * KVW + (PAGES - KEPT) * KVW + G * LS + KVW + 2 * LS + (PAGES + 1) * P + P // 2
            deck = sb("deck", [P, DECK], ctx=ph)
            assert DECK >= 3 * D + 8 * P
            at[0] = 0

            def deal(n, rows=P):
                at[0] += n
                return deck[0:rows, at[0] - n:at[0]]

            kpg = deal(PAGES * KVW).rearrange("p (a n) -> p a n", a=PAGES)
            vpg_own = deal((PAGES - KEPT) * KVW).rearrange("p (a n) -> p a n", a=PAGES - KEPT)
            vpg = [keep[:, after_qS + p * KVW:after_qS + (p + 1) * KVW] for p in range(KEPT)] + [
                vpg_own[:, p, :] for p in range(PAGES - KEPT)]
            KTs = deal(G * LS).rearrange("p (g n) -> p g n", g=G)
            vnew = deal(KVW, T_S)
            rel = deal(LS)
            lgS = deal(LS)
            pTs = deal((PAGES + 1) * P).rearrange("p (a n) -> p a n", a=PAGES + 1)
            pick = deal(P // 2).bitcast(BF16)
            free = after_qS + KEPT * KVW
            qb = keep[:, free:free + P]
            oN = keep[:, free + P:free + P + HD]
            st1 = sb("st1", [P, 4], ctx=ph)
            gexE = sb("gexE", [P, 2, N], ctx=ph)
            y = [deck[:, i * D:(i + 1) * D] for i in range(3)]
            gq, sqj = (deck[:, 3 * D + 4 * P * i:3 * D + 4 * P * (i + 1)] for i in range(2))
            NQ_OUT = segs["out"][2]
            sq = sb("sq", [P, 3, NQ_OUT], ctx=ph)
            ms = sb("ms", [P, 3], ctx=ph)
            rt = sb("rt", [P, 3], ctx=ph)
            nt = sb("nt", [P, 3], ctx=ph)
            rf = sb("rf", [P, 3], ctx=ph)
            gated_a, exped_a = sem("gated_a"), sem("exped_a")
            (e_in, e_rel, e_k, e_v, e_pick, e_vnew, e_kt, e_kcA, e_kcD, e_kn, e_s, e_lg, e_mx, e_exp, e_ri, e_pt,
             e_ptA, e_pv, e_on, e_ot, e_o) = (sem(n) for n in (
                 "e_in", "e_rel", "e_k", "e_v", "e_pick", "e_vnew", "e_kt", "e_kcA", "e_kcD", "e_kn", "e_s", "e_lg",
                 "e_mx", "e_exp", "e_ri", "e_pt", "e_ptA", "e_pv", "e_on", "e_ot", "e_o"))
            f_in = [sem(f"f_in{m}") for m in range(KT // 4)]
            NQ = segs["ga"][2]
            BQ = NB_S // NQ
            assert BQ == 2 and PAGES == 8 and KVW == 512 and LS <= 3 * 512

            def pe_weave(pe, q, j):
                u, s = j // 8, j % 8
                b = q * BQ + u
                if s in (1, 2):
                    for p in range(4 * s - 4, 4 * s):
                        if p == 0:
                            pe.wait_ge(e_k, b * (16 * PAGES) + 16 * PAGES)
                            pe.wait_ge(e_ptA, b)
                        if p == 3:
                            pe.wait_ge(e_o, b)
                        if p >= 4:
                            pe.wait_ge((e_kcA, e_kcD)[p % 2], b * (PAGES // 2) + (p - 4) // 2 + 1)
                        for g in range(G):
                            tr = nc.tensor.transpose(sbank[p % 4][:, g * P:(g + 1) * P], kpg[:, p, g * P:(g + 1) * P], ident[:])
                        tr.then_inc(e_kt, 1)
                if s == 3:
                    pe.wait_ge(e_pick, b * 16 + 16)
                    pe.wait_ge(e_kcA, b * (PAGES // 2) + PAGES // 2)
                    pe.wait_ge(e_kcD, b * (PAGES // 2) + PAGES // 2)
                    pe.wait_ge(e_kn, b * 2 + 2)
                    for c in range(0, LS, 512):
                        z = min(LS, c + 512)
                        nc.tensor.matmul(wide[:, c:z], pick, maskS[:, c:z], start=True, stop=True)
                        for g in range(G):
                            mm = nc.tensor.matmul(wide[32 * g:32 * g + 32, c:z], qb[:, 32 * g:32 * g + 32], KTs[:, g, c:z],
                                                  start=False, stop=True, skip_group_check=True)
                    mm.then_inc(e_s, 1)
                if s == 5:
                    pe.wait_ge(e_exp, b + 1)
                    for p in range(PAGES + 1):
                        r = P if p < PAGES else T_S
                        tr = nc.tensor.transpose(wide[0:r, p * P:(p + 1) * P], lgS[:, p * P:p * P + r], ident[:])
                    tr.then_inc(e_pt, 1)
                if s == 6:
                    pe.wait_ge(e_ptA, b + 1)
                    pe.wait_ge(e_v, b * (16 * PAGES) + 16 * PAGES)
                    pe.wait_ge(e_vnew, b * 16 + 16)
                    for p in range(PAGES + 1):
                        r = P if p < PAGES else T_S
                        v = vpg[p] if p < PAGES else vnew
                        for g in range(G):
                            mm = nc.tensor.matmul(sbank[3][32 * g:32 * g + 32, 0:HD], pTs[0:r, p, 32 * g:32 * g + 32],
                                                  v[:, g * P:(g + 1) * P], start=p == 0, stop=p == PAGES,
                                                  skip_group_check=True)
                    mm.then_inc(e_pv, 1)
                if s == 7:
                    pe.wait_ge(e_on, b + 1)
                    nc.tensor.transpose(sbank[3][:, P:2 * P], oN, ident[:]).then_inc(e_ot, 1)

            def turned_keys(eng, copy, s, b, even, done):
                eng.wait_ge(e_s, b)
                for p in range(4 * s - 4 + (0 if even else 1), 4 * s, 2):
                    eng.wait_ge(e_kt, b * PAGES + (p + 1))
                    copy(KTs[:, :, p * P:(p + 1) * P], sbank[p % 4].rearrange("p (g n) -> p g n", g=G)).then_inc(done, 1)

            def act_weave(act, q, j):
                u, s = j // 8, j % 8
                b = q * BQ + u
                if s in (1, 2):
                    turned_keys(act, lambda o, i: nc.scalar.activation(o, i, ACT.Copy), s, b, True, e_kcA)
                if s == 4:
                    act.wait_ge(e_mx, b + 1)
                    nc.scalar.activation(lgS, lgS, ACT.Exp, bias=st1[:, 0:1], accum_out=st1[:, 1:2]).then_inc(e_exp, 1)
                if s == 5:
                    act.wait_ge(e_pt, b + 1)
                    act.wait_ge(e_pv, b)
                    nc.scalar.activation(pTs[:, 0:PAGES, :], wide[:, 0:PAST].rearrange("p (a n) -> p a n", n=P), ACT.Copy)
                    nc.scalar.activation(pTs[0:T_S, PAGES, :], wide[0:T_S, PAST:PAST + P], ACT.Copy).then_inc(e_ptA, 1)
                if s == 7:
                    act.wait_ge(e_ot, b + 1)
                    nc.scalar.activation(qS[:, :, ds(b * T_S, T_S)], sbank[3][:, P:2 * P].rearrange("p (h n) -> p h n", h=H),
                                         ACT.Copy).then_inc(e_o, 1)

            def dve_weave(dve, q, j):
                u, s = j // 8, j % 8
                b = q * BQ + u
                if s in (1, 2):
                    turned_keys(dve, nc.vector.tensor_copy, s, b, False, e_kcD)
                if s == 2:
                    dve.wait_ge(e_in, 16)
                    nc.vector.tensor_copy(KTs[:, :, PAST:LS], kT[:, :, ds(b * T_S + T_P, T_S)]).then_inc(e_kn, 1)
                    nc.vector.tensor_copy(qb.rearrange("p (h n) -> p h n", h=H), qS[:, :, ds(b * T_S, T_S)]).then_inc(e_kn, 1)
                if s == 3:
                    dve.wait_ge(e_rel, 16 * H)
                    dve.wait_ge(e_s, b + 1)
                    dve.wait_ge(e_pt, b)
                    nc.vector.scalar_tensor_tensor(lgS, wide[:, 0:LS], SCALE, rel, ALU.mult, ALU.add).then_inc(e_lg, 1)
                    dve.wait_ge(e_lg, b + 1)
                    nc.vector.tensor_reduce(st1[:, 0:1], lgS, AX.X, ALU.max, negate=True).then_inc(e_mx, 1)
                if s == 5:
                    dve.wait_ge(e_exp, b + 1)
                    nc.vector.reciprocal(st1[:, 2:3], st1[:, 1:2]).then_inc(e_ri, 1)
                if s == 6:
                    dve.wait_ge(e_ri, b + 1)
                    dve.wait_ge(e_pv, b + 1)
                    dve.wait_ge(e_ot, b)
                    nc.vector.tensor_scalar(oN, sbank[3][:, 0:HD], st1[:, 2:3], None, ALU.mult).then_inc(e_on, 1)

            (f_mul, f_hi, f_lo, f_t, f_add, f_sq, f_gq, f_g, f_sum, f_rt, f_rf, f_x, f_gd) = (sem(n) for n in (
                 "f_mul", "f_hi", "f_lo", "f_t", "f_add", "f_sq", "f_gq", "f_g", "f_sum", "f_rt", "f_rf", "f_x", "f_gd"))
            f_y = {e: sem(f"f_y_{e}") for e in ("act", "dve")}
            f_out = {e: sem(f"f_out_{e}") for e in ("act", "dve")}
            MIX = KT // 4
            HALF = MIX // 2
            FOUR = 4 * N
            spots = [keep[:, 0:FOUR]] + [y[0][:, k * FOUR:(k + 1) * FOUR] for k in range(3)] + [
                keep[:, after_qS + k * FOUR:after_qS + (k + 1) * FOUR] for k in range(2)] + [
                y[i][:, k * FOUR:(k + 1) * FOUR] for i in (1, 2) for k in range(3)]
            spots = [x.rearrange("p (a n) -> p a n", a=4) for x in spots]
            assert FOUR <= G * N and 3 * FOUR <= PAGES * KVW
            STEPS = len(spots) // 2
            om = [spots[2 * (m % STEPS)] for m in range(MIX)]
            gm = [spots[2 * (m % STEPS) + 1] for m in range(MIX)]
            UP_FRONT = 3
            rows = [t["x_prompt"][0, 0:P], t["x_prompt"][0, P:T_P], t["x_sample"].rearrange("b s d -> (b s) d")]
            outs = [out[0][0, 0:P], out[0][0, P:T_P], out[1].rearrange("b s d -> (b s) d")]

            def load_mix(eng, m):
                if m < HALF:
                    eng.dma_start(om[m], tiles(mixT, 4 * m, 4)).then_inc(f_in[m], 16)
                    eng.dma_start(gm[m], tiles(projT, T_GB + 4 * m, 4)).then_inc(f_in[m], 16)
                else:
                    k = 4 * (m - HALF)
                    for half in range(2):
                        eng.wait_ge(stored[half], 16 * (segs["ga"][4] + m - HALF + 1))
                    eng.dma_start(om[m][:, :, 0:T_P], tiles(oT, k, 4)[:, :, 0:T_P]).then_inc(f_in[m], 16)
                    eng.dma_start(gm[m], tiles(projT, T_GA + k, 4)).then_inc(f_in[m], 16)

            def gate_branch(pool, m):
                pool.wait_ge(f_in[m], 32)
                if m < HALF:
                    ins = nc.gpsimd.tensor_tensor(om[m], om[m], gm[m], ALU.mult)
                else:
                    k = 4 * (m - HALF)
                    nc.gpsimd.tensor_tensor(om[m][:, :, 0:T_P], om[m][:, :, 0:T_P], gm[m][:, :, 0:T_P], ALU.mult)
                    ins = nc.gpsimd.tensor_tensor(om[m][:, :, T_P:N], qS[:, k:k + 4, :], gm[m][:, :, T_P:N], ALU.mult)
                ins.then_inc(f_mul, 1)

            CUTS = {"dve": ((0, 0, D // 2), (0, D // 2, D), (2, 0, D // 2), (2, D // 2, D)),
                    "act": ((1, 0, D // 4), (1, D // 4, D // 2), (1, D // 2, 3 * D // 4), (1, 3 * D // 4, D))}

            def scaled(eng, name, mul):
                eng.wait_ge(f_rf, 1)
                eng.wait_ge(f_g, NQ_OUT)
                eng.wait_ge(f_gd, 1)
                for n, (i, a, z) in enumerate(CUTS[name]):
                    r = TT[i][1]
                    mul(y[i][0:r, a:z], rf[0:r, i:i + 1]).then_inc(f_y[name], 1)
                    if name != "dve":
                        eng.wait_ge(f_y[name], n + 1)
                        eng.dma_start(outs[i][:, a:z], y[i][0:r, a:z]).then_inc(f_out[name], 16)
                if name != "dve":
                    eng.wait_ge(f_out[name], 16 * len(CUTS[name]))

            def squares(act, q):
                for i in range(3):
                    r = TT[i][1]
                    act.wait_ge(f_sum, 1)
                    act.wait_ge(f_add, q * 3 + (i + 1))
                    act.wait_ge(f_sq, q * 3 + i)
                    nc.scalar.activation(sqj[0:r, :], y[i][0:r, ds(q * (4 * P), 4 * P)], ACT.Square,
                                         accum_out=sq[0:r, i, ds(q, 1)]).then_inc(f_sq, 1)

            def act_mix(act, m):
                k0 = (4 * m + KT // 2) % KT
                act.wait_ge(f_mul, m + 1)
                nc.scalar.activation(XH[:, k0:k0 + 4, :], om[m], ACT.Copy).then_inc(f_hi, 1)

            def dve_mix(dve, m):
                k0 = (4 * m + KT // 2) % KT
                dve.wait_ge(f_hi, m + 1)
                nc.vector.tensor_tensor(XL[:, k0:k0 + 4, :], om[m], XH[:, k0:k0 + 4, :].bitcast(F32),
                                        ALU.subtract).then_inc(f_lo, 1)

            def then_mix(weave, mix, first, end):
                def last_weave(eng, q, j):
                    weave(eng, q, j)
                    if j == QC - 1:
                        for m in range(first, end):
                            mix(eng, m)
                return last_weave

            def first_mix(act):
                act.wait_ge(chunk_used, segs["out"][3])
                act_mix(act, 0)

            def mix_weave(mix):
                def weave(eng, q, j):
                    if j < MIX - UP_FRONT:
                        mix(eng, UP_FRONT + j)
                return weave

            def act_out_weave(act, q, j):
                if j == 4:
                    squares(act, q - 1)

            def residual(dve, q):
                for i in range(3):
                    r = TT[i][1]
                    cols = y[i][0:r, ds(q * (4 * P), 4 * P)]
                    if i == 0:
                        dve.wait_ge(f_x, 48)
                        dve.wait_ge(f_t, q + 1)
                    nc.vector.tensor_tensor(cols, sbank[i][0:r, :], cols, ALU.add).then_inc(f_add, 1)

            def dve_out_weave(dve, q, j):
                if j == 2:
                    residual(dve, q - 1)

            def turn(pe, q):
                quad0 = segs["out"][4]
                pe.wait_ge(evac[0], q + (quad0 + 1))
                pe.wait_ge(evac[1], q + (quad0 + 2))
                pe.wait_ge(f_add, q * 3)
                for i, (c0, r) in enumerate(TT):
                    for n in range(4):
                        tr = nc.tensor.transpose(sbank[i][0:r, n * P:(n + 1) * P], stg[n // 2][:, n % 2, c0:c0 + r], ident[:])
                tr.then_inc(f_t, 1)

            def pe_out_weave(pe, q, j):
                if j == 2:
                    turn(pe, q - 1)

            block = ph.enter_context(nc.Block())

            def stages_stored(eng):
                eng.wait_ge(ut_out, 16 * POOLW // (4 * P) * (NB_S + 1))
                eng.wait_ge(w_st, 16 * NG)
                eng.wait_ge(a_st, 16 * H)

            @block.sync
            def _(sp):
                stages_stored(sp)
                for h in range(H):
                    bias = biasS[h:h + 1, T_S - 1:T_S - 1 + T_S * (LS + T_S - 1)].rearrange("o (a n) -> (o a) n", n=LS + T_S - 1)
                    sp.dma_start(rel[h * T_S:(h + 1) * T_S, :], bias[:, 0:LS]).then_inc(e_rel, 16)
                load_segment(sp, "ga")
                sp.wait_ge(e_pv, NB_S)
                sp.wait_ge(f_in[2], 32)
                for m in range(HALF, MIX):
                    if m >= STEPS:
                        sp.wait_ge(f_lo, m - STEPS + 1)
                    load_mix(sp, m)
                load_segment(sp, "out")
                for n, (i, a, z) in enumerate(CUTS["dve"]):
                    sp.wait_ge(f_y["dve"], n + 1)
                    sp.dma_start(outs[i][:, a:z], y[i][0:TT[i][1], a:z]).then_inc(f_out["dve"], 16)
                sp.wait_ge(f_out["dve"], 16 * len(CUTS["dve"]))

            @block.gpsimd
            def _(pool):
                def load_pages(b, cache, dst, landed):
                    src = t[cache][0].rearrange("n r g d -> n r (g d)")
                    for p in range(PAGES):
                        page = pool.value_load(ptab[0:1, ds(b * PAGES + p, 1)], min_val=0, max_val=N_PHYS - 1)
                        pool.dma_start(dst[p], tile_rows(src, page)).then_inc(landed, 16)

                def load_pick(b):
                    pool.dma_start(pick, tile_rows(t["c_pick"], b)).then_inc(e_pick, 16)

                def load_vnew(b):
                    pool.dma_start(vnew, out[7][0, ds(b, 1)].rearrange("b s g d -> (b s) (g d)")).then_inc(e_vnew, 16)

                stages_stored(pool)
                pool.wait_ge(u_old, 16)
                keys = [kpg[:, p, :] for p in range(PAGES)]
                load_pages(0, "cache_k", keys, e_k)
                pool.dma_start(qS, projT[T_Q:T_Q + H, :, T_P:N].rearrange("h p n -> p h n")).then_inc(e_in, 16)
                load_pick(0)
                load_pages(0, "cache_v", vpg, e_v)
                load_vnew(0)
                with pool.Fori(1, NB_S) as b:
                    pool.wait_ge(e_kt, b * PAGES)
                    alone(pool)
                    load_pages(b, "cache_k", keys, e_k)
                    pool.wait_ge(e_s, b)
                    alone(pool)
                    load_pick(b)
                    pool.wait_ge(e_pv, b)
                    alone(pool)
                    load_pages(b, "cache_v", vpg, e_v)
                    load_vnew(b)
                pool.wait_ge(e_kt, NB_S * PAGES)
                pool.wait_ge(e_kn, NB_S * 2)
                for m in range(2):
                    load_mix(pool, m)
                for m in range(2):
                    gate_branch(pool, m)
                pool.wait_ge(e_pv, NB_S)
                for m in range(2, HALF):
                    load_mix(pool, m)
                for m in range(2, MIX):
                    if m == HALF:
                        pool.wait_ge(e_o, NB_S)
                    gate_branch(pool, m)
                pool.wait_ge(f_lo, MIX)
                for i in range(3):
                    pool.dma_start(y[i][0:TT[i][1], :], rows[i]).then_inc(f_x, 16)

                def weigh(q, tiles_):
                    pool.wait_ge(f_g, q)
                    alone(pool)
                    pool.dma_start(gq, t["final_g"].rearrange("(o d) -> o d", o=1)[
                        :, ds(q * (4 * P), 4 * P)].to_broadcast([P, 4 * P])).then_inc(f_gq, 16)
                    pool.wait_ge(f_gq, q * 16 + 16)
                    pool.wait_ge(f_sq, q * 3 + 3)
                    for i in tiles_:
                        cols = y[i][0:TT[i][1], ds(q * (4 * P), 4 * P)]
                        ins = nc.gpsimd.tensor_tensor(cols, cols, gq[0:TT[i][1], :], ALU.mult)
                    ins.then_inc(f_g, 1)

                with pool.Fori(0, NQ_OUT - 1) as q:
                    weigh(q, (0, 1, 2))
                weigh(NQ_OUT - 1, (0, ))
                pool.wait_ge(f_g, NQ_OUT)

            @block.scalar
            def _(act):
                gate = (gexE[:], exped_a, gated_a)
                with act.Fori(0, NQ - 1) as q:
                    act_quad(act, "ga", q, act_weave, gate=gate)
                act_quad(act, "ga", NQ - 1, then_mix(act_weave, act_mix, 1, UP_FRONT), gate=gate, early=first_mix)
                act_quad(act, "out", 0, mix_weave(act_mix), turned=f_t)
                with act.Fori(1, NQ_OUT - 1) as q:
                    act_quad(act, "out", q, act_out_weave, turned=f_t)
                act_quad(act, "out", NQ_OUT - 1, act_out_weave, True, turned=f_t)
                squares(act, NQ_OUT - 1)
                act.wait_ge(f_sum, 3)
                nc.scalar.activation(rt[:], ms[:], ACT.Sqrt).then_inc(f_rt, 1)
                scaled(act, "act", lambda o, r: nc.scalar.activation(o, o, ACT.Copy, scale=r))

            @block.vector
            def _(dve):
                gate = (gexE[:], exped_a, gated_a)
                with dve.Fori(0, NQ - 1) as q:
                    dve_quad(dve, "ga", q, dve_weave, gate=gate)
                dve_quad(dve, "ga", NQ - 1, then_mix(dve_weave, dve_mix, 0, UP_FRONT - 1), gate=gate)
                dve_mix(dve, UP_FRONT - 1)
                dve_quad(dve, "out", 0, mix_weave(dve_mix), turned=f_t)
                nc.vector.memset(sq[:], 1.0).then_inc(f_sum, 1)
                with dve.Fori(1, NQ_OUT - 1) as q:
                    dve_quad(dve, "out", q, dve_out_weave, turned=f_t)
                dve_quad(dve, "out", NQ_OUT - 1, dve_out_weave, True, turned=f_t)
                residual(dve, NQ_OUT - 1)
                dve.wait_ge(f_sq, 3 * NQ_OUT)
                nc.vector.tensor_reduce(ms[:], sq[:], AX.X, ALU.add).then_inc(f_sum, 1)
                dve.wait_ge(f_sum, 2)
                nc.vector.tensor_scalar(ms[:], ms[:], 1.0 / D, EPS, ALU.mult, ALU.add).then_inc(f_sum, 1)
                dve.wait_ge(f_gq, 16 * NQ_OUT)
                for i in (1, 2):
                    cols = y[i][0:TT[i][1], D - 4 * P:D]
                    ins = nc.vector.tensor_tensor(cols, cols, gq[0:TT[i][1], :], ALU.mult)
                ins.then_inc(f_gd, 1)
                dve.wait_ge(f_rt, 1)
                nc.vector.reciprocal(rt[:], rt[:]).then_inc(f_sum, 1)
                dve.wait_ge(f_sum, 4)
                nc.vector.tensor_tensor(nt[:], rt[:], rt[:], ALU.mult).then_inc(f_sum, 1)
                dve.wait_ge(f_sum, 5)
                nc.vector.tensor_tensor(nt[:], nt[:], ms[:], ALU.mult).then_inc(f_sum, 1)
                dve.wait_ge(f_sum, 6)
                nc.vector.tensor_scalar(nt[:], nt[:], -0.5, 1.5, ALU.mult, ALU.add).then_inc(f_sum, 1)
                dve.wait_ge(f_sum, 7)
                nc.vector.tensor_tensor(rf[:], rt[:], nt[:], ALU.mult).then_inc(f_rf, 1)
                scaled(dve, "dve", lambda o, r: nc.vector.tensor_scalar(o, o, r, None, ALU.mult))

            @block.tensor
            def _(pe):
                pe_segment(pe, "ga", pe_weave)
                pe_quad(pe, "out", 0, before=lambda pe, j: pe.wait_ge(f_lo, min(j, CH - 1) + 1))
                with pe.Fori(1, NQ_OUT) as q:
                    pe_quad(pe, "out", q, pe_out_weave)
                turn(pe, NQ_OUT - 1)


_INS = ["x_prompt", "x_sample", "cache_k", "cache_v", "cache_idx_k", "state_pool", "page_table", "rel_bias", "ln_g",
        "w_in", "w_pool", "pool_scale", "w_out", "final_g"]


def kernel(**inputs):
    import math

    import ml_dtypes
    import concourse.bacc as _bacc
    from concourse.bass_utils import run_bass_kernel_spmd as _run

    nc = _bacc.Bacc("TRN2", target_bir_lowering=False, num_devices=1, dynamic_dma_scratch_size=8192)
    arrays, t = {}, {}

    def give(name, a):
        a = np.ascontiguousarray(a)
        arrays[name] = a
        t[name] = nc.dram_tensor(name, a.shape, mybir.dt.from_np(a.dtype), kind="ExternalInput").ap()

    for name in _INS:
        give(name, inputs[name])
    _, t_p, d = inputs["x_prompt"].shape
    b_s, t_s, _ = inputs["x_sample"].shape
    depth, n_phys, page, g, hd = inputs["cache_k"].shape
    idd = inputs["cache_idx_k"].shape[-1]
    past = inputs["page_table"].shape[1] * page
    nbk, h = inputs["rel_bias"].shape
    poolw, state = inputs["pool_scale"].shape[1], inputs["state_pool"].shape[2]

    f32, p = np.float32, P
    give("c_ident", np.eye(p, dtype=f32))
    rows = np.arange(p)[:, None]
    causal = np.concatenate([np.arange(p)[None] > rows, np.arange(t_p)[None] > rows + p], axis=1)
    give("c_causal", np.where(causal, f32(NEG), f32(0)))
    give("c_causal_s", np.where(np.arange(t_s)[None] > (np.arange(b_s * t_s) % t_s)[:, None], f32(NEG), f32(0)))
    dist = np.maximum(past + t_s - 1 - np.arange(past + t_s + p), 0)
    exact = nbk // 2
    far = exact + (np.log(np.maximum(dist, 1).astype(f32) / f32(exact)) / f32(math.log(128 / exact))
                   * f32(nbk - exact)).astype(np.int32)
    bucket = np.where(dist < exact, dist, np.minimum(far, nbk - 1))
    give("c_onehot", (np.arange(nbk)[:, None] == bucket[None]).astype(f32))
    pos = np.arange(state + 1)
    count = np.stack([1.0 / np.minimum(pos + 1, w) for w in (2, 4, 8, 16)]).astype(f32)
    give("c_count", np.broadcast_to(count[None], (p,) + count.shape))
    k, m = np.arange(p)[None, :, None], np.arange(p)[None, None, :]
    pick = (k == np.arange(b_s)[:, None, None] * t_s + m % t_s)
    give("c_pick", pick.astype(ml_dtypes.bfloat16))

    shapes = [(1, t_p, d), (b_s, t_s, d), (depth, 1, t_p, g, hd), (depth, 1, t_p, g, hd), (depth, 1, t_p, idd),
              (depth, 1, state, poolw), (depth, b_s, t_s, g, hd), (depth, b_s, t_s, g, hd), (depth, b_s, t_s, idd),
              (depth, b_s, state, poolw)]
    out = [nc.dram_tensor(f"out_{i}", s, F32, kind="ExternalOutput").ap() for i, s in enumerate(shapes)]
    hybrid_layer(nc, t, out)
    r = _run(nc, [arrays], core_ids=[0])
    return tuple(r.results[0][f"out_{i}"] for i in range(len(shapes)))
```
